# Optimizing a Trainium2 kernel written in Bass

```python
import math
import jax
import jax.numpy as jnp
from jax import lax
import numpy as np

D_MODEL = 1024
BATCH = 1
SEQ = 128
DEPTH = 2
DEC_BATCH = 1
DEC_SEQ = 512
PAST_LEN = 128

GRID_W = 64
POOL_WINDOWS = (2, 4, 8, 16)
POOL_GROUP = 128
POOL_WIDTH = POOL_GROUP * len(POOL_WINDOWS)
N_HEADS = 8
QK_NOPE = 64
QK_ROPE = 32
QK_HEAD = QK_NOPE + QK_ROPE
V_HEAD = 64
Q_RANK = 384
KV_RANK = 256
ATTN_WIDTH = N_HEADS * V_HEAD
MIX_WIDTH = POOL_WIDTH + ATTN_WIDTH
IN_WIDTH = POOL_WIDTH + Q_RANK + KV_RANK + QK_ROPE
N_EXPERTS = 16
N_GROUPS = 4
EXPERTS_PER_GROUP = N_EXPERTS // N_GROUPS
TOP_K = 2
D_EXPERT = 256
ROPE_BASE = 10000.0
EPS = 1e-6
Q_BLOCK = 128

kernel_name = 'hybrid_pool_mla_moe_diffusion_step'

def rms_norm(x, g):
    xf = x.astype(jnp.float32)
    y = xf * lax.rsqrt(jnp.mean(xf * xf, axis=-1, keepdims=True) + EPS)
    return (y * g.astype(jnp.float32)).astype(x.dtype)

def axial_rope(rows):
    row = jnp.repeat(jnp.arange(rows), GRID_W).astype(jnp.float32)
    col = jnp.tile(jnp.arange(GRID_W), rows).astype(jnp.float32)
    n_freq = QK_ROPE // 4
    inv = ROPE_BASE ** (-jnp.arange(n_freq, dtype=jnp.float32) / n_freq)
    ang = jnp.concatenate([row[:, None] * inv, col[:, None] * inv], axis=-1)
    return jnp.cos(ang)[:, None, :], jnp.sin(ang)[:, None, :]

def apply_rope(t, cos, sin):
    half = QK_ROPE // 2
    nope = t[..., :QK_NOPE]
    r1 = t[..., QK_NOPE:QK_NOPE + half].astype(jnp.float32)
    r2 = t[..., QK_NOPE + half:].astype(jnp.float32)
    rot = jnp.concatenate([r1 * cos - r2 * sin, r1 * sin + r2 * cos], axis=-1).astype(t.dtype)
    return jnp.concatenate([nope, rot], axis=-1)

def pool_mixer(u, pool_w, pool_scale):
    B, L, _ = u.shape
    uf = u.astype(jnp.float32)
    csum = jnp.concatenate([jnp.zeros((B, 1, POOL_WIDTH), jnp.float32), jnp.cumsum(uf, axis=1)], axis=1)
    t = jnp.arange(L)
    outs = []
    for g, w in enumerate(POOL_WINDOWS):
        lo = jnp.clip(t - w // 2, 0, L)
        hi = jnp.clip(t + w // 2, 0, L)
        sl = slice(g * POOL_GROUP, (g + 1) * POOL_GROUP)
        cg = csum[:, :, sl]
        mean = (cg[:, hi] - cg[:, lo]) / (hi - lo).astype(jnp.float32)[None, :, None]
        d = (mean - uf[:, :, sl]).astype(u.dtype)
        outs.append(d @ pool_w[g])
    return jnp.concatenate(outs, axis=-1) * pool_scale

def mla_keys(ckv, kr, w_ukv, k_norm_g):
    B, N, _ = ckv.shape
    kv = (ckv @ w_ukv).reshape(B, N, N_HEADS, QK_NOPE + V_HEAD)
    k_nope, v = kv[..., :QK_NOPE], kv[..., QK_NOPE:]
    k = jnp.concatenate([k_nope, jnp.broadcast_to(kr[:, :, None, :], (B, N, N_HEADS, QK_ROPE))], axis=-1)
    return rms_norm(k, k_norm_g), v

def attend(q, k, v):
    B, L, H, Dk = q.shape
    nb = L // Q_BLOCK
    qb = jnp.moveaxis(q.reshape(B, nb, Q_BLOCK, H, Dk), 1, 0)
    scale = 1.0 / math.sqrt(Dk)

    def block(qi):
        s = jnp.einsum('bqhd,bkhd->bhqk', qi, k, preferred_element_type=jnp.float32) * scale
        p = jax.nn.softmax(s, axis=-1).astype(v.dtype)
        return jnp.einsum('bhqk,bkhd->bqhd', p, v)

    o = lax.map(block, qb)
    return jnp.moveaxis(o, 0, 1).reshape(B, L, H * v.shape[-1])

def moe(h, router_w, router_b, w_gate, w_up, w_down):
    B, L, D = h.shape
    t = h.reshape(B * L, D)
    scores = jax.nn.sigmoid(jnp.dot(t, router_w, preferred_element_type=jnp.float32))
    sel = scores + router_b.astype(jnp.float32)
    grp_score = jnp.sum(lax.top_k(sel.reshape(-1, N_GROUPS, EXPERTS_PER_GROUP), TOP_K)[0], axis=-1)
    best = jnp.argmax(grp_score, axis=-1)
    in_group = (jnp.arange(N_EXPERTS) // EXPERTS_PER_GROUP)[None, :] == best[:, None]
    _, idx = lax.top_k(jnp.where(in_group, sel, -jnp.inf), TOP_K)
    wts = jnp.take_along_axis(scores, idx, axis=-1)
    wts = wts / jnp.sum(wts, axis=-1, keepdims=True)
    gates = jnp.sum(jax.nn.one_hot(idx, N_EXPERTS, dtype=jnp.float32) * wts[..., None], axis=1).astype(h.dtype)
    a = jnp.einsum('td,edf->tef', t, w_gate)
    b = jnp.einsum('td,edf->tef', t, w_up)
    act = jax.nn.silu(a) * b * gates[:, :, None]
    return jnp.einsum('tef,efd->td', act, w_down).reshape(B, L, D)

def trunk_layer(x, cond, p, router_w, router_b, latent_ctx):
    B, L, _ = x.shape
    mod = (jax.nn.silu(cond) @ p['ada_w'] + p['ada_b'])[:, None, :]
    shift1, scale1, gate1, shift2, scale2, gate2 = jnp.split(mod, 6, axis=-1)
    h = rms_norm(x, p['norm1_g']) * (1 + scale1) + shift1
    proj = h @ p['w_in']
    u, cq, ckv, kr = jnp.split(proj, [POOL_WIDTH, POOL_WIDTH + Q_RANK, POOL_WIDTH + Q_RANK + KV_RANK], axis=-1)
    pool_out = pool_mixer(u, p['pool_w'], p['pool_scale'])
    ckv = rms_norm(ckv, p['kv_a_norm_g'])
    q = (rms_norm(cq, p['q_a_norm_g']) @ p['w_uq']).reshape(B, L, N_HEADS, QK_HEAD)
    q = rms_norm(q, p['q_norm_g'])
    k, v = mla_keys(ckv, kr, p['w_ukv'], p['k_norm_g'])
    if latent_ctx is not None:
        k_ctx, v_ctx, cos, sin = latent_ctx
        q = apply_rope(q, cos, sin)
        k = jnp.concatenate([k_ctx, apply_rope(k, cos, sin)], axis=1)
        v = jnp.concatenate([v_ctx, v], axis=1)
    attn = attend(q, k, v)
    x = x + gate1 * (jnp.concatenate([pool_out, attn], axis=-1) @ p['w_out'])
    h2 = rms_norm(x, p['norm2_g']) * (1 + scale2) + shift2
    x = x + gate2 * moe(h2, router_w, router_b, p['w_gate'], p['w_up'], p['w_down'])
    return x, ckv, kr

def setup_inputs(seed: int = 0) -> dict:
    key = jax.random.key(seed)
    ks = jax.random.split(key, 32)

    def nrm(k, shape, s):
        return jax.random.normal(k, shape, jnp.float32) * s

    def gain(k, shape):
        return 1.0 + 0.05 * jax.random.normal(k, shape, jnp.float32)

    return {
        'x_prompt': nrm(ks[0], (BATCH, SEQ, D_MODEL), 1.0),
        'x_sample': nrm(ks[1], (DEC_BATCH, DEC_SEQ, D_MODEL), 1.0),
        'cache_ckv': nrm(ks[2], (DEC_BATCH, DEPTH, PAST_LEN, KV_RANK), 1.0),
        'cache_krope': nrm(ks[3], (DEC_BATCH, DEPTH, PAST_LEN, QK_ROPE), 1.0),
        'c': nrm(ks[4], (DEC_BATCH, D_MODEL), 1.0),
        'c_ctx': nrm(ks[5], (D_MODEL,), 1.0),
        'ada_w': nrm(ks[6], (DEPTH, D_MODEL, 6 * D_MODEL), 0.5 * D_MODEL ** -0.5),
        'ada_b': nrm(ks[7], (DEPTH, 6 * D_MODEL), 0.02),
        'norm1_g': gain(ks[8], (DEPTH, D_MODEL)),
        'norm2_g': gain(ks[9], (DEPTH, D_MODEL)),
        'w_in': nrm(ks[10], (DEPTH, D_MODEL, IN_WIDTH), D_MODEL ** -0.5),
        'pool_w': nrm(ks[11], (DEPTH, len(POOL_WINDOWS), POOL_GROUP, POOL_GROUP), POOL_GROUP ** -0.5),
        'pool_scale': gain(ks[12], (DEPTH, POOL_WIDTH)),
        'q_a_norm_g': gain(ks[13], (DEPTH, Q_RANK)),
        'w_uq': nrm(ks[14], (DEPTH, Q_RANK, N_HEADS * QK_HEAD), Q_RANK ** -0.5),
        'kv_a_norm_g': gain(ks[15], (DEPTH, KV_RANK)),
        'w_ukv': nrm(ks[16], (DEPTH, KV_RANK, N_HEADS * (QK_NOPE + V_HEAD)), KV_RANK ** -0.5),
        'q_norm_g': gain(ks[17], (DEPTH, QK_HEAD)),
        'k_norm_g': gain(ks[18], (DEPTH, QK_HEAD)),
        'w_out': nrm(ks[19], (DEPTH, MIX_WIDTH, D_MODEL), MIX_WIDTH ** -0.5),
        'router_w': nrm(ks[20], (D_MODEL, N_EXPERTS), D_MODEL ** -0.5),
        'router_b': nrm(ks[21], (N_EXPERTS,), 0.01),
        'w_gate': nrm(ks[22], (DEPTH, N_EXPERTS, D_MODEL, D_EXPERT), D_MODEL ** -0.5),
        'w_up': nrm(ks[23], (DEPTH, N_EXPERTS, D_MODEL, D_EXPERT), D_MODEL ** -0.5),
        'w_down': nrm(ks[24], (DEPTH, N_EXPERTS, D_EXPERT, D_MODEL), D_EXPERT ** -0.5),
    }

def reference(x_prompt, x_sample, cache_ckv, cache_krope, c, c_ctx, ada_w, ada_b, norm1_g, norm2_g, w_in, pool_w,
              pool_scale, q_a_norm_g, w_uq, kv_a_norm_g, w_ukv, q_norm_g, k_norm_g, w_out, router_w, router_b,
              w_gate, w_up, w_down):
    rows = x_sample.shape[1] // GRID_W
    cos, sin = axial_rope(rows)
    y_prompt, y_sample = x_prompt, x_sample
    ckv_list, kr_list = [], []
    for l in range(DEPTH):
        p = dict(ada_w=ada_w[l], ada_b=ada_b[l], norm1_g=norm1_g[l], norm2_g=norm2_g[l], w_in=w_in[l],
                 pool_w=pool_w[l], pool_scale=pool_scale[l], q_a_norm_g=q_a_norm_g[l], w_uq=w_uq[l],
                 kv_a_norm_g=kv_a_norm_g[l], w_ukv=w_ukv[l], q_norm_g=q_norm_g[l], k_norm_g=k_norm_g[l],
                 w_out=w_out[l], w_gate=w_gate[l], w_up=w_up[l], w_down=w_down[l])
        y_prompt, ckv, kr = trunk_layer(y_prompt, c_ctx[None, :], p, router_w, router_b, None)
        ckv_list.append(ckv)
        kr_list.append(kr)
        k_ctx, v_ctx = mla_keys(cache_ckv[:, l], cache_krope[:, l], w_ukv[l], k_norm_g[l])
        y_sample, _, _ = trunk_layer(y_sample, c, p, router_w, router_b, (k_ctx, v_ctx, cos, sin))
    new_ckv = jnp.stack(ckv_list, axis=1)
    new_krope = jnp.stack(kr_list, axis=1)
    return (y_prompt, y_sample, new_ckv, new_krope)


_drawn_inputs = setup_inputs


def setup_inputs(seed=0):
    import zlib

    import numpy as np

    out = dict(_drawn_inputs(seed))
    spreads = {}
    factors = {'cache_ckv': 2.916,
     'cache_krope': 5.507,
     'q_a_norm_g': 6.488,
     'q_norm_g': 8.0,
     'k_norm_g': 8.0}
    for name, (base, spread) in spreads.items():
        noise = np.random.default_rng([zlib.crc32(name.encode()), seed]).standard_normal(out[name].shape)
        drawn = base * np.exp(spread * noise) if base else spread * noise
        out[name] = jnp.asarray(drawn.astype(out[name].dtype))
    for name, factor in factors.items():
        out[name] = (out[name] * factor).astype(out[name].dtype)
    return out
```

```python
from contextlib import ExitStack

import numpy as np

import concourse.bass as bass
from concourse import mybir

F32 = mybir.dt.float32
I32 = mybir.dt.int32
U32 = mybir.dt.uint32
ALU = mybir.AluOpType
ACT = mybir.ActivationFunctionType
AX = mybir.AxisListType

P = 128
DEPTH = 2
D = 1024
DC = D // P
SEQ, DEC = 128, 512
NT = (SEQ + DEC) // P
NTOK = NT * P
GRID_W = 64
WINDOWS = (2, 4, 8, 16)
NG = len(WINDOWS)
POOLW = NG * P
H = 8
NOPE, ROPE, VH = 64, 32, 64
QH = NOPE + ROPE
QR, KVR = 384, 256
QC, KC = QR // P, KVR // P
INW = POOLW + QR + KVR + ROPE
NE, EG, GE = 16, 4, 4
DE = 256
EPS = 1e-6
SCALE = 1.0 / float(np.sqrt(QH))
NKT = NT + 1
NLK = NKT - 1
CTX = NKT - 1
NPIECE = 6
HALF = 512
NBLK = 26
NSLOT = NBLK * P
UNITS = [(t, h) for t in range(NT) for h in range(H)]
NU = len(UNITS)
GAP = 16
PW = GAP + SEQ + GAP + DEC + GAP
CTX0, LAT0 = GAP, GAP + SEQ + GAP

ADA_AT = {2 + n: (2 + n // 8, (n // 4) % 2, n % 4) for n in range(24)}


def constants():
    cols, at = [], {}

    def put(name, a):
        full = np.zeros((P, a.shape[1]), np.float32)
        full[:a.shape[0]] = a
        at[name] = (sum(c.shape[1] for c in cols), a.shape[1])
        cols.append(full)

    put("ident", np.eye(P, dtype=np.float32))
    for c in range(2):
        put(f"sel{c}", np.repeat((np.arange(P) % 32 == c).astype(np.float32)[:, None], P, 1))
    bsel = np.zeros((12, 12, 32), np.float32)
    for j in range(12):
        bsel[j, j, 0:2] = 1
    put("bias_sel", bsel.reshape(12, -1))
    rows = DEC // GRID_W
    inv = (np.float32(10000.0) ** (-np.arange(ROPE // 4, dtype=np.float32) / np.float32(ROPE // 4))).astype(np.float32)
    row = np.repeat(np.arange(rows), GRID_W).astype(np.float32)
    col = np.tile(np.arange(GRID_W), rows).astype(np.float32)
    ang = np.concatenate([row[:, None] * inv, col[:, None] * inv], -1).astype(np.float32)
    for name, f in (("cos", np.cos), ("sin", np.sin)):
        v = f(ang).astype(np.float32).reshape(NT - 1, P, ROPE // 2).transpose(1, 0, 2)
        put(name, v.reshape(P, -1))
    edge = np.ones((NG, 16), np.float32)
    for g, w in enumerate(WINDOWS):
        for t in range(8):
            edge[g, t] = w / min(w, t + w // 2)
            left = 8 - t
            edge[g, 8 + t] = w / min(w, w // 2 + min(left, w // 2))
    put("edge", np.tile(edge.reshape(1, -1), (P, 1)))
    i = np.arange(P)
    put("before", (i[:, None] < i[None, :]).astype(np.float32))
    put("ones", np.ones((P, P), np.float32))
    put("lower", np.tile((i[:4, None] > i[None, :4]).astype(np.float32).reshape(1, -1), (P, 1)))
    put("row", np.tile(i[None, :].astype(np.float32), (P, 1)))
    put("block", np.tile(np.arange(NBLK, dtype=np.float32)[None], (P, 1)))
    put("kblock", np.tile((np.arange(5) * P).astype(np.float32)[None], (P, 1)))
    put("token", (np.arange(NT)[None] * P + i[:, None]).astype(np.float32))
    put("mhalf", np.full((P, 8), -0.5, np.float32))
    return np.concatenate(cols, 1), at


def step_kernel(nc, x_prompt, x_sample, cache_ckv, cache_krope, c, c_ctx, ada_w, ada_b, norm1_g, norm2_g, w_in, pool_w,
                pool_scale, q_a_norm_g, w_uq, kv_a_norm_g, w_ukv, q_norm_g, k_norm_g, w_out, router_w, router_b,
                w_gate, w_up, w_down, consts, y_prompt, y_sample, new_ckv, new_krope, const_at):
    es = ExitStack()
    with es:
        def sb(name, shape, dt=F32):
            return es.enter_context(nc.sbuf_tensor(name, shape, dt))

        def sem(name):
            return es.enter_context(nc.semaphore(name))

        x = sb("x", [P, NT, D])
        actT = sb("actT", [P, DC, NTOK])
        BIGW = 3 * 6144
        big = sb("big", [P, BIGW])
        low = sb("low", [P, 8960])
        ada_ring = [sb(f"ada_ring{i}", [P, 4, HALF]) for i in range(2)]
        mod = sb("mod", [P, 6144])
        cst = sb("cst", [P, sum(n for _, n in const_at.values())])
        bias_rows = sb("bias_rows", [12, HALF])
        part_s = sb("part_s", [P, HALF])
        gain = sb("gain", [P, D])
        condT = sb("condT", [P, DC, 32])
        rw = sb("rw", [P, DC, NE])
        rb = sb("rb", [P, NE])
        gq = sb("gq", [P, QH])
        gk = sb("gk", [P, QH])
        pscale = sb("pscale", [P, NG])
        kr = sb("kr", [P, NKT, ROPE])
        krr = sb("krr", [P, NKT, ROPE])
        rope_t = sb("rope_t", [P, 2, ROPE])
        ss = sb("ss", [P, 2 * NT])
        rs = sb("rs", [P, 2 * NT])
        head_ss = sb("head_ss", [P, 2, 2, H])
        head_rs = sb("head_rs", [P, 2, 2, H])
        kr_ss = sb("kr_ss", [P, NKT])
        low_ss = sb("low_ss", [P, NT, 2])
        low_rs = sb("low_rs", [P, NT, 2])
        nmax = sb("nmax", [P, 2])
        mx = sb("mx", [P, 2])
        esum = sb("esum", [P, NU])
        rsum = sb("rsum", [P, H])
        slot_i = sb("slot_i", [P, 2 * NT], U32)
        slot_a = sb("slot_a", [P, 2 * NT], U32)
        slot_b = sb("slot_b", [P, 2 * NT], U32)
        gates2 = sb("gates2", [P, 2 * NT])
        idx = sb("idx", [P, NBLK], U32)
        eid = sb("eid", [P, NBLK], I32)

        def k_(name):
            a, n = const_at[name]
            return cst[:, a:a + n]

        ident = k_("ident")

        def view(t, lo, shape):
            n = int(np.prod(shape))
            v = t[:, lo:lo + n]
            if len(shape) == 2:
                return v.rearrange("p (a b) -> p a b", b=shape[1])
            if len(shape) == 3:
                return v.rearrange("p (a b c) -> p a b c", b=shape[1], c=shape[2])
            return v

        win = view(big, 0, (DC, INW))
        cache_n = view(big, DC * INW, (KVR,))
        ckv_keep = view(big, DC * INW + KVR, (KVR,))
        gqa = view(big, DC * INW + 2 * KVR, (QR,))
        gkva = view(big, DC * INW + 2 * KVR + QR, (KVR,))
        crow = part_s[0:16, 0:P]
        qT = view(big, 0, (H, NTOK))
        kT = view(big, 5120, (H, NKT * P))
        V = view(big, 11264, (NKT, H * VH))
        cqT = view(big, 14336, (QC, NTOK))
        ckvT = view(big, 16256, (KC, NKT * P))
        prob = [view(big, 14336 + 640 * i, (NLK, P)) for i in range(2)]
        probT = [view(big, 15616 + 640 * i, (NLK, P)) for i in range(2)]
        onat = view(big, 16896, (HALF,))
        wgu = [view(big, 6144 * i, (DC, 2 * DE)) for i in range(2)]
        wd = [view(big, 6144 * i + 4096, (2, D)) for i in range(2)]
        xn = [view(big, 12288 + D * i, (D,)) for i in range(2)]
        xg = xn
        xgT = [view(big, 14336 + D * i, (DC, P)) for i in range(2)]
        act_n = view(big, 16384, (DE,))
        sil = view(big, 16384 + DE, (DE,))
        acT = view(big, 16384 + 2 * DE, (2, P))
        yb = view(big, 17408, (D,))
        comb = [view(big, 14336 + D * i, (D,)) for i in range(4)]
        rt = 14336
        sel_s = view(big, rt, (NT * EG, GE))
        sig = view(big, rt + 80, (NT * EG, GE))
        cmp4 = view(big, rt + 160, (NT * EG, GE, GE))
        eq4 = view(big, rt + 480, (NT * EG, GE, GE))
        chosen = view(big, rt + 800, (NT * EG, GE))
        rank = view(big, rt + 880, (NT * EG, GE))
        gsc = view(big, rt + 960, (NT, EG))
        gcmp = view(big, rt + 980, (NT, EG, EG))
        geq = view(big, rt + 1060, (NT, EG, EG))
        best = view(big, rt + 1140, (NT, EG))
        mask = view(big, rt + 1160, (NT, NE))
        gts = view(big, rt + 1240, (NT, NE))
        den = view(big, rt + 1320, (NT,))
        hot = view(big, rt + 1330, (2, NT, NE))
        slot1 = view(big, rt + 1490, (NT, NE))
        pick = view(big, rt + 1570, (2, NT))
        nbc = view(big, rt + 1590, (NE, 5))
        nb = view(big, rt + 1670, (NE,))
        endb = view(big, rt + 1690, (NE,))
        start = view(big, rt + 1710, (NE,))
        ecmp = view(big, rt + 1730, (NBLK, NE))
        eidf = view(big, rt + 2146, (NBLK,))
        slot_p = view(big, rt + 2180, (2 * NT,))
        slot_q = view(big, rt + 2190, (2 * NT,))
        onep = [view(big, rt + 2200 + P * i, (P,)) for i in range(2)]
        oneb = [view(big, rt + 2456 + 32 * i, (NBLK,)) for i in range(2)]
        prod = view(big, rt + 2520, (2, NT, NE))
        wuq = view(low, 0, (QC, H * QH))
        wukv = view(low, 2304, (KC, H * (NOPE + VH)))
        pw = view(low, 4352, (NG, P))
        wo = [view(low, 4864, (DC, HALF)), view(low, 0, (DC, HALF))]
        G = view(mod, 0, (2, D))
        S = view(mod, 2 * D, (2, D))
        gate = view(mod, 4 * D, (2, D))
        u = view(mod, 0, (NG, PW))
        pa = view(mod, NG * PW, (PW,))
        pb = view(mod, (NG + 1) * PW, (PW,))
        qn = view(mod, 4480, (H, QH))
        kn = view(mod, 4480 + H * QH, (H, QH))
        cn = view(mod, 4480, (QR + KVR,))
        sq_x = yb
        sq_cq, sq_ckv = view(big, 17792, (QR,)), view(big, 17792 + QR, (KVR,))
        flat = actT[:, :, :].rearrange("p a b -> p (a b)")
        sq_q = view(flat, 4 * NTOK, (H, QH))
        sq_k = view(flat, 6 * NTOK, (H, NOPE))
        sq_kr = view(flat, 7 * NTOK, (ROPE,))
        rq = [view(gain, i * H * 16, (H, 16)) for i in range(4)]
        out_s = [view(big, 14336 + HALF * i, (HALF,)) for i in range(4)]

        bank = [es.enter_context(nc.psum_tensor(f"bank{i}", [P, HALF], F32)) for i in range(4, 8)]
        pair = [es.enter_context(nc.psum_tensor(f"pair{i}", [P, 2 * HALF], F32)) for i in range(2)]
        tb4, tb5, o6, a7 = bank

        h2_rows = nc.dram_tensor("h2_rows", [NTOK, D], F32, kind="Internal").ap()
        y_rows = nc.dram_tensor("y_rows", [NSLOT, D], F32, kind="Internal").ap()

        ld_start = sem("ld_start")
        ld_ada = [sem("ld_ada0"), sem("ld_ada1")]
        ld_bias = sem("ld_bias")
        ld_gain = sem("ld_gain")
        ld_win = sem("ld_win")
        ld_low = sem("ld_low")
        ld_small = sem("ld_small")
        ld_wo = [sem("ld_wo0"), sem("ld_wo1")]
        ld_exp = [sem("ld_exp0"), sem("ld_exp1")]
        ada_used = sem("ada_used")
        gain_used = sem("gain_used")
        blocks_done = sem("blocks_done")
        win_used = sem("win_used")
        proj_used = sem("proj_used")
        wo_used = sem("wo_used")
        eid_ready = sem("eid_ready")
        layer_go = sem("layer_go")
        out_done = sem("out_done")
        g_in = [sem("g_in0"), sem("g_in1")]
        c_in = [sem(f"c_in{i}") for i in range(4)]
        cond_t = sem("cond_t")
        cond_s = sem("cond_s")
        start_d = sem("start_d")

        cleared = []

        def lsem(name):
            cleared.append(sem(name))
            return cleared[-1]

        layer_end = lsem("layer_end")
        dv = lsem("dve_chain")
        pl = lsem("pool_chain")
        ac = lsem("act_chain")
        ada_part, ada_part_s, ada_bc, ada_bc_s = (lsem(n) for n in ("ada_part", "ada_part_s", "ada_bc", "ada_bc_s"))
        x_sq, x_rs = lsem("x_sq"), lsem("x_rs")
        h_ready, h_t, h_ta, h_td = (lsem(n) for n in ("h_ready", "h_t", "h_ta", "h_td"))
        h_st = [lsem("h_st0"), lsem("h_st1")]
        in_mm, in_act, in_dve = lsem("in_mm"), lsem("in_act"), lsem("in_dve")
        low_sq, low_r, low_t, low_ta, low_td = (lsem(n) for n in ("low_sq", "low_r", "low_t", "low_ta", "low_td"))
        ckv_out = lsem("ckv_out")
        q_mm, kv_mm, q_sq, k_sq, q_ss, k_ss, q_rs, k_rs = (lsem(n) for n in ("q_mm", "kv_mm", "q_sq", "k_sq", "q_ss",
                                                                            "k_ss", "q_rs", "k_rs"))
        v_cp, q_n, k_n, q_rd, k_rd = (lsem(n) for n in ("v_cp", "q_n", "k_n", "q_rd", "k_rd"))
        qk_t, qk_ta, qk_td = lsem("qk_t"), lsem("qk_ta"), lsem("qk_td")
        krr_s = lsem("krr_s")
        keep_s, keep_out = lsem("keep_s"), lsem("keep_out")
        pool_z, pool_d, pool_mm, pool_ea, pool_ed = (lsem(n) for n in ("pool_z", "pool_d", "pool_mm", "pool_ea",
                                                                        "pool_ed"))
        s_sc, s_mx, s_exp, s_pt, s_pta, s_ptb, s_pv, s_on, s_ot, s_otc = (lsem(n) for n in (
            "s_sc", "s_mx", "s_exp", "s_pt", "s_pta", "s_ptb", "s_pv", "s_on", "s_ot", "s_otc"))
        op_mm, op_g, op_x = lsem("op_mm"), lsem("op_g"), lsem("op_x")
        r_mm, r_e, r_mask, r_tot, r_one, r_pe1, r_idx, r_route = (lsem(n) for n in (
            "r_mm", "r_e", "r_mask", "r_tot", "r_one", "r_pe1", "r_idx", "r_route"))
        b_t, b_ta, b_td, b_gu, b_sil, b_act, b_at, b_atc, b_dn, b_ya, b_yd, b_st = (lsem(n) for n in (
            "b_t", "b_ta", "b_td", "b_gu", "b_sil", "b_act", "b_at", "b_atc", "b_dn", "b_ya", "b_yd", "b_st"))
        c_hi, c_gt = lsem("c_hi"), lsem("c_gt")

        C_USES = [sum((2 * t + w) % 4 == k for t in range(NT) for w in range(2)) for k in range(4)]
        ctx_of = lambda t: 0 if t == 0 else 1
        key_tile = lambda t: CTX if t == 0 else t
        KV_ORDER = [key_tile(t) for t in range(NT)] + [0]

        block = es.enter_context(nc.Block())

        @block.sync
        def _(sp):
            sp.dma_start(cst[:, :], consts).then_inc(ld_start, 16)
            sp.dma_start(crow[0:8], c_ctx.rearrange("(k p) -> k p", p=P)).then_inc(ld_start, 16)
            sp.dma_start(crow[8:16], c.rearrange("b (k p) -> (b k) p", p=P)).then_inc(ld_start, 16)
            sp.dma_start(x[:, 0, :], x_prompt[0]).then_inc(ld_start, 16)
            sp.dma_start(x[:, 1:NT, :], x_sample[0].rearrange("(t p) d -> p t d", p=P)).then_inc(ld_start, 16)
            sp.dma_start(rw[:, :, :], router_w.rearrange("(k p) e -> p k e", p=P)).then_inc(ld_start, 16)
            sp.dma_start(rb[:, :], router_b.rearrange("(a e) -> a e", a=1).broadcast_to([P, NE])).then_inc(ld_start, 16)
            with sp.Fori(0, DEPTH) as l:
                quarter = [0]

                def load_ada(p):
                    for n in range(2):
                        for kh in range(2):
                            q = quarter[0]
                            sp.wait_ge(ada_used, l * (4 * NPIECE) + max(q, 1))
                            src = ada_w[l, kh * HALF:(kh + 1) * HALF, p * D + n * HALF:p * D + (n + 1) * HALF]
                            sp.dma_start(ada_ring[q % 2][:, :, :], src.rearrange("(k p) n -> p k n", p=P))\
                              .then_inc(ld_ada[q % 2], 16)
                            quarter[0] += 1

                sp.wait_ge(blocks_done, l * NBLK + 1)
                sp.dma_start(bias_rows[:, :], ada_b[l].rearrange("(j n) -> j n", n=HALF)).then_inc(ld_bias, 16)
                sp.dma_start(gain[:, :], norm1_g[l].rearrange("(a n) -> a n", a=1).broadcast_to([P, D]))\
                  .then_inc(ld_gain, 16)
                load_ada(0)
                load_ada(1)
                sp.wait_ge(wo_used, l + 1)
                for dst, src in ((gq, q_norm_g), (gk, k_norm_g)):
                    sp.dma_start(dst[:, :], src[l].rearrange("(a n) -> a n", a=1).broadcast_to([P, dst.shape[1]]))\
                      .then_inc(ld_small, 16)
                sp.dma_start(pscale[:, :], pool_scale[l].rearrange("(g p) -> p g", p=P),
                             allow_slow_non_contiguous=True).then_inc(ld_small, 16)
                sp.dma_start(kr[:, 0, :], cache_krope[0, l]).then_inc(ld_small, 16)
                sp.wait_ge(blocks_done, l * NBLK + 2)
                sp.dma_start(cache_n, cache_ckv[0, l]).then_inc(ld_small, 16)
                for dst, src in ((gqa, q_a_norm_g), (gkva, kv_a_norm_g)):
                    sp.dma_start(dst, src[l].rearrange("(a n) -> a n", a=1).broadcast_to([P, dst.shape[1]]))\
                      .then_inc(ld_small, 16)
                sp.dma_start(win[:, :, :], w_in[l].rearrange("(k p) n -> p k n", p=P)).then_inc(ld_win, 16)
                sp.dma_start(wuq[:, :, :], w_uq[l].rearrange("(k p) n -> p k n", p=P)).then_inc(ld_low, 16)
                sp.dma_start(wukv[:, :, :], w_ukv[l].rearrange("(k p) n -> p k n", p=P)).then_inc(ld_low, 16)
                sp.dma_start(pw[:, :, :], pool_w[l].rearrange("g p n -> p g n")).then_inc(ld_low, 16)
                sp.dma_start(wo[0][:, :, :], w_out[l, :, 0:HALF].rearrange("(k p) n -> p k n", p=P))\
                  .then_inc(ld_wo[0], 16)
                load_ada(2)
                sp.wait_ge(proj_used, l + 1)
                sp.dma_start(wo[1][:, :, :], w_out[l, :, HALF:D].rearrange("(k p) n -> p k n", p=P))\
                  .then_inc(ld_wo[1], 16)
                sp.wait_ge(gain_used, l * 2 + 1)
                sp.dma_start(gain[:, :], norm2_g[l].rearrange("(a n) -> a n", a=1).broadcast_to([P, D]))\
                  .then_inc(ld_gain, 16)
                load_ada(3)
                load_ada(4)
                load_ada(5)
                with sp.Fori(0, NBLK // 2) as i:
                    for s in range(2):
                        sp.wait_ge(blocks_done, (l * NBLK + s + 1) + i * 2)
                        sp.wait_ge(eid_ready, l + 1)
                        e = sp.value_load(eid[0:1, bass.ds(i * 2 + s, 1)], min_val=0, max_val=NE - 1)
                        sp.dma_start(wgu[s][:, :, 0:DE], w_gate[l, e].rearrange("(k p) n -> p k n", p=P))\
                          .then_inc(ld_exp[s], 16)
                        sp.dma_start(wgu[s][:, :, DE:2 * DE], w_up[l, e].rearrange("(k p) n -> p k n", p=P))\
                          .then_inc(ld_exp[s], 16)
                        sp.dma_start(wd[s][:, :, :], w_down[l, e].rearrange("(k p) n -> p k n", p=P))\
                          .then_inc(ld_exp[s], 16)
            sp.wait_ge(layer_go, DEPTH)
            sp.dma_start(y_prompt[0], x[:, 0, :]).then_inc(out_done, 16)
            sp.dma_start(y_sample[0].rearrange("(t p) d -> p t d", p=P), x[:, 1:NT, :]).then_inc(out_done, 16)
            sp.wait_ge(out_done, (DEPTH + 2) * 16)

        @block.tensor
        def _(pe):
            mm, tr = nc.tensor.matmul, nc.tensor.transpose
            pe.sem_inc(blocks_done, 2)
            pe.sem_inc(ada_used, 1)
            pe.sem_inc(wo_used, 1)
            pe.wait_ge(ld_start, 16 * 7)
            tr(a7[:, 0:16], crow, ident[0:16, 0:16]).then_inc(cond_t, 1)
            pe.wait_ge(cond_s, 1)
            with pe.Fori(0, DEPTH) as l:
                quarter = [0]

                def ada_step(p, n, step):
                    a = 2 * p + n
                    if step < 2:
                        q = quarter[0]
                        pe.wait_ge(ld_ada[q % 2], (l * (2 * NPIECE) + q // 2 + 1) * 16)
                        if step == 0 and a > 0:
                            pe.wait_ge(ada_bc_s, 2 * a)
                        for k in range(4):
                            m = mm(a7[32 * k:32 * k + 32, :], condT[:, 4 * step + k, :], ada_ring[q % 2][:, k, :],
                                   start=(step == 0), stop=(step == 1 and k > 0), tile_position=(0, 32 * k),
                                   skip_group_check=True)
                        m.then_inc(ada_used, 1)
                        quarter[0] += 1
                        if step == 1:
                            mm(a7[0:32, :], k_("bias_sel")[0:12, 32 * a:32 * a + 32], bias_rows[:, :], start=False,
                               stop=True, skip_group_check=True).then_inc(ada_part, 1)
                    else:
                        cnd = step - 2
                        pe.wait_ge(ada_part_s, a + 1)
                        if cnd:
                            pe.wait_ge(ada_bc_s, 2 * a + 1)
                        mm(a7[:, :], k_(f"sel{cnd}"), part_s[:, :], start=True, stop=True).then_inc(ada_bc, 1)

                def ada(p):
                    for n in range(2):
                        for step in range(4):
                            ada_step(p, n, step)

                pe.wait_ge(ld_bias, (l + 1) * 16)
                ada(0)
                ada(1)

                def turn_h(t, first):
                    j = first + t
                    pe.wait_ge(h_ready, j + 1)
                    if j > 0:
                        pe.wait_ge(h_ta, j)
                        pe.wait_ge(h_td, j)
                    for k in range(DC):
                        dst = (tb4, tb5)[k // 4]
                        m = tr(dst[:, (k % 4) * P:(k % 4 + 1) * P], xn[t % 2][:, k * P:(k + 1) * P], ident)
                    m.then_inc(h_t, 1)

                def in_proj(t):
                    pe.wait_ge(h_ta, t + 1)
                    pe.wait_ge(h_td, t + 1)
                    if t == 0:
                        pe.wait_ge(ld_win, (l + 1) * 16)
                    if t >= 2:
                        pe.wait_ge(in_act, t - 1)
                        pe.wait_ge(in_dve, t - 1)
                    for lo, n, at in ((POOLW, QR, 0), (POOLW + QR, KVR + ROPE, HALF)):
                        for k in range(DC):
                            m = mm(pair[t % 2][:, at:at + n], actT[:, k, t * P:(t + 1) * P], win[:, k, lo:lo + n],
                                   start=(k == 0), stop=(k == DC - 1))
                    m.then_inc(in_mm, 1)

                def turn_low(j):
                    if j < NT:
                        pe.wait_ge(in_dve, j + 1)
                    else:
                        pe.wait_ge(ld_small, (l + 1) * (7 * 16))
                    if j > 0:
                        pe.wait_ge(low_ta, min(j, NT))
                        pe.wait_ge(low_td, j)
                    if j < NT:
                        for k in range(QC):
                            m = tr(o6[:, k * P:(k + 1) * P], cn[:, k * P:(k + 1) * P], ident)
                    for k in range(KC):
                        src = cn[:, QR + k * P:QR + (k + 1) * P] if j < NT else cache_n[:, k * P:(k + 1) * P]
                        m = tr(a7[:, k * P:(k + 1) * P], src, ident)
                    m.then_inc(low_t, 1)

                turn_h(0, 0)
                for t in range(NT):
                    if t + 1 < NT:
                        turn_h(t + 1, 0)
                    in_proj(t)
                    if t == 0:
                        pe.wait_ge(ada_bc_s, 8)
                    if t > 0:
                        turn_low(t - 1)
                for g in range(NG):
                    j = NT + g
                    pe.wait_ge(in_act, j - 1)
                    pe.wait_ge(in_dve, j - 1)
                    for at, t0, n in ((0, P, DEC), (HALF, 0, P)):
                        for k in range(DC):
                            m = mm(pair[j % 2][:, at:at + n], win[:, k, g * P:(g + 1) * P], actT[:, k, t0:t0 + n],
                                   start=(k == 0), stop=(k == DC - 1))
                    m.then_inc(in_mm, 1)
                    if g == 0:
                        turn_low(NT - 1)
                    if g == 1:
                        turn_low(NT)
                pe.wait_ge(in_act, NT + NG)
                pe.wait_ge(in_dve, NT + NG)

                pe.wait_ge(ld_low, (l + 1) * 48)

                def q_proj(t):
                    pe.wait_ge(low_ta, t + 1)
                    if t > 0:
                        pe.wait_ge(q_sq, t)
                        pe.wait_ge(q_rd, t)
                    for n in range(2):
                        for k in range(QC):
                            m = mm(pair[0][:, n * HALF:n * HALF + 4 * QH], cqT[:, k, t * P:(t + 1) * P],
                                   wuq[:, k, n * 4 * QH:(n + 1) * 4 * QH], start=(k == 0), stop=(k == QC - 1))
                    m.then_inc(q_mm, 1)

                def kv_proj(j):
                    kt = KV_ORDER[j]
                    pe.wait_ge(low_td, j + 1)
                    if j > 0:
                        pe.wait_ge(k_sq, j)
                        pe.wait_ge(v_cp, j)
                        pe.wait_ge(k_rd, j)
                    for n in range(2):
                        for k in range(KC):
                            m = mm(pair[1][:, n * HALF:(n + 1) * HALF], ckvT[:, k, kt * P:(kt + 1) * P],
                                   wukv[:, k, n * HALF:(n + 1) * HALF], start=(k == 0), stop=(k == KC - 1))
                    m.then_inc(kv_mm, 1)

                def turn_heads(src, job):
                    if job > 0:
                        pe.wait_ge(qk_ta, job)
                        pe.wait_ge(qk_td, job)
                    else:
                        pe.wait_ge(h_ta, NT)
                        pe.wait_ge(h_td, NT)
                    for h in range(H):
                        dst = (tb4, tb5)[h // 4]
                        m = tr(dst[0:QH, (h % 4) * P:(h % 4 + 1) * P], src[:, h, :], ident)
                    m.then_inc(qk_t, 1)

                q_proj(0)
                kv_proj(0)
                for j in range(NT + 1):
                    if j < NT:
                        pe.wait_ge(q_n, j + 1)
                        turn_heads(qn, 2 * j)
                        if j + 1 < NT:
                            q_proj(j + 1)
                    pe.wait_ge(k_n, j + 1)
                    turn_heads(kn, 2 * j + 1 if j < NT else 2 * NT)
                    if j + 1 <= NT:
                        kv_proj(j + 1)
                for g in range(NG):
                    pe.wait_ge(pool_d, g + 1)
                    if g == 0:
                        pe.wait_ge(k_rd, NT + 1)
                        pe.wait_ge(v_cp, NT + 1)
                        pe.wait_ge(k_sq, NT + 1)
                    if g >= 2:
                        pe.wait_ge(pool_ea, g - 1)
                        pe.wait_ge(pool_ed, g - 1)
                    mm(pair[g % 2][:, 0:DEC], pw[:, g, :], u[:, g, LAT0:LAT0 + DEC], start=True, stop=True)
                    mm(pair[g % 2][:, HALF:HALF + SEQ], pw[:, g, :], u[:, g, CTX0:CTX0 + SEQ], start=True, stop=True)\
                        .then_inc(pool_mm, 1)
                pe.wait_ge(pool_mm, NG)
                pe.sem_inc(proj_used, 1)

                def scores(un):
                    t, h = UNITS[un]
                    if un < 2:
                        if un == 0:
                            pe.wait_ge(qk_ta, 2 * NT + 1)
                            pe.wait_ge(qk_td, 2 * NT + 1)
                        pe.wait_ge(pool_ea, NG - 1 + un)
                        pe.wait_ge(pool_ed, NG - 1 + un)
                    else:
                        pe.wait_ge(s_exp, un - 1)
                    q = qT[0:QH, h, t * P:(t + 1) * P]
                    dst = pair[un % 2]
                    if t == 0:
                        m = mm(dst[:, 0:P], q, kT[0:QH, h, CTX * P:NKT * P], start=True, stop=True)
                    else:
                        mm(dst[:, 0:HALF], q, kT[0:QH, h, 0:HALF], start=True, stop=True)
                        m = mm(dst[:, HALF:NLK * P], q, kT[0:QH, h, HALF:NLK * P], start=True, stop=True)
                    m.then_inc(s_sc, 1)

                def turn_prob(un):
                    t, h = UNITS[un]
                    pe.wait_ge(s_exp, un + 1)
                    if un > 0:
                        pe.wait_ge(s_pta, un)
                        pe.wait_ge(s_ptb, un)
                    for k in range(1 if t == 0 else NLK):
                        dst = tb4[:, k * P:(k + 1) * P] if k < 3 else tb5[:, (k - 3) * P:(k - 2) * P]
                        m = tr(dst, prob[un % 2][:, k, :], ident)
                    m.then_inc(s_pt, 1)

                def weigh(un):
                    t, h = UNITS[un]
                    pe.wait_ge(s_pta, un + 1)
                    pe.wait_ge(s_ptb, un + 1)
                    if h == 0 and t > 0:
                        pe.wait_ge(s_on, t)
                    tiles = [CTX] if t == 0 else list(range(NLK))
                    for k, kt in enumerate(tiles):
                        m = mm(o6[:, h * VH:(h + 1) * VH], probT[un % 2][:, k, :], V[:, kt, h * VH:(h + 1) * VH],
                               start=(k == 0), stop=(k == len(tiles) - 1))
                    m.then_inc(s_pv, 1)

                def turn_out(t):
                    pe.wait_ge(s_on, t + 1)
                    pe.wait_ge(s_pta, min(NU, (t + 1) * H + 1))
                    for k in range(4):
                        m = tr(tb4[:, k * P:(k + 1) * P], onat[:, k * P:(k + 1) * P], ident)
                    m.then_inc(s_ot, 1)
                    pe.wait_ge(s_otc, t + 1)

                scores(0)
                for un in range(NU + 2):
                    if un + 1 < NU:
                        scores(un + 1)
                    if 1 <= un <= NU:
                        weigh(un - 1)
                    if un >= H + 1 and (un - 1) % H == 0:
                        turn_out((un - 1) // H - 1)
                    if un < NU:
                        turn_prob(un)
                    if un in ADA_AT:
                        ada_step(*ADA_AT[un])
                pe.wait_ge(s_otc, NT)

                for n in range(2):
                    pe.wait_ge(ld_wo[n], (l + 1) * 16)
                    for t in range(NT):
                        j = n * NT + t
                        if j >= 4:
                            pe.wait_ge(op_g, j - 3)
                        dst = pair[(j % 4) // 2][:, (j % 2) * HALF:(j % 2 + 1) * HALF]
                        for k in range(DC):
                            m = mm(dst, actT[:, k, t * P:(t + 1) * P], wo[n][:, k, :], start=(k == 0),
                                   stop=(k == DC - 1))
                        m.then_inc(op_mm, 1)
                pe.wait_ge(op_mm, 2 * NT)
                pe.sem_inc(wo_used, 1)

                turn_h(0, NT)
                for t in range(NT):
                    if t + 1 < NT:
                        turn_h(t + 1, NT)
                    pe.wait_ge(h_ta, NT + t + 1)
                    pe.wait_ge(h_td, NT + t + 1)
                    for k in range(DC):
                        m = mm(o6[:, t * NE:(t + 1) * NE], actT[:, k, t * P:(t + 1) * P], rw[:, k, :],
                               start=(k == 0), stop=(k == DC - 1))
                m.then_inc(r_mm, 1)
                pe.wait_ge(r_mask, 1)
                pe.wait_ge(op_g, 2 * NT)
                pos = pair[0][:, 0:NT * NE].rearrange("p (t e) -> p t e", e=NE)
                mm(pos, k_("before"), mask, start=True, stop=False, skip_group_check=True)
                for i in range(NT - 1):
                    for t in range(i + 1, NT):
                        m = mm(pos[:, t, :], k_("ones"), mask[:, i, :], start=False, stop=(i == NT - 2),
                               skip_group_check=True)
                for i in range(NT):
                    m = mm(pair[0][:, HALF:HALF + NE], k_("ones"), mask[:, i, :], start=(i == 0), stop=(i == NT - 1))
                m.then_inc(r_tot, 1)
                for j in range(2 * NT):
                    pe.wait_ge(r_one, j + 1)
                    mm(pair[1][:, 0:NBLK], onep[j % 2], oneb[j % 2], start=(j == 0), stop=(j == 2 * NT - 1))\
                        .then_inc(r_pe1, 1)
                ada(5)

                pe.sem_inc(b_at, 1)
                with pe.Fori(0, NBLK // 2) as i:
                    for s in range(2):
                        b = i * 2 + s
                        pe.wait_ge(g_in[s], l * (NBLK // 2 * 16) + (i * 16 + 16))
                        pe.wait_ge(b_ta, b + 1)
                        pe.wait_ge(b_td, b + 1)
                        for k in range(DC):
                            m = tr(pair[0][:, k * P:(k + 1) * P], xg[s][:, k * P:(k + 1) * P], ident)
                        m.then_inc(b_t, 1)
                        pe.wait_ge(b_ta, b + 2)
                        pe.wait_ge(b_td, b + 2)
                        pe.wait_ge(ld_exp[s], l * (NBLK // 2 * 48) + (i * 48 + 48))
                        pe.wait_ge(b_act, b + 1)
                        for k in range(DC):
                            m = mm(tb4[:, :], xgT[s][:, k, :], wgu[s][:, k, :], start=(k == 0), stop=(k == DC - 1))
                        m.then_inc(b_gu, 1)
                        pe.wait_ge(b_act, b + 2)
                        for k in range(2):
                            m = tr(tb5[:, k * P:(k + 1) * P], act_n[:, k * P:(k + 1) * P], ident)
                        m.then_inc(b_at, 1)
                        pe.wait_ge(b_atc, b + 1)
                        pe.wait_ge(b_ya, b + 1)
                        pe.wait_ge(b_yd, b + 1)
                        for n in range(2):
                            for k in range(2):
                                m = mm(pair[1][:, n * HALF:(n + 1) * HALF], acT[:, k, :],
                                       wd[s][:, k, n * HALF:(n + 1) * HALF], start=(k == 0), stop=(k == 1))
                        m.then_inc(b_dn, 1)
                        pe.wait_ge(b_dn, b + 1)
                        pe.sem_inc(blocks_done, 1)
                pe.sem_inc(layer_end, 1)
                pe.wait_ge(layer_go, l + 1)

        @block.scalar
        def _(act):
            f = nc.scalar.activation
            act.wait_ge(cond_t, 1)
            act.wait_ge(start_d, 1)
            act.wait_ge(ld_start, 16 * 7)
            f(condT[:, :, 0:2], a7[:, 0:16].rearrange("p (c k) -> p k c", k=DC), ACT.Silu).then_inc(cond_s, 1)
            with act.Fori(0, DEPTH) as l:
                def ada_rows(a):
                    act.wait_ge(ada_part, a + 1)
                    if a > 0:
                        act.wait_ge(ada_bc, 2 * a)
                    f(part_s[:, :], a7[:, :], ACT.Copy).then_inc(ada_part_s, 1)

                def evac_h(t, first):
                    act.wait_ge(h_t, first + t + 1)
                    f(actT[:, 0:4, t * P:(t + 1) * P], tb4[:, :].rearrange("p (k n) -> p k n", n=P), ACT.Copy)\
                        .then_inc(h_ta, 1)

                for t in range(NT):
                    if t > 0:
                        act.wait_ge(x_sq, t)
                    f(sq_x, x[:, t, :], ACT.Square, accum_out=ss[:, t:t + 1]).then_inc(x_sq, 1)
                for a in range(4):
                    ada_rows(a)

                def low_squares(t):
                    act.wait_ge(in_mm, t + 1)
                    if t > 0:
                        act.wait_ge(low_sq, t)
                    src = pair[t % 2]
                    f(sq_cq, src[:, 0:QR], ACT.Square, accum_out=low_ss[:, t, 0:1])
                    f(sq_ckv, src[:, HALF:HALF + KVR], ACT.Square, accum_out=low_ss[:, t, 1:2]).then_inc(low_sq, 1)
                    f(kr[:, key_tile(t), :], src[:, HALF + KVR:HALF + KVR + ROPE], ACT.Copy).then_inc(in_act, 1)

                def evac_cq(t):
                    act.wait_ge(low_t, t + 1)
                    f(cqT[:, :, t * P:(t + 1) * P], o6[:, 0:QR].rearrange("p (k n) -> p k n", n=P), ACT.Copy)\
                        .then_inc(low_ta, 1)

                evac_h(0, 0)
                for t in range(NT):
                    if t + 1 < NT:
                        evac_h(t + 1, 0)
                    low_squares(t)
                    if t == 0:
                        act.wait_ge(in_act, 1)
                        act.dma_start(new_krope[0, l], kr[:, CTX, :]).then_inc(out_done, 16)
                    if t > 0:
                        evac_cq(t - 1)
                    if t == 1:
                        act.wait_ge(keep_s, 1)
                        act.dma_start(new_ckv[0, l], ckv_keep).then_inc(keep_out, 16)
                for g in range(NG):
                    j = NT + g
                    act.wait_ge(in_mm, j + 1)
                    f(u[:, g, LAT0:LAT0 + DEC], pair[j % 2][:, 0:DEC], ACT.Copy).then_inc(in_act, 1)
                    if g == 0:
                        evac_cq(NT - 1)

                def q_squares(t):
                    act.wait_ge(q_mm, t + 1)
                    if t > 0:
                        act.wait_ge(q_ss, t)
                    for n in range(2):
                        m = f(sq_q[:, 4 * n:4 * n + 4, :],
                              pair[0][:, n * HALF:n * HALF + 4 * QH].rearrange("p (h d) -> p h d", d=QH), ACT.Square)
                    m.then_inc(q_sq, 1)

                def kv_read(j):
                    kt = KV_ORDER[j]
                    act.wait_ge(kv_mm, j + 1)
                    if j > 0:
                        act.wait_ge(k_ss, j)
                    f(sq_kr, kr[:, kt, :], ACT.Square, accum_out=kr_ss[:, kt:kt + 1])
                    for n in range(2):
                        m = f(sq_k[:, 4 * n:4 * n + 4, :],
                              pair[1][:, n * HALF:(n + 1) * HALF].rearrange("p (h d) -> p h d", d=P)[:, :, 0:NOPE],
                              ACT.Square)
                    m.then_inc(k_sq, 1)
                    for n in range(2):
                        m = f(V[:, kt, n * 256:(n + 1) * 256].rearrange("p (h d) -> p h d", d=VH),
                              pair[1][:, n * HALF:(n + 1) * HALF].rearrange("p (h d) -> p h d", d=P)[:, :, NOPE:P],
                              ACT.Copy)
                    m.then_inc(v_cp, 1)

                def evac_heads(dst, tile, job):
                    act.wait_ge(qk_t, job + 1)
                    f(dst[0:QH, 0:4, tile * P:(tile + 1) * P], tb4[0:QH, :].rearrange("p (k n) -> p k n", n=P),
                      ACT.Copy).then_inc(qk_ta, 1)

                act.wait_ge(ld_small, (l + 1) * (7 * 16))
                act.wait_ge(keep_out, 16)
                q_squares(0)
                kv_read(0)
                for j in range(NT + 1):
                    if j < NT:
                        evac_heads(qT, j, 2 * j)
                        if j + 1 < NT:
                            q_squares(j + 1)
                    evac_heads(kT, KV_ORDER[j], 2 * j + 1 if j < NT else 2 * NT)
                    if j + 1 <= NT:
                        kv_read(j + 1)
                for g in range(NG):
                    act.wait_ge(pool_mm, g + 1)
                    f(actT[:, g, P:NTOK], pair[g % 2][:, 0:DEC], ACT.Copy, scale=pscale[:, g:g + 1])\
                        .then_inc(pool_ea, 1)

                def exps(un):
                    t, _ = UNITS[un]
                    n = 1 if t == 0 else NLK
                    act.wait_ge(s_mx, un + 1)
                    if un >= 2:
                        act.wait_ge(s_pt, un - 1)
                    f(prob[un % 2][:, 0:n, :], pair[un % 2][:, 0:n * P].rearrange("p (k n) -> p k n", n=P), ACT.Exp,
                      bias=nmax[:, un % 2:un % 2 + 1], scale=SCALE, accum_out=esum[:, un:un + 1]).then_inc(s_exp, 1)

                for un in range(NU + 2):
                    if un < NU:
                        exps(un)
                    if un >= H + 1 and (un - 1) % H == 0:
                        t = (un - 1) // H - 1
                        act.wait_ge(s_ot, t + 1)
                        f(actT[:, 4:8, t * P:(t + 1) * P], tb4[:, :].rearrange("p (k n) -> p k n", n=P), ACT.Copy)\
                            .then_inc(s_otc, 1)
                    if un < NU:
                        n = 1 if UNITS[un][0] == 0 else 3
                        act.wait_ge(s_pt, un + 1)
                        if un >= 2:
                            act.wait_ge(s_pv, un - 1)
                        f(probT[un % 2][:, 0:n, :], tb4[:, 0:n * P].rearrange("p (k n) -> p k n", n=P), ACT.Copy)\
                            .then_inc(s_pta, 1)
                    if un in ADA_AT and ADA_AT[un][2] == 1:
                        ada_rows(2 * ADA_AT[un][0] + ADA_AT[un][1])

                for t in range(NT):
                    act.wait_ge(op_x, NT + t + 1)
                    act.wait_ge(x_sq, NT + t)
                    f(sq_x, x[:, t, :], ACT.Square, accum_out=ss[:, NT + t:NT + t + 1]).then_inc(x_sq, 1)
                for t in range(NT):
                    evac_h(t, NT)
                    act.wait_ge(h_ready, NT + t + 1)
                    act.dma_start(h2_rows[t * P:(t + 1) * P, :], xn[t % 2]).then_inc(h_st[t % 2], 16)
                act.wait_ge(r_mm, 1)
                f(sig, o6[:, 0:NT * NE].rearrange("p (a b) -> p a b", b=GE), ACT.Exp, scale=-1.0).then_inc(r_e, 1)
                ada_rows(10)
                ada_rows(11)

                for count, n in ((b_ta, 1), (b_ya, 1), (b_st, 16)):
                    act.sem_inc(count, n)
                with act.Fori(0, NBLK // 2) as i:
                    for s in range(2):
                        b = i * 2 + s
                        act.wait_ge(b_t, b + 1)
                        f(xgT[s][:, 0:4, :], pair[0][:, 0:HALF].rearrange("p (k n) -> p k n", n=P), ACT.Copy)\
                            .then_inc(b_ta, 1)
                        act.wait_ge(b_gu, b + 1)
                        f(sil, tb4[:, 0:DE], ACT.Silu).then_inc(b_sil, 1)
                        act.wait_ge(b_at, b + 2)
                        f(acT[:, :, :], tb5[:, 0:2 * P].rearrange("p (k n) -> p k n", n=P), ACT.Copy).then_inc(b_atc, 1)
                        act.wait_ge(b_dn, b + 1)
                        act.wait_ge(b_st, b * 16 + 16)
                        f(yb[:, 0:HALF], pair[1][:, 0:HALF], ACT.Copy).then_inc(b_ya, 1)
                        act.wait_ge(b_ya, b + 2)
                        act.wait_ge(b_yd, b + 2)
                        act.dma_start(y_rows[bass.ds(b * P, P), :], yb).then_inc(b_st, 16)
                for t in range(NT):
                    k = (2 * t) % 4
                    act.wait_ge(c_in[k], l * (C_USES[k] * 16) + (t // 2 + 1) * 16)
                    f(comb[k], comb[k], ACT.Copy, scale=gates2[:, t:t + 1]).then_inc(c_hi, 1)
                act.sem_inc(layer_end, 1)
                act.wait_ge(layer_go, l + 1)
            

        @block.gpsimd
        def _(pool):
            tt, ts = nc.gpsimd.tensor_tensor, nc.gpsimd.tensor_scalar
            mhalf = k_("mhalf")
            with pool.Fori(0, DEPTH) as l:
                chain = [0]

                def link(ins):
                    ins.then_inc(pl, 1)
                    chain[0] += 1
                    pool.wait_ge(pl, chain[0])

                def row_rs(j):
                    pool.wait_ge(x_sq, j + 1)
                    link(ts(ss[:, j:j + 1], ss[:, j:j + 1], 1.0 / D, EPS, ALU.mult, ALU.add))
                    tt(rs[:, j:j + 1], ss[:, j:j + 1], mhalf[:, 0:1], ALU.pow).then_inc(x_rs, 1)

                pool.wait_ge(ld_start, 16 * 7)
                for t in range(NT):
                    row_rs(t)
                for t in range(NT):
                    pool.wait_ge(low_sq, t + 1)
                    ts(low_ss[:, t, 0:1], low_ss[:, t, 0:1], 1.0 / QR, EPS, ALU.mult, ALU.add)
                    link(ts(low_ss[:, t, 1:2], low_ss[:, t, 1:2], 1.0 / KVR, EPS, ALU.mult, ALU.add))
                    tt(low_rs[:, t, :], low_ss[:, t, :], mhalf[:, 0:2], ALU.pow).then_inc(low_r, 1)
                pool.wait_ge(h_ready, NT)
                for lo, hi in ((0, GAP), (GAP + SEQ, LAT0), (LAT0 + DEC, PW)):
                    m = nc.gpsimd.memset(u[:, :, lo:hi], 0.0)
                m.then_inc(pool_z, 1)

                def rope_key(j):
                    kt = KV_ORDER[j]
                    if j == 0:
                        pool.wait_ge(ld_small, (l + 1) * (7 * 16))
                    if not 1 <= kt <= NT - 1:
                        tt(krr[:, kt, :], kr[:, kt, :], gk[:, NOPE:QH], ALU.mult).then_inc(krr_s, 1)
                        return
                    link(tt(rope_t[:, 0, :], kr[:, kt, :], gk[:, NOPE:QH], ALU.mult))
                    hr = ROPE // 2
                    a, c2 = rope_t[:, 0, :], rope_t[:, 1, :]
                    cos, sin = (k_(n)[:, (kt - 1) * hr:kt * hr] for n in ("cos", "sin"))
                    link(tt(krr[:, kt, 0:hr], a[:, 0:hr], cos, ALU.mult))
                    link(tt(krr[:, kt, hr:ROPE], a[:, 0:hr], sin, ALU.mult))
                    link(tt(c2[:, 0:hr], a[:, hr:ROPE], sin, ALU.mult))
                    link(tt(c2[:, hr:ROPE], a[:, hr:ROPE], cos, ALU.mult))
                    tt(krr[:, kt, 0:hr], krr[:, kt, 0:hr], c2[:, 0:hr], ALU.subtract)
                    tt(krr[:, kt, hr:ROPE], krr[:, kt, hr:ROPE], c2[:, hr:ROPE], ALU.add).then_inc(krr_s, 1)

                def head_rs_of(j, which):
                    s_ = head_ss[:, j % 2, which, :]
                    if which == 1:
                        kt = KV_ORDER[j]
                        link(tt(s_, s_, kr_ss[:, kt:kt + 1].broadcast_to([P, H]), ALU.add))
                    link(ts(s_, s_, 1.0 / QH, EPS, ALU.mult, ALU.add))
                    tt(head_rs[:, j % 2, which, :], s_, mhalf, ALU.pow).then_inc((q_rs, k_rs)[which], 1)

                def pool_group(g):
                    if g == 0:
                        pool.wait_ge(in_act, NT + NG)
                        pool.wait_ge(in_dve, NT + NG)
                        pool.wait_ge(pool_z, 1)
                    src, bufs = u[:, g, :], (pa, pb)
                    link(tt(pa[:, 1:PW], src[:, 0:PW - 1], src[:, 1:PW], ALU.add))
                    for lv in range(1, g + 1):
                        r, lo = 1 << (lv - 1), 1 << lv
                        hi = PW + 1 - lo
                        a, b = bufs[(lv - 1) % 2], bufs[lv % 2]
                        link(tt(b[:, lo:hi], a[:, lo - r:hi - r], a[:, lo + r:hi + r], ALU.add))
                    w = bufs[g % 2]
                    e = k_("edge")[:, 16 * g:16 * g + 16]
                    for first, n in ((CTX0, SEQ), (LAT0, DEC)):
                        link(tt(w[:, first:first + 8], w[:, first:first + 8], e[:, 0:8], ALU.mult))
                        link(tt(w[:, first + n - 8:first + n], w[:, first + n - 8:first + n], e[:, 8:16], ALU.mult))
                    link(ts(w[:, GAP:PW - GAP], w[:, GAP:PW - GAP], 1.0 / WINDOWS[g], 0.0, ALU.mult, ALU.add))
                    tt(u[:, g, GAP:PW - GAP], w[:, GAP:PW - GAP], u[:, g, GAP:PW - GAP], ALU.subtract)\
                        .then_inc(pool_d, 1)

                for j in range(NT + 1):
                    if j < NT:
                        pool.wait_ge(q_ss, j + 1)
                        if j >= 2:
                            pool.wait_ge(q_rd, j - 1)
                        head_rs_of(j, 0)
                    rope_key(j)
                    pool.wait_ge(k_ss, j + 1)
                    if j >= 2:
                        pool.wait_ge(k_n, j - 1)
                    head_rs_of(j, 1)
                    if j < NG:
                        pool_group(j)

                for j in range(2 * NT):
                    n, t = divmod(j, NT)
                    pool.wait_ge(op_g, j + 1)
                    xs = x[:, t, n * HALF:(n + 1) * HALF]
                    tt(xs, xs, out_s[j % 4], ALU.add).then_inc(op_x, 1)
                for t in range(NT):
                    row_rs(NT + t)

                pool.wait_ge(r_idx, 1)
                pool.wait_ge(h_st[0], 16 * 3)
                pool.wait_ge(h_st[1], 16 * 2)
                pool.wait_ge(h_t, 2 * NT)
                for b in range(NBLK):
                    if b >= 2:
                        pool.wait_ge(b_t, b - 1)
                    nc.gpsimd.indirect_dma_start(
                        xg[b % 2], None, h2_rows, bass.IndirectOffsetOnAxis(ap=idx[:, b:b + 1], axis=0))\
                        .then_inc(g_in[b % 2], 16)
                pool.wait_ge(b_st, (NBLK + 1) * 16)
                for t in range(NT):
                    for w in range(2):
                        k = (2 * t + w) % 4
                        if t >= 2:
                            pool.wait_ge(c_gt, t - 1)
                        nc.gpsimd.indirect_dma_start(
                            comb[k], None, y_rows,
                            bass.IndirectOffsetOnAxis(ap=slot_i[:, w * NT + t:w * NT + t + 1], axis=0))\
                            .then_inc(c_in[k], 16)
                pool.sem_inc(layer_end, 1)
                pool.wait_ge(layer_go, l + 1)

        @block.vector
        def _(ve):
            v = nc.vector
            v.memset(condT[:, :, :], 0.0).then_inc(start_d, 1)
            with ve.Fori(0, DEPTH) as l:
                chain = [0]

                def link(ins):
                    ins.then_inc(dv, 1)
                    chain[0] += 1
                    ve.wait_ge(dv, chain[0])

                def ada_half(a, cnd):
                    p, n = divmod(a, 2)
                    cols = slice(n * HALF, (n + 1) * HALF)
                    ve.wait_ge(ada_bc, 2 * a + cnd + 1)
                    if p % 3 == 1:
                        ve.wait_ge(ld_gain, l * 32 + (16 if p == 1 else 32))
                        m = v.scalar_tensor_tensor(G[:, cnd, cols], a7[:, :], 1.0, gain[:, cols], ALU.add, ALU.mult)
                    else:
                        m = v.tensor_copy((S if p % 3 == 0 else gate)[:, cnd, cols], a7[:, :])
                    m.then_inc(ada_bc_s, 1)

                def ada_out(a):
                    ada_half(a, 0)
                    ada_half(a, 1)

                def norm(t, j):
                    ve.wait_ge(x_rs, j + 1)
                    if j >= 2:
                        ve.wait_ge(h_t, j - 1)
                    if j >= NT + 2:
                        ve.wait_ge(h_st[t % 2], 16 * (t // 2))
                    c2 = ctx_of(t)
                    link(v.scalar_tensor_tensor(xn[t % 2], x[:, t, :], rs[:, j:j + 1], G[:, c2, :], ALU.mult, ALU.mult))
                    v.tensor_tensor(xn[t % 2], xn[t % 2], S[:, c2, :], ALU.add).then_inc(h_ready, 1)

                def evac_h(t, first):
                    ve.wait_ge(h_t, first + t + 1)
                    v.tensor_copy(actT[:, 4:8, t * P:(t + 1) * P], tb5[:, :].rearrange("p (k n) -> p k n", n=P))\
                        .then_inc(h_td, 1)

                ve.wait_ge(ld_start, 16 * 7)
                for a in range(4):
                    ada_out(a)
                ve.wait_ge(ada_bc_s, 8)
                ve.sem_inc(gain_used, 1)
                norm(0, 0)
                norm(1, 1)

                def low_norm(t):
                    ve.wait_ge(low_r, t + 1)
                    ve.wait_ge(in_act, t + 1)
                    if t > 0:
                        ve.wait_ge(low_t, t)
                    else:
                        ve.wait_ge(ld_small, (l + 1) * (7 * 16))
                    src = pair[t % 2]
                    stt = v.scalar_tensor_tensor
                    if t == 0:
                        stt(ckv_keep, src[:, HALF:HALF + KVR], low_rs[:, t, 1:2], gkva, ALU.mult, ALU.mult)\
                            .then_inc(keep_s, 1)
                    stt(cn[:, 0:QR], src[:, 0:QR], low_rs[:, t, 0:1], gqa, ALU.mult, ALU.mult)
                    stt(cn[:, QR:QR + KVR], src[:, HALF:HALF + KVR], low_rs[:, t, 1:2], gkva, ALU.mult, ALU.mult)\
                        .then_inc(in_dve, 1)

                def evac_ckv(j):
                    kt = KV_ORDER[j]
                    ve.wait_ge(low_t, j + 1)
                    v.tensor_copy(ckvT[:, :, kt * P:(kt + 1) * P], a7[:, 0:KVR].rearrange("p (k n) -> p k n", n=P))\
                        .then_inc(low_td, 1)

                evac_h(0, 0)
                for t in range(NT):
                    if t + 2 < NT:
                        norm(t + 2, t + 2)
                    if t + 1 < NT:
                        evac_h(t + 1, 0)
                    low_norm(t)
                    if t > 0:
                        evac_ckv(t - 1)
                for g in range(NG):
                    j = NT + g
                    ve.wait_ge(in_mm, j + 1)
                    v.tensor_copy(u[:, g, CTX0:CTX0 + SEQ], pair[j % 2][:, HALF:HALF + SEQ]).then_inc(in_dve, 1)
                    if g == 0:
                        evac_ckv(NT - 1)
                    if g == 1:
                        evac_ckv(NT)

                def bc(a, n):
                    return a.unsqueeze(2).broadcast_to([P, a.shape[1], n])

                def q_norm(t):
                    ve.wait_ge(q_sq, t + 1)
                    v.tensor_reduce(head_ss[:, t % 2, 0, :], sq_q, AX.X, ALU.add).then_inc(q_ss, 1)
                    ve.wait_ge(q_rs, t + 1)
                    if t > 0:
                        ve.wait_ge(qk_t, 2 * t - 1)
                    for n in range(2):
                        m = v.tensor_tensor(qn[:, 4 * n:4 * n + 4, :],
                                            pair[0][:, n * HALF:n * HALF + 4 * QH].rearrange("p (h d) -> p h d", d=QH),
                                            bc(head_rs[:, t % 2, 0, 4 * n:4 * n + 4], QH), ALU.mult)
                    m.then_inc(q_rd, 1)
                    ve.wait_ge(q_rd, t + 1)
                    gq_b = gq[:, :].unsqueeze(1).broadcast_to([P, H, QH])
                    if t == 0:
                        v.tensor_tensor(qn, qn, gq_b, ALU.mult).then_inc(q_n, 1)
                        return
                    link(v.tensor_tensor(qn, qn, gq_b, ALU.mult))
                    hr = ROPE // 2
                    r1, r2 = qn[:, :, NOPE:NOPE + hr], qn[:, :, NOPE + hr:QH]
                    cos, sin = (k_(n)[:, (t - 1) * hr:t * hr].unsqueeze(1).broadcast_to([P, H, hr])
                                for n in ("cos", "sin"))
                    v.tensor_tensor(rq[0], r1, sin, ALU.mult)
                    v.tensor_tensor(rq[1], r2, sin, ALU.mult)
                    v.tensor_tensor(rq[2], r1, cos, ALU.mult)
                    link(v.tensor_tensor(rq[3], r2, cos, ALU.mult))
                    v.tensor_tensor(r1, rq[2], rq[1], ALU.subtract)
                    v.tensor_tensor(r2, rq[0], rq[3], ALU.add).then_inc(q_n, 1)

                def k_norm(j):
                    kt = KV_ORDER[j]
                    ve.wait_ge(k_sq, j + 1)
                    v.tensor_reduce(head_ss[:, j % 2, 1, :], sq_k, AX.X, ALU.add).then_inc(k_ss, 1)
                    ve.wait_ge(k_rs, j + 1)
                    ve.wait_ge(v_cp, j + 1)
                    if j > 0:
                        ve.wait_ge(qk_t, 2 * j)
                    r = head_rs[:, j % 2, 1, :]
                    for n in range(2):
                        m = v.tensor_tensor(
                            kn[:, 4 * n:4 * n + 4, 0:NOPE],
                            pair[1][:, n * HALF:(n + 1) * HALF].rearrange("p (h d) -> p h d", d=P)[:, :, 0:NOPE],
                            bc(r[:, 4 * n:4 * n + 4], NOPE), ALU.mult)
                    m.then_inc(k_rd, 1)
                    ve.wait_ge(krr_s, j + 1)
                    v.tensor_tensor(kn[:, :, NOPE:QH], krr[:, kt, :].unsqueeze(1).broadcast_to([P, H, ROPE]),
                                    bc(r, ROPE), ALU.mult)
                    ve.wait_ge(k_rd, j + 1)
                    v.tensor_tensor(kn[:, :, 0:NOPE], kn[:, :, 0:NOPE],
                                    gk[:, 0:NOPE].unsqueeze(1).broadcast_to([P, H, NOPE]), ALU.mult).then_inc(k_n, 1)

                def evac_heads(dst, tile, job):
                    ve.wait_ge(qk_t, job + 1)
                    v.tensor_copy(dst[0:QH, 4:8, tile * P:(tile + 1) * P],
                                  tb5[0:QH, :].rearrange("p (k n) -> p k n", n=P)).then_inc(qk_td, 1)

                ve.wait_ge(low_t, NT + 1)
                ve.wait_ge(keep_out, 16)
                q_norm(0)
                k_norm(0)
                for j in range(NT + 1):
                    if j < NT:
                        evac_heads(qT, j, 2 * j)
                        if j + 1 < NT:
                            q_norm(j + 1)
                    evac_heads(kT, KV_ORDER[j], 2 * j + 1 if j < NT else 2 * NT)
                    if j + 1 <= NT:
                        k_norm(j + 1)
                for g in range(NG):
                    ve.wait_ge(pool_mm, g + 1)
                    v.tensor_scalar(actT[:, g, 0:P], pair[g % 2][:, HALF:HALF + SEQ], pscale[:, g:g + 1], None, ALU.mult)\
                        .then_inc(pool_ed, 1)

                def maxes(un):
                    t, _ = UNITS[un]
                    n = P if t == 0 else NLK * P
                    ve.wait_ge(s_sc, un + 1)
                    link(v.tensor_reduce(mx[:, un % 2:un % 2 + 1], pair[un % 2][:, 0:n], AX.X, ALU.max))
                    if un >= 2:
                        ve.wait_ge(s_exp, un - 1)
                    v.tensor_scalar(nmax[:, un % 2:un % 2 + 1], mx[:, un % 2:un % 2 + 1], -SCALE, None, ALU.mult)\
                        .then_inc(s_mx, 1)

                def tile_out(t):
                    ve.wait_ge(s_exp, (t + 1) * H)
                    link(v.reciprocal(rsum[:, :], esum[:, t * H:(t + 1) * H]))
                    ve.wait_ge(s_pv, (t + 1) * H)
                    if t > 0:
                        ve.wait_ge(s_ot, t)
                    v.tensor_tensor(onat.rearrange("p (h d) -> p h d", d=VH),
                                    o6[:, :].rearrange("p (h d) -> p h d", d=VH), bc(rsum[:, :], VH), ALU.mult)\
                        .then_inc(s_on, 1)

                maxes(0)
                for un in range(NU + 1):
                    if un + 1 < NU:
                        maxes(un + 1)
                    if un >= H and un % H == 0:
                        tile_out(un // H - 1)
                    if un < NU:
                        ve.wait_ge(s_pt, un + 1)
                        if UNITS[un][0] == 0:
                            ve.sem_inc(s_ptb, 1)
                        else:
                            if un >= 2:
                                ve.wait_ge(s_pv, un - 1)
                            v.tensor_copy(probT[un % 2][:, 3:NLK, :], tb5[:, 0:2 * P].rearrange("p (k n) -> p k n", n=P))\
                                .then_inc(s_ptb, 1)
                    if un in ADA_AT:
                        p, n, step = ADA_AT[un]
                        if step >= 2:
                            ada_half(2 * p + n, step - 2)
                ve.wait_ge(ada_bc_s, 20)
                ve.sem_inc(gain_used, 1)

                for j in range(2 * NT):
                    n, t = divmod(j, NT)
                    ve.wait_ge(op_mm, j + 1)
                    if j >= 4:
                        ve.wait_ge(op_x, j - 3)
                    src = pair[(j % 4) // 2][:, (j % 2) * HALF:(j % 2 + 1) * HALF]
                    v.tensor_tensor(out_s[j % 4], src, gate[:, ctx_of(t), n * HALF:(n + 1) * HALF], ALU.mult)\
                        .then_inc(op_g, 1)

                norm(0, NT)
                norm(1, NT + 1)
                for t in range(NT):
                    evac_h(t, NT)
                    if t + 2 < NT:
                        norm(t + 2, NT + t + 2)

                tt, ts, red = v.tensor_tensor, v.tensor_scalar, v.tensor_reduce
                ve.wait_ge(r_e, 1)
                link(ts(sig, sig, 1.0, None, ALU.add))
                link(v.reciprocal(sig, sig))
                rb_b = rb[:, :].unsqueeze(1).broadcast_to([P, NT, NE])
                by_tile = lambda a: a.rearrange("p (t g) k -> p t (g k)", t=NT)
                link(tt(by_tile(sel_s), by_tile(sig), rb_b, ALU.add))

                def ranks(out, val, gt, eq, n):
                    q = val.shape[1]
                    a = val.unsqueeze(3).broadcast_to([P, q, n, n])
                    b = val.unsqueeze(2).broadcast_to([P, q, n, n])
                    tt(gt, b, a, ALU.is_gt)
                    link(tt(eq, b, a, ALU.is_equal))
                    low_b = k_("lower").unsqueeze(1).broadcast_to([P, q, n * n])
                    link(tt(eq.rearrange("p q i j -> p q (i j)"), eq.rearrange("p q i j -> p q (i j)"), low_b, ALU.mult))
                    link(tt(gt, gt, eq, ALU.add))
                    link(red(out, gt, AX.X, ALU.add))

                ranks(rank, sel_s, cmp4, eq4, GE)
                link(ts(chosen, rank, 2.0, None, ALU.is_lt))
                link(tt(rank, sel_s, chosen, ALU.mult))
                link(red(gsc.rearrange("p t g -> p (t g)"), rank, AX.X, ALU.add))
                ranks(best, gsc, gcmp, geq, EG)
                link(ts(best, best, 1.0, None, ALU.is_lt))
                tt(mask.rearrange("p t (g k) -> p (t g) k", k=GE), chosen,
                   best.rearrange("p t g -> p (t g)").unsqueeze(2).broadcast_to([P, NT * EG, GE]), ALU.mult)\
                    .then_inc(r_mask, 1)
                ve.wait_ge(r_mask, 1)
                link(tt(gts, by_tile(sig), mask, ALU.mult))
                link(red(den, gts, AX.X, ALU.add))
                link(v.reciprocal(den, den))
                link(tt(gts, gts, bc(den, NE), ALU.mult))
                ve.wait_ge(r_tot, 1)
                tot = pair[0][:, HALF:HALF + NE]
                link(tt(nbc, bc(tot, 5), k_("kblock").unsqueeze(1).broadcast_to([P, NE, 5]), ALU.is_gt))
                link(red(nb, nbc, AX.X, ALU.add))
                link(v.tensor_tensor_scan(endb, k_("ones")[:, 0:NE], nb, 0.0, ALU.mult, ALU.add))
                tt(start, endb, nb, ALU.subtract)
                link(tt(ecmp, endb.unsqueeze(1).broadcast_to([P, NBLK, NE]), bc(k_("block"), NE), ALU.is_le))
                link(red(eidf, ecmp, AX.X, ALU.add))
                link(ts(eid[:, :], eidf, float(NE - 1), None, ALU.min))
                ve.sem_inc(eid_ready, 1)
                pos = pair[0][:, 0:NT * NE].rearrange("p (t e) -> p t e", e=NE)
                link(ts(start, start, float(P), 1.0, ALU.mult, ALU.add))
                link(tt(slot1, pos, start.unsqueeze(1).broadcast_to([P, NT, NE]), ALU.add))
                link(tt(slot1, slot1, mask, ALU.mult))
                red(pick[:, 0, :], slot1, AX.X, ALU.max)
                link(red(den, slot1, AX.X, ALU.add))
                link(tt(pick[:, 1, :], den, pick[:, 0, :], ALU.subtract))
                for w in range(2):
                    m = tt(hot[:, w], slot1, bc(pick[:, w, :], NE), ALU.is_equal)
                link(m)
                for w in range(2):
                    m = tt(prod[:, w], hot[:, w], gts, ALU.mult)
                link(m)
                for w in range(2):
                    m = red(gates2[:, w * NT:(w + 1) * NT], prod[:, w], AX.X, ALU.add)
                link(m)
                flat_pick = pick.rearrange("p w t -> p (w t)")
                link(ts(slot_i[:, :], flat_pick, -1.0, None, ALU.add))
                ts(slot_a[:, :], slot_i[:, :], P - 1, None, ALU.bitwise_and)
                link(ts(slot_b[:, :], slot_i[:, :], 7, None, ALU.logical_shift_right))
                v.tensor_copy(slot_p, slot_a[:, :])
                link(v.tensor_copy(slot_q, slot_b[:, :]))
                for j in range(2 * NT):
                    if j >= 2:
                        ve.wait_ge(r_pe1, j - 1)
                    ts(onep[j % 2], k_("row"), slot_p[:, j:j + 1], None, ALU.is_equal)
                    ts(oneb[j % 2], k_("block"), slot_q[:, j:j + 1], k_("token")[:, j % NT:j % NT + 1], ALU.is_equal,
                       ALU.mult).then_inc(r_one, 1)
                ve.wait_ge(r_pe1, 2 * NT)
                v.tensor_copy(idx[:, :], pair[1][:, 0:NBLK]).then_inc(r_idx, 1)
                ada_out(10)
                ada_out(11)

                for count in (b_td, b_act, b_yd):
                    ve.sem_inc(count, 1)
                with ve.Fori(0, NBLK // 2) as i:
                    for s in range(2):
                        b = i * 2 + s
                        ve.wait_ge(b_t, b + 1)
                        v.tensor_copy(xgT[s][:, 4:8, :], pair[0][:, HALF:2 * HALF].rearrange("p (k n) -> p k n", n=P))\
                            .then_inc(b_td, 1)
                        ve.wait_ge(b_sil, b + 1)
                        ve.wait_ge(b_at, b + 1)
                        v.tensor_tensor(act_n, sil, tb4[:, DE:2 * DE], ALU.mult).then_inc(b_act, 1)
                        ve.wait_ge(b_dn, b + 1)
                        ve.wait_ge(b_st, b * 16 + 16)
                        v.tensor_copy(yb[:, HALF:D], pair[1][:, HALF:2 * HALF]).then_inc(b_yd, 1)
                ve.wait_ge(ada_bc_s, 24)
                for t in range(NT):
                    k = (2 * t) % 4
                    ve.wait_ge(c_hi, t + 1)
                    ve.wait_ge(c_in[k + 1], l * (C_USES[k + 1] * 16) + (t // 2 + 1) * 16)
                    link(v.scalar_tensor_tensor(comb[k + 1], comb[k + 1], gates2[:, NT + t:NT + t + 1], comb[k],
                                                ALU.mult, ALU.add))
                    link(tt(comb[k + 1], comb[k + 1], gate[:, ctx_of(t), :], ALU.mult))
                    tt(x[:, t, :], x[:, t, :], comb[k + 1], ALU.add).then_inc(c_gt, 1)
                ve.wait_ge(c_gt, NT)
                ve.wait_ge(layer_end, 3)
                for s in cleared:
                    ve.sem_clear(s)
                ve.sem_inc(layer_go, 1)


def kernel(**inputs):
    import concourse.bacc as bacc
    from concourse.bass_utils import run_bass_kernel_spmd

    arrays = {n: np.ascontiguousarray(inputs[n]) for n in INS}
    table, at = constants()
    arrays["consts"] = table
    nc = bacc.Bacc("TRN2", target_bir_lowering=False, num_devices=1)
    ins = {n: nc.dram_tensor(n, a.shape, mybir.dt.from_np(a.dtype), kind="ExternalInput").ap()
           for n, a in arrays.items()}
    outs = {n: nc.dram_tensor(n, s, F32, kind="ExternalOutput").ap() for n, s in OUTS.items()}
    step_kernel(nc, **ins, **outs, const_at=at)
    r = run_bass_kernel_spmd(nc, [arrays], core_ids=[0])
    return tuple(r.results[0][n] for n in OUTS)


INS = ["x_prompt", "x_sample", "cache_ckv", "cache_krope", "c", "c_ctx", "ada_w", "ada_b", "norm1_g", "norm2_g", "w_in",
       "pool_w", "pool_scale", "q_a_norm_g", "w_uq", "kv_a_norm_g", "w_ukv", "q_norm_g", "k_norm_g", "w_out",
       "router_w", "router_b", "w_gate", "w_up", "w_down"]
OUTS = {"y_prompt": (1, SEQ, D), "y_sample": (1, DEC, D), "new_ckv": (1, DEPTH, SEQ, KVR),
        "new_krope": (1, DEPTH, SEQ, ROPE)}
```

```python
from contextlib import ExitStack

import numpy as np

import concourse.bass as bass
from concourse import mybir

F32 = mybir.dt.float32
I32 = mybir.dt.int32
U32 = mybir.dt.uint32
ALU = mybir.AluOpType
ACT = mybir.ActivationFunctionType
AX = mybir.AxisListType

P = 128
DEPTH = 2
D = 1024
DC = D // P
SEQ, DEC = 128, 512
NT = (SEQ + DEC) // P
NTOK = NT * P
GRID_W = 64
WINDOWS = (2, 4, 8, 16)
NG = len(WINDOWS)
POOLW = NG * P
H = 8
NOPE, ROPE, VH = 64, 32, 64
QH = NOPE + ROPE
QR, KVR = 384, 256
QC, KC = QR // P, KVR // P
INW = POOLW + QR + KVR + ROPE
NE, EG, GE = 16, 4, 4
DE = 256
EPS = 1e-6
SCALE = 1.0 / float(np.sqrt(QH))
NKT = NT + 1
NLK = NKT - 1
CTX = NKT - 1
NPIECE = 6
HALF = 512
NBLK = 26
NBLK_MIN = 2 * NTOK // P
FILLS = -(-(NBLK - NBLK_MIN) // NT)
NSLOT = NBLK * P
UNITS = [(t, h) for t in range(NT) for h in range(H)]
NU = len(UNITS)
GAP = 16
PW = GAP + SEQ + GAP + DEC + GAP
CTX0, LAT0 = GAP, GAP + SEQ + GAP

COL_STEPS = [(a, step) for a in range(4) for step in range(3)]
ROW_STEPS = [(a, step) for a in range(4, 10) for step in range(4)] + [(a, step) for a in (10, 11) for step in range(2)]
ADA_AT = {2 + n: st for n, st in enumerate(ROW_STEPS)}
BC_BEFORE = [0, 1, 2, 3] + [4 + 2 * n for n in range(8)] + [20]


def constants():
    cols, at = [], {}

    def put(name, a):
        full = np.zeros((P, a.shape[1]), np.float32)
        full[:a.shape[0]] = a
        at[name] = (sum(c.shape[1] for c in cols), a.shape[1])
        cols.append(full)

    put("ident", np.eye(P, dtype=np.float32))
    for c in range(2):
        put(f"sel{c}", np.repeat((np.arange(P) % 32 == c).astype(np.float32)[:, None], P, 1))
    put("selcol", np.stack([(np.arange(P) % 32 == c).astype(np.float32) for c in range(2)], 1))
    bsel = np.zeros((12, 12, 32), np.float32)
    for j in range(12):
        bsel[j, j, 0:2] = 1
    put("bias_sel", bsel.reshape(12, -1))
    rows = DEC // GRID_W
    inv = (np.float32(10000.0) ** (-np.arange(ROPE // 4, dtype=np.float32) / np.float32(ROPE // 4))).astype(np.float32)
    row = np.repeat(np.arange(rows), GRID_W).astype(np.float32)
    col = np.tile(np.arange(GRID_W), rows).astype(np.float32)
    ang = np.concatenate([row[:, None] * inv, col[:, None] * inv], -1).astype(np.float32)
    for name, f in (("cos", np.cos), ("sin", np.sin)):
        v = f(ang).astype(np.float32).reshape(NT - 1, P, ROPE // 2).transpose(1, 0, 2)
        put(name, v.reshape(P, -1))
    edge = np.ones((NG, 16), np.float32)
    for g, w in enumerate(WINDOWS):
        for t in range(8):
            edge[g, t] = w / min(w, t + w // 2)
            left = 8 - t
            edge[g, 8 + t] = w / min(w, w // 2 + min(left, w // 2))
    put("edge", np.tile(edge.reshape(1, -1), (P, 1)))
    i = np.arange(P)
    put("before", (i[:, None] < i[None, :]).astype(np.float32))
    put("ones", np.ones((P, P), np.float32))
    put("lower", np.tile((i[:4, None] > i[None, :4]).astype(np.float32).reshape(1, -1), (P, 1)))
    put("row", np.tile(i[None, :].astype(np.float32), (P, 1)))
    put("block", np.tile(np.arange(NBLK, dtype=np.float32)[None], (P, 1)))
    put("kblock", np.tile((np.arange(5) * P).astype(np.float32)[None], (P, 1)))
    put("token", (np.arange(NT)[None] * P + i[:, None]).astype(np.float32))
    put("mhalf", np.full((P, 8), -0.5, np.float32))
    return np.concatenate(cols, 1), at


def step_kernel(nc, x_prompt, x_sample, cache_ckv, cache_krope, c, c_ctx, ada_w, ada_b, norm1_g, norm2_g, w_in, pool_w,
                pool_scale, q_a_norm_g, w_uq, kv_a_norm_g, w_ukv, q_norm_g, k_norm_g, w_out, router_w, router_b,
                w_gate, w_up, w_down, consts, y_prompt, y_sample, new_ckv, new_krope, const_at):
    es = ExitStack()
    with es:
        def sb(name, shape, dt=F32):
            return es.enter_context(nc.sbuf_tensor(name, shape, dt))

        def sem(name):
            return es.enter_context(nc.semaphore(name))

        x = sb("x", [P, NT, D])
        actT = sb("actT", [P, DC, NTOK])
        BIGW = 3 * 6144
        big = sb("big", [P, BIGW])
        low = sb("low", [P, 8960])
        ada_ring = [sb(f"ada_ring{i}", [P, 4, HALF]) for i in range(2)]
        mod = sb("mod", [P, 6144])
        cst = sb("cst", [P, sum(n for _, n in const_at.values())])
        bias_rows = sb("bias_rows", [12, HALF])
        part_s = sb("part_s", [P, HALF])
        gain = sb("gain", [P, D])
        condT = sb("condT", [P, DC, 32])
        gcol = sb("gcol", [P, DC, 2])
        scol = sb("scol", [P, DC, 2])
        gn1 = sb("gn1", [P, DC])
        ctl = sb("ctl", [P, 2], I32)
        pairs = sb("pairs", [P, 1])
        rw = sb("rw", [P, DC, NE])
        rb = sb("rb", [P, NE])
        gq = sb("gq", [P, QH])
        gk = sb("gk", [P, QH])
        pscale = sb("pscale", [P, NG])
        kr = sb("kr", [P, NKT, ROPE])
        krr = sb("krr", [P, NKT, ROPE])
        rope_t = sb("rope_t", [P, 2, ROPE])
        ss = sb("ss", [P, 2 * NT])
        rs = sb("rs", [P, 2 * NT])
        head_ss = sb("head_ss", [P, 2, 2, H])
        head_rs = sb("head_rs", [P, 2, 2, H])
        kr_ss = sb("kr_ss", [P, NKT])
        low_ss = sb("low_ss", [P, NT, 2])
        low_rs = sb("low_rs", [P, NT, 2])
        nmax = sb("nmax", [P, 2])
        mx = sb("mx", [P, 2])
        esum = sb("esum", [P, NU])
        rsum = sb("rsum", [P, H])
        slot_i = sb("slot_i", [P, 2 * NT], U32)
        slot_a = sb("slot_a", [P, 2 * NT], U32)
        slot_b = sb("slot_b", [P, 2 * NT], U32)
        gates2 = sb("gates2", [P, 2 * NT])
        idx = sb("idx", [P, NBLK], U32)
        eid = sb("eid", [P, NBLK], I32)

        def k_(name):
            a, n = const_at[name]
            return cst[:, a:a + n]

        ident = k_("ident")

        def view(t, lo, shape):
            n = int(np.prod(shape))
            v = t[:, lo:lo + n]
            if len(shape) == 2:
                return v.rearrange("p (a b) -> p a b", b=shape[1])
            if len(shape) == 3:
                return v.rearrange("p (a b c) -> p a b c", b=shape[1], c=shape[2])
            return v

        win = view(big, 0, (DC, INW))
        cache_n = view(big, DC * INW, (KVR,))
        ckv_keep = view(big, DC * INW + KVR, (KVR,))
        gqa = view(big, DC * INW + 2 * KVR, (QR,))
        gkva = view(big, DC * INW + 2 * KVR + QR, (KVR,))
        crow = part_s[0:16, 0:P]
        qT = view(big, 0, (H, NTOK))
        kT = view(big, 5120, (H, NKT * P))
        V = view(big, 11264, (NKT, H * VH))
        cqT = view(big, 14336, (QC, NTOK))
        ckvT = view(big, 16256, (KC, NKT * P))
        prob = [view(big, 14336 + 640 * i, (NLK, P)) for i in range(2)]
        probT = [view(big, 15616 + 640 * i, (NLK, P)) for i in range(2)]
        onat = view(big, 16896, (HALF,))
        wgu = [view(big, 6144 * i, (DC, 2 * DE)) for i in range(2)]
        wd = [view(big, 6144 * i + 4096, (2, D)) for i in range(2)]
        xn = [view(big, 12288 + D * i, (D,)) for i in range(2)]
        xg = xn
        xgT = [view(big, 14336 + D * i, (DC, P)) for i in range(2)]
        act_n = [view(big, 16384 + DE * i, (DE,)) for i in range(2)]
        sil = [view(big, 16384 + DE * (2 + i), (DE,)) for i in range(2)]
        acT = [view(part_s, 2 * P * i, (2, P)) for i in range(2)]
        yb = view(big, 17408, (D,))
        comb = [view(big, 14336 + D * i, (D,)) for i in range(4)]
        rt = 14336
        sel_s = view(big, rt, (NT * EG, GE))
        sig = view(big, rt + 80, (NT * EG, GE))
        cmp4 = view(big, rt + 160, (NT * EG, GE, GE))
        eq4 = view(big, rt + 480, (NT * EG, GE, GE))
        chosen = view(big, rt + 800, (NT * EG, GE))
        rank = view(big, rt + 880, (NT * EG, GE))
        gsc = view(big, rt + 960, (NT, EG))
        gcmp = view(big, rt + 980, (NT, EG, EG))
        geq = view(big, rt + 1060, (NT, EG, EG))
        best = view(big, rt + 1140, (NT, EG))
        mask = view(big, rt + 1160, (NT, NE))
        gts = view(big, rt + 1240, (NT, NE))
        den = view(big, rt + 1320, (NT,))
        hot = view(big, rt + 1330, (2, NT, NE))
        slot1 = view(big, rt + 1490, (NT, NE))
        pick = view(big, rt + 1570, (2, NT))
        nbc = view(big, rt + 1590, (NE, 5))
        nb = view(big, rt + 1670, (NE,))
        endb = view(big, rt + 1690, (NE,))
        start = view(big, rt + 1710, (NE,))
        ecmp = view(big, rt + 1730, (NBLK, NE))
        eidf = view(big, rt + 2146, (NBLK,))
        slot_p = view(big, rt + 2180, (2 * NT,))
        slot_q = view(big, rt + 2190, (2 * NT,))
        onep = [view(big, rt + 2200 + P * i, (P,)) for i in range(2)]
        oneb = [view(big, rt + 2456 + 32 * i, (NBLK,)) for i in range(2)]
        prod = view(big, rt + 2520, (2, NT, NE))
        pcmp = view(big, rt + 2680, (NBLK // 2,))
        wuq = view(low, 0, (QC, H * QH))
        wukv = view(low, 2304, (KC, H * (NOPE + VH)))
        pw = view(low, 4352, (NG, P))
        wo = [view(low, 4864, (DC, HALF)), view(low, 0, (DC, HALF))]
        G = view(mod, 0, (2, D))
        S = view(mod, 2 * D, (2, D))
        gate = view(mod, 4 * D, (2, D))
        u = view(mod, 0, (NG, PW))
        pa = view(mod, NG * PW, (PW,))
        pb = view(mod, (NG + 1) * PW, (PW,))
        qn = view(mod, 4480, (H, QH))
        kn = view(mod, 4480 + H * QH, (H, QH))
        cn = view(mod, 4480, (QR + KVR,))
        sq_x = yb
        sq_cq, sq_ckv = view(big, 17792, (QR,)), view(big, 17792 + QR, (KVR,))
        flat = actT[:, :, :].rearrange("p a b -> p (a b)")
        sq_q = view(flat, 4 * NTOK, (H, QH))
        sq_k = view(flat, 6 * NTOK, (H, NOPE))
        sq_kr = view(flat, 7 * NTOK, (ROPE,))
        rq = [view(gain, i * H * 16, (H, 16)) for i in range(4)]
        out_s = [view(big, 14336 + HALF * i, (HALF,)) for i in range(4)]

        bank = [es.enter_context(nc.psum_tensor(f"bank{i}", [P, HALF], F32)) for i in range(4, 8)]
        pair = [es.enter_context(nc.psum_tensor(f"pair{i}", [P, 2 * HALF], F32)) for i in range(2)]
        tb4, tb5, o6, a7 = bank

        h2_rows = nc.dram_tensor("h2_rows", [NTOK, D], F32, kind="Internal").ap()
        y_rows = nc.dram_tensor("y_rows", [NSLOT, D], F32, kind="Internal").ap()

        ld_start = sem("ld_start")
        ld_ada = [sem("ld_ada0"), sem("ld_ada1")]
        ld_bias = sem("ld_bias")
        ld_gain = sem("ld_gain")
        ld_win = sem("ld_win")
        ld_low = sem("ld_low")
        ld_small = sem("ld_small")
        ld_wo = [sem("ld_wo0"), sem("ld_wo1")]
        ld_gu = [sem("ld_gu0"), sem("ld_gu1")]
        ld_dn = [sem("ld_dn0"), sem("ld_dn1")]
        ld_gn1 = sem("ld_gn1")
        ada_used = sem("ada_used")
        gu_used, dn_used = sem("gu_used"), sem("dn_used")
        moe_done = sem("moe_done")
        win_used = sem("win_used")
        proj_used = sem("proj_used")
        wo_used = sem("wo_used")
        eid_ready = sem("eid_ready")
        layer_go = sem("layer_go")
        y_fill = sem("y_fill")
        stream_go = sem("stream_go")
        out_done = sem("out_done")
        g_in = [sem("g_in0"), sem("g_in1")]
        c_in = [sem(f"c_in{i}") for i in range(4)]
        first_ada = [sem(f"first_{n}") for n in ("part", "part_s", "bc", "bc_s")]
        cond_t = sem("cond_t")
        cond_s = sem("cond_s")
        start_d = sem("start_d")

        cleared = []

        def lsem(name):
            cleared.append(sem(name))
            return cleared[-1]

        layer_end = lsem("layer_end")
        dv = lsem("dve_chain")
        pl = lsem("pool_chain")
        ac = lsem("act_chain")
        ada_part, ada_part_s, ada_bc, ada_bc_s = (lsem(n) for n in ("ada_part", "ada_part_s", "ada_bc", "ada_bc_s"))
        layer_ada = (ada_part, ada_part_s, ada_bc, ada_bc_s)
        x_sq, x_rs = lsem("x_sq"), lsem("x_rs")
        h_ready, h_t, h_ta, h_td = (lsem(n) for n in ("h_ready", "h_t", "h_ta", "h_td"))
        h_st = [lsem("h_st0"), lsem("h_st1")]
        in_mm, in_act, in_dve = lsem("in_mm"), lsem("in_act"), lsem("in_dve")
        low_sq, low_r, low_t, low_ta, low_td = (lsem(n) for n in ("low_sq", "low_r", "low_t", "low_ta", "low_td"))
        ckv_out = lsem("ckv_out")
        q_mm, kv_mm, q_sq, k_sq, q_ss, k_ss, q_rs, k_rs = (lsem(n) for n in ("q_mm", "kv_mm", "q_sq", "k_sq", "q_ss",
                                                                            "k_ss", "q_rs", "k_rs"))
        v_cp, q_n, k_n, q_rd, k_rd = (lsem(n) for n in ("v_cp", "q_n", "k_n", "q_rd", "k_rd"))
        qk_t, qk_ta, qk_td = lsem("qk_t"), lsem("qk_ta"), lsem("qk_td")
        krr_s = lsem("krr_s")
        keep_s, keep_out = lsem("keep_s"), lsem("keep_out")
        pool_z, pool_d, pool_mm, pool_ea, pool_ed = (lsem(n) for n in ("pool_z", "pool_d", "pool_mm", "pool_ea",
                                                                        "pool_ed"))
        s_sc, s_mx, s_exp, s_pt, s_pta, s_ptb, s_pv, s_on, s_ot, s_otc = (lsem(n) for n in (
            "s_sc", "s_mx", "s_exp", "s_pt", "s_pta", "s_ptb", "s_pv", "s_on", "s_ot", "s_otc"))
        op_mm, op_g, op_x = lsem("op_mm"), lsem("op_g"), lsem("op_x")
        r_mm, r_e, r_mask, r_tot, r_one, r_pe1, r_idx, r_ctl, y_done = (lsem(n) for n in (
            "r_mm", "r_e", "r_mask", "r_tot", "r_one", "r_pe1", "r_idx", "r_ctl", "y_done"))
        b_t, b_ta, b_td, b_gu, b_sil, b_act, b_at, b_atc, b_dn, b_ya, b_yd, b_st = (lsem(n) for n in (
            "b_t", "b_ta", "b_td", "b_gu", "b_sil", "b_act", "b_at", "b_atc", "b_dn", "b_ya", "b_yd", "b_st"))
        c_hi, c_gt = lsem("c_hi"), lsem("c_gt")

        C_USES = [sum((2 * t + w) % 4 == k for t in range(NT) for w in range(2)) for k in range(4)]
        ctx_of = lambda t: 0 if t == 0 else 1
        key_tile = lambda t: CTX if t == 0 else t
        KV_ORDER = [key_tile(t) for t in range(NT)] + [0]

        block = es.enter_context(nc.Block())

        @block.sync
        def _(sp):
            sp.dma_start(cst[:, :], consts).then_inc(ld_start, 16)
            sp.dma_start(crow[0:8], c_ctx.rearrange("(k p) -> k p", p=P)).then_inc(ld_start, 16)
            sp.dma_start(crow[8:16], c.rearrange("b (k p) -> (b k) p", p=P)).then_inc(ld_start, 16)
            sp.dma_start(x[:, 0, :], x_prompt[0]).then_inc(ld_start, 16)
            sp.dma_start(x[:, 1:NT, :], x_sample[0].rearrange("(t p) d -> p t d", p=P)).then_inc(ld_start, 16)
            sp.dma_start(rw[:, :, :], router_w.rearrange("(k p) e -> p k e", p=P)).then_inc(ld_start, 16)
            sp.dma_start(rb[:, :], router_b.rearrange("(a e) -> a e", a=1).broadcast_to([P, NE])).then_inc(ld_start, 16)
            sp.dma_start(bias_rows[0:4, :], ada_b[0, 0:2 * D].rearrange("(j n) -> j n", n=HALF)).then_inc(ld_bias, 16)
            sp.dma_start(gn1[:, :], norm1_g[0].rearrange("(k p) -> p k", p=P), allow_slow_non_contiguous=True)\
              .then_inc(ld_gn1, 16)

            def load_quarter(layer, a, kh, q):
                src = ada_w[layer, kh * HALF:(kh + 1) * HALF, a * HALF:(a + 1) * HALF]
                sp.dma_start(ada_ring[q % 2][:, :, :], src.rearrange("(k p) n -> p k n", p=P)).then_inc(ld_ada[q % 2], 16)

            for q in range(8):
                if q >= 2:
                    sp.wait_ge(ada_used, q - 1)
                load_quarter(0, q // 2, q % 2, q)
            with sp.Fori(0, DEPTH) as l:
                nxt = (l + 1) % DEPTH

                def load_ada(p):
                    for q in range(4 * p, 4 * p + 4):
                        sp.wait_ge(ada_used, l * (4 * NPIECE) + (8 + q - 1))
                        load_quarter(nxt if p < 2 else l, q // 2, q % 2, q)

                sp.wait_ge(wo_used, l + 1)
                for dst, src in ((gq, q_norm_g), (gk, k_norm_g)):
                    sp.dma_start(dst[:, :], src[l].rearrange("(a n) -> a n", a=1).broadcast_to([P, dst.shape[1]]))\
                      .then_inc(ld_small, 16)
                sp.dma_start(pscale[:, :], pool_scale[l].rearrange("(g p) -> p g", p=P),
                             allow_slow_non_contiguous=True).then_inc(ld_small, 16)
                sp.dma_start(kr[:, 0, :], cache_krope[0, l]).then_inc(ld_small, 16)
                sp.wait_ge(moe_done, l + 1)
                sp.dma_start(cache_n, cache_ckv[0, l]).then_inc(ld_small, 16)
                for dst, src in ((gqa, q_a_norm_g), (gkva, kv_a_norm_g)):
                    sp.dma_start(dst, src[l].rearrange("(a n) -> a n", a=1).broadcast_to([P, dst.shape[1]]))\
                      .then_inc(ld_small, 16)
                sp.dma_start(win[:, :, :], w_in[l].rearrange("(k p) n -> p k n", p=P)).then_inc(ld_win, 16)
                sp.dma_start(wuq[:, :, :], w_uq[l].rearrange("(k p) n -> p k n", p=P)).then_inc(ld_low, 16)
                sp.dma_start(wukv[:, :, :], w_ukv[l].rearrange("(k p) n -> p k n", p=P)).then_inc(ld_low, 16)
                sp.dma_start(pw[:, :, :], pool_w[l].rearrange("g p n -> p g n")).then_inc(ld_low, 16)
                sp.wait_ge(first_ada[3], 4)
                sp.dma_start(bias_rows[0:4, :], ada_b[nxt, 0:2 * D].rearrange("(j n) -> j n", n=HALF))\
                  .then_inc(ld_bias, 16)
                sp.dma_start(bias_rows[4:12, :], ada_b[l, 2 * D:6 * D].rearrange("(j n) -> j n", n=HALF))\
                  .then_inc(ld_bias, 16)
                sp.dma_start(gn1[:, :], norm1_g[nxt].rearrange("(k p) -> p k", p=P), allow_slow_non_contiguous=True)\
                  .then_inc(ld_gn1, 16)
                load_ada(0)
                load_ada(1)
                sp.dma_start(wo[0][:, :, :], w_out[l, :, 0:HALF].rearrange("(k p) n -> p k n", p=P))\
                  .then_inc(ld_wo[0], 16)
                load_ada(2)
                sp.wait_ge(proj_used, l + 1)
                sp.dma_start(gain[:, :], norm2_g[l].rearrange("(a n) -> a n", a=1).broadcast_to([P, D]))\
                  .then_inc(ld_gain, 16)
                load_ada(3)
                sp.dma_start(wo[1][:, :, :], w_out[l, :, HALF:D].rearrange("(k p) n -> p k n", p=P))\
                  .then_inc(ld_wo[1], 16)
                load_ada(4)
                load_ada(5)
                sp.wait_ge(eid_ready, l + 1)
                sp.sem_inc(stream_go, 1)
                n_pairs = sp.value_load(ctl[0:1, 0:1], min_val=NBLK_MIN // 2, max_val=NBLK // 2)
                before = sp.value_load(ctl[0:1, 1:2], min_val=0, max_val=DEPTH * NBLK // 2)
                with sp.Fori(0, n_pairs) as i:
                    es_ = []
                    for s in range(2):
                        sp.wait_ge(gu_used, (before + i) * 2 + (s + 1))
                        e = sp.value_load(eid[0:1, bass.ds(i * 2 + s, 1)], min_val=0, max_val=NE - 1)
                        es_.append(e)
                        sp.dma_start(wgu[s][:, :, 0:DE], w_gate[l, e].rearrange("(k p) n -> p k n", p=P))\
                          .then_inc(ld_gu[s], 16)
                        sp.dma_start(wgu[s][:, :, DE:2 * DE], w_up[l, e].rearrange("(k p) n -> p k n", p=P))\
                          .then_inc(ld_gu[s], 16)
                    for s in range(2):
                        sp.wait_ge(dn_used, (before + i) * 2 + (s + 1))
                        sp.dma_start(wd[s][:, :, :], w_down[l, es_[s]].rearrange("(k p) n -> p k n", p=P))\
                          .then_inc(ld_dn[s], 16)
            sp.wait_ge(layer_go, DEPTH)
            sp.dma_start(y_prompt[0], x[:, 0, :]).then_inc(out_done, 16)
            sp.dma_start(y_sample[0].rearrange("(t p) d -> p t d", p=P), x[:, 1:NT, :]).then_inc(out_done, 16)
            sp.wait_ge(out_done, (DEPTH + 2) * 16)

        @block.tensor
        def _(pe):
            mm, tr = nc.tensor.matmul, nc.tensor.transpose
            pe.sem_inc(gu_used, 2)
            pe.sem_inc(dn_used, 2)
            pe.sem_inc(moe_done, 1)
            pe.sem_inc(wo_used, 1)
            pe.wait_ge(ld_start, 16 * 7)
            tr(a7[:, 0:16], crow, ident[0:16, 0:16]).then_inc(cond_t, 1)
            pe.wait_ge(cond_s, 1)
            pe.wait_ge(ld_bias, 16)

            def ada_sums(a, step, counts):
                for k in range(4):
                    m = mm(a7[32 * k:32 * k + 32, :], condT[:, 4 * step + k, :], ada_ring[step][:, k, :],
                           start=(step == 0), stop=(step == 1 and k > 0), tile_position=(0, 32 * k),
                           skip_group_check=True)
                m.then_inc(ada_used, 1)
                if step == 1:
                    mm(a7[0:32, :], k_("bias_sel")[0:12, 32 * a:32 * a + 32] if counts is layer_ada else
                       k_("bias_sel")[0:4, 32 * a:32 * a + 32],
                       bias_rows[:, :] if counts is layer_ada else bias_rows[0:4, :], start=False, stop=True,
                       skip_group_check=True).then_inc(counts[0], 1)

            def ada_columns(a, counts):
                pe.wait_ge(counts[1], a + 1)
                for k in range(4):
                    m = mm(a7[:, 2 * k:2 * k + 2], part_s[:, k * P:(k + 1) * P], k_("selcol"), start=True, stop=True)
                m.then_inc(counts[2], 1)

            for a in range(4):
                for step in range(2):
                    pe.wait_ge(ld_ada[step], 16 * (a + 1))
                    if step == 0 and a > 0:
                        pe.wait_ge(first_ada[3], a)
                    ada_sums(a, step, first_ada)
                ada_columns(a, first_ada)
            pe.wait_ge(first_ada[3], 4)
            with pe.Fori(0, DEPTH) as l:
                def ada_step(a, step):
                    if step < 2:
                        pe.wait_ge(ld_ada[step], (l * (2 * NPIECE) + (4 + a + 1)) * 16)
                        if step == 0:
                            if a == 0:
                                pe.wait_ge(low_td, NT + 1)
                                pe.wait_ge(ld_bias, (l + 1) * 32 + 16)
                            else:
                                pe.wait_ge(ada_bc_s, BC_BEFORE[min(a, 10)])
                                pe.wait_ge(ada_part_s, a)
                        ada_sums(a, step, layer_ada)
                    elif a < 4:
                        ada_columns(a, layer_ada)
                    else:
                        ada_rows_out(a, step - 2, part_s[:, :])

                def ada_rows_out(a, cnd, rows):
                    pe.wait_ge(ada_part_s, a + 1)
                    pe.wait_ge(ada_bc_s, BC_BEFORE[a] + cnd)
                    mm(a7[:, :], k_(f"sel{cnd}"), rows, start=True, stop=True).then_inc(ada_bc, 1)

                def turn_h(t, first):
                    j = first + t
                    pe.wait_ge(h_ready, j + 1)
                    if j > 0:
                        pe.wait_ge(h_ta, j)
                        pe.wait_ge(h_td, j)
                    for k in range(DC):
                        dst = (tb4, tb5)[k // 4]
                        m = tr(dst[:, (k % 4) * P:(k % 4 + 1) * P], xn[t % 2][:, k * P:(k + 1) * P], ident)
                    m.then_inc(h_t, 1)

                def in_proj(t):
                    pe.wait_ge(h_ta, t + 1)
                    pe.wait_ge(h_td, t + 1)
                    if t == 0:
                        pe.wait_ge(ld_win, (l + 1) * 16)
                    if t >= 2:
                        pe.wait_ge(in_act, t - 1)
                        pe.wait_ge(in_dve, t - 1)
                    for lo, n, at in ((POOLW, QR, 0), (POOLW + QR, KVR + ROPE, HALF)):
                        for k in range(DC):
                            m = mm(pair[t % 2][:, at:at + n], actT[:, k, t * P:(t + 1) * P], win[:, k, lo:lo + n],
                                   start=(k == 0), stop=(k == DC - 1))
                    m.then_inc(in_mm, 1)

                def turn_low(j):
                    if j < NT:
                        pe.wait_ge(in_dve, j + 1)
                    else:
                        pe.wait_ge(ld_small, (l + 1) * (7 * 16))
                    if j > 0:
                        pe.wait_ge(low_ta, min(j, NT))
                        pe.wait_ge(low_td, j)
                    if j < NT:
                        for k in range(QC):
                            m = tr(o6[:, k * P:(k + 1) * P], cn[:, k * P:(k + 1) * P], ident)
                    for k in range(KC):
                        src = cn[:, QR + k * P:QR + (k + 1) * P] if j < NT else cache_n[:, k * P:(k + 1) * P]
                        m = tr(a7[:, k * P:(k + 1) * P], src, ident)
                    m.then_inc(low_t, 1)

                turn_h(0, 0)
                for t in range(NT):
                    if t + 1 < NT:
                        turn_h(t + 1, 0)
                    in_proj(t)
                    if t > 0:
                        turn_low(t - 1)
                for g in range(NG):
                    j = NT + g
                    pe.wait_ge(in_act, j - 1)
                    pe.wait_ge(in_dve, j - 1)
                    for at, t0, n in ((0, P, DEC), (HALF, 0, P)):
                        for k in range(DC):
                            m = mm(pair[j % 2][:, at:at + n], win[:, k, g * P:(g + 1) * P], actT[:, k, t0:t0 + n],
                                   start=(k == 0), stop=(k == DC - 1))
                    m.then_inc(in_mm, 1)
                    if g == 0:
                        turn_low(NT - 1)
                    if g == 1:
                        turn_low(NT)
                pe.wait_ge(in_act, NT + NG)
                pe.wait_ge(in_dve, NT + NG)

                pe.wait_ge(ld_low, (l + 1) * 48)

                def q_proj(t):
                    pe.wait_ge(low_ta, t + 1)
                    if t > 0:
                        pe.wait_ge(q_sq, t)
                        pe.wait_ge(q_rd, t)
                    for n in range(2):
                        for k in range(QC):
                            m = mm(pair[0][:, n * HALF:n * HALF + 4 * QH], cqT[:, k, t * P:(t + 1) * P],
                                   wuq[:, k, n * 4 * QH:(n + 1) * 4 * QH], start=(k == 0), stop=(k == QC - 1))
                    m.then_inc(q_mm, 1)

                def kv_proj(j):
                    kt = KV_ORDER[j]
                    pe.wait_ge(low_td, j + 1)
                    if j > 0:
                        pe.wait_ge(k_sq, j)
                        pe.wait_ge(v_cp, j)
                        pe.wait_ge(k_rd, j)
                    for n in range(2):
                        for k in range(KC):
                            m = mm(pair[1][:, n * HALF:(n + 1) * HALF], ckvT[:, k, kt * P:(kt + 1) * P],
                                   wukv[:, k, n * HALF:(n + 1) * HALF], start=(k == 0), stop=(k == KC - 1))
                    m.then_inc(kv_mm, 1)

                def turn_heads(src, job):
                    if job > 0:
                        pe.wait_ge(qk_ta, job)
                        pe.wait_ge(qk_td, job)
                    else:
                        pe.wait_ge(h_ta, NT)
                        pe.wait_ge(h_td, NT)
                    for h in range(H):
                        dst = (tb4, tb5)[h // 4]
                        m = tr(dst[0:QH, (h % 4) * P:(h % 4 + 1) * P], src[:, h, :], ident)
                    m.then_inc(qk_t, 1)

                q_proj(0)
                kv_proj(0)
                for j in range(NT + 1):
                    if j < NT:
                        pe.wait_ge(q_n, j + 1)
                        turn_heads(qn, 2 * j)
                        if j + 1 < NT:
                            q_proj(j + 1)
                    pe.wait_ge(k_n, j + 1)
                    turn_heads(kn, 2 * j + 1 if j < NT else 2 * NT)
                    if j + 1 <= NT:
                        kv_proj(j + 1)
                    for st in COL_STEPS[2 * j:2 * j + 2]:
                        ada_step(*st)
                for g in range(NG):
                    pe.wait_ge(pool_d, g + 1)
                    if g == 0:
                        pe.wait_ge(k_rd, NT + 1)
                        pe.wait_ge(v_cp, NT + 1)
                        pe.wait_ge(k_sq, NT + 1)
                    if g >= 2:
                        pe.wait_ge(pool_ea, g - 1)
                        pe.wait_ge(pool_ed, g - 1)
                    mm(pair[g % 2][:, 0:DEC], pw[:, g, :], u[:, g, LAT0:LAT0 + DEC], start=True, stop=True)
                    mm(pair[g % 2][:, HALF:HALF + SEQ], pw[:, g, :], u[:, g, CTX0:CTX0 + SEQ], start=True, stop=True)\
                        .then_inc(pool_mm, 1)
                pe.wait_ge(pool_mm, NG)
                pe.sem_inc(proj_used, 1)

                def scores(un):
                    t, h = UNITS[un]
                    if un < 2:
                        if un == 0:
                            pe.wait_ge(qk_ta, 2 * NT + 1)
                            pe.wait_ge(qk_td, 2 * NT + 1)
                        pe.wait_ge(pool_ea, NG - 1 + un)
                        pe.wait_ge(pool_ed, NG - 1 + un)
                    else:
                        pe.wait_ge(s_exp, un - 1)
                    q = qT[0:QH, h, t * P:(t + 1) * P]
                    dst = pair[un % 2]
                    if t == 0:
                        m = mm(dst[:, 0:P], q, kT[0:QH, h, CTX * P:NKT * P], start=True, stop=True)
                    else:
                        mm(dst[:, 0:HALF], q, kT[0:QH, h, 0:HALF], start=True, stop=True)
                        m = mm(dst[:, HALF:NLK * P], q, kT[0:QH, h, HALF:NLK * P], start=True, stop=True)
                    m.then_inc(s_sc, 1)

                def turn_prob(un):
                    t, h = UNITS[un]
                    pe.wait_ge(s_exp, un + 1)
                    if un > 0:
                        pe.wait_ge(s_pta, un)
                        pe.wait_ge(s_ptb, un)
                    for k in range(1 if t == 0 else NLK):
                        dst = tb4[:, k * P:(k + 1) * P] if k < 3 else tb5[:, (k - 3) * P:(k - 2) * P]
                        m = tr(dst, prob[un % 2][:, k, :], ident)
                    m.then_inc(s_pt, 1)

                def weigh(un):
                    t, h = UNITS[un]
                    pe.wait_ge(s_pta, un + 1)
                    pe.wait_ge(s_ptb, un + 1)
                    if h == 0 and t > 0:
                        pe.wait_ge(s_on, t)
                    tiles = [CTX] if t == 0 else list(range(NLK))
                    for k, kt in enumerate(tiles):
                        m = mm(o6[:, h * VH:(h + 1) * VH], probT[un % 2][:, k, :], V[:, kt, h * VH:(h + 1) * VH],
                               start=(k == 0), stop=(k == len(tiles) - 1))
                    m.then_inc(s_pv, 1)

                def turn_out(t):
                    pe.wait_ge(s_on, t + 1)
                    pe.wait_ge(s_pta, min(NU, (t + 1) * H + 1))
                    for k in range(4):
                        m = tr(tb4[:, k * P:(k + 1) * P], onat[:, k * P:(k + 1) * P], ident)
                    m.then_inc(s_ot, 1)
                    pe.wait_ge(s_otc, t + 1)

                scores(0)
                for un in range(NU + 2):
                    if un + 1 < NU:
                        scores(un + 1)
                    if 1 <= un <= NU:
                        weigh(un - 1)
                    if un >= H + 1 and (un - 1) % H == 0:
                        turn_out((un - 1) // H - 1)
                    if un < NU:
                        turn_prob(un)
                    if un in ADA_AT:
                        ada_step(*ADA_AT[un])
                pe.wait_ge(s_otc, NT)

                for n in range(2):
                    pe.wait_ge(ld_wo[n], (l + 1) * 16)
                    for t in range(NT):
                        j = n * NT + t
                        if j >= 4:
                            pe.wait_ge(op_g, j - 3)
                        dst = pair[(j % 4) // 2][:, (j % 2) * HALF:(j % 2 + 1) * HALF]
                        for k in range(DC):
                            m = mm(dst, actT[:, k, t * P:(t + 1) * P], wo[n][:, k, :], start=(k == 0),
                                   stop=(k == DC - 1))
                        m.then_inc(op_mm, 1)
                pe.wait_ge(op_mm, 2 * NT)
                pe.sem_inc(wo_used, 1)

                turn_h(0, NT)
                for t in range(NT):
                    if t + 1 < NT:
                        turn_h(t + 1, NT)
                    pe.wait_ge(h_ta, NT + t + 1)
                    pe.wait_ge(h_td, NT + t + 1)
                    for k in range(DC):
                        m = mm(o6[:, t * NE:(t + 1) * NE], actT[:, k, t * P:(t + 1) * P], rw[:, k, :],
                               start=(k == 0), stop=(k == DC - 1))
                m.then_inc(r_mm, 1)
                pe.wait_ge(r_mask, 1)
                pe.wait_ge(op_g, 2 * NT)
                pos = pair[0][:, 0:NT * NE].rearrange("p (t e) -> p t e", e=NE)
                mm(pos, k_("before"), mask, start=True, stop=False, skip_group_check=True)
                for i in range(NT - 1):
                    for t in range(i + 1, NT):
                        m = mm(pos[:, t, :], k_("ones"), mask[:, i, :], start=False, stop=(i == NT - 2),
                               skip_group_check=True)
                for i in range(NT):
                    m = mm(pair[0][:, HALF:HALF + NE], k_("ones"), mask[:, i, :], start=(i == 0), stop=(i == NT - 1))
                m.then_inc(r_tot, 1)
                for j in range(2 * NT):
                    pe.wait_ge(r_one, j + 1)
                    mm(pair[1][:, 0:NBLK], onep[j % 2], oneb[j % 2], start=(j == 0), stop=(j == 2 * NT - 1))\
                        .then_inc(r_pe1, 1)
                for a in (10, 11):
                    for cnd in range(2):
                        ada_rows_out(a, cnd, gain[:, (a - 10) * HALF:(a - 9) * HALF])

                pe.sem_inc(b_at, 2)
                pe.wait_ge(r_ctl, 1)
                n_pairs = pe.value_load(ctl[0:1, 0:1], min_val=NBLK_MIN // 2, max_val=NBLK // 2)
                before = pe.value_load(ctl[0:1, 1:2], min_val=0, max_val=DEPTH * NBLK // 2)
                pe.wait_ge(ada_bc_s, 20)
                with pe.Fori(0, n_pairs) as i:
                    for s in range(2):
                        b = i * 2 + s
                        pe.wait_ge(g_in[s], (before + i) * 16 + 16)
                        pe.wait_ge(b_ta, b + 1)
                        pe.wait_ge(b_td, b + 1)
                        if s == 1:
                            pe.wait_ge(b_atc, b)
                        for k in range(DC):
                            dst = pair[0][:, k * P:(k + 1) * P] if s == 0 else (o6, a7)[k // 4][:, k % 4 * P:(k % 4 + 1) * P]
                            m = tr(dst, xg[s][:, k * P:(k + 1) * P], ident)
                        m.then_inc(b_t, 1)
                    for s in range(2):
                        b = i * 2 + s
                        pe.wait_ge(b_ta, b + 2)
                        pe.wait_ge(b_td, b + 2)
                        pe.wait_ge(ld_gu[s], (before + i) * 32 + 32)
                        pe.wait_ge(b_act, b + 1)
                        for k in range(DC):
                            m = mm((tb4, tb5)[s][:, :], xgT[s][:, k, :], wgu[s][:, k, :], start=(k == 0),
                                   stop=(k == DC - 1))
                        m.then_inc(b_gu, 1)
                    for s in range(2):
                        b = i * 2 + s
                        pe.wait_ge(b_act, b + 3)
                        if s == 0:
                            pe.wait_ge(b_gu, b + 2)
                            pe.sem_inc(gu_used, 2)
                        for k in range(2):
                            m = tr((o6, a7)[s][:, k * P:(k + 1) * P], act_n[s][:, k * P:(k + 1) * P], ident)
                        m.then_inc(b_at, 1)
                        pe.wait_ge(b_atc, b + 2)
                        pe.wait_ge(ld_dn[s], (before + i) * 16 + 16)
                        pe.wait_ge(b_ya, b + 1)
                        pe.wait_ge(b_yd, b + 1)
                        for n in range(2):
                            for k in range(2):
                                m = mm(pair[1][:, n * HALF:(n + 1) * HALF], acT[s][:, k, :],
                                       wd[s][:, k, n * HALF:(n + 1) * HALF], start=(k == 0), stop=(k == 1))
                        m.then_inc(b_dn, 1)
                        pe.wait_ge(b_dn, b + 1)
                        pe.sem_inc(dn_used, 1)
                pe.sem_inc(moe_done, 1)
                pe.sem_inc(layer_end, 1)
                pe.wait_ge(layer_go, l + 1)

        @block.scalar
        def _(act):
            f = nc.scalar.activation
            act.wait_ge(cond_t, 1)
            act.wait_ge(start_d, 1)
            act.wait_ge(ld_start, 16 * 7)
            f(condT[:, :, 0:2], a7[:, 0:16].rearrange("p (c k) -> p k c", k=DC), ACT.Silu).then_inc(cond_s, 1)
            for a in range(4):
                act.wait_ge(first_ada[0], a + 1)
                if a > 0:
                    act.wait_ge(first_ada[2], a)
                f(part_s[:, :], a7[:, :], ACT.Copy).then_inc(first_ada[1], 1)
            for b in range(NBLK_MIN, NBLK, NT):
                n = min(NT, NBLK - b)
                act.dma_start(y_rows[b * P:(b + n) * P, :].rearrange("(t p) d -> p t d", p=P), x[:, 0:n, :])\
                    .then_inc(y_fill, 16)
            with act.Fori(0, DEPTH) as l:
                def ada_rows(a):
                    act.wait_ge(ada_part, a + 1)
                    if a > 0:
                        act.wait_ge(ada_bc, BC_BEFORE[min(a, 10)])
                    f(part_s[:, :] if a < 10 else gain[:, (a - 10) * HALF:(a - 9) * HALF], a7[:, :], ACT.Copy)\
                        .then_inc(ada_part_s, 1)

                def evac_h(t, first):
                    act.wait_ge(h_t, first + t + 1)
                    cols, src = slice(t * P, (t + 1) * P), tb4[:, :].rearrange("p (k n) -> p k n", n=P)
                    if first:
                        f(actT[:, 0:4, cols], src, ACT.Copy).then_inc(h_ta, 1)
                        return
                    c2 = ctx_of(t)
                    for k in range(4):
                        m = f(actT[:, k, cols], src[:, k, :], ACT.Identity, scale=gcol[:, k, c2:c2 + 1],
                              bias=scol[:, k, c2:c2 + 1])
                    m.then_inc(h_ta, 1)

                for t in range(NT):
                    if t > 0:
                        act.wait_ge(x_sq, t)
                    f(sq_x, x[:, t, :], ACT.Square, accum_out=ss[:, t:t + 1]).then_inc(x_sq, 1)
                act.wait_ge(first_ada[3], 4)

                def low_squares(t):
                    act.wait_ge(in_mm, t + 1)
                    if t > 0:
                        act.wait_ge(low_sq, t)
                    src = pair[t % 2]
                    f(sq_cq, src[:, 0:QR], ACT.Square, accum_out=low_ss[:, t, 0:1])
                    f(sq_ckv, src[:, HALF:HALF + KVR], ACT.Square, accum_out=low_ss[:, t, 1:2]).then_inc(low_sq, 1)
                    f(kr[:, key_tile(t), :], src[:, HALF + KVR:HALF + KVR + ROPE], ACT.Copy).then_inc(in_act, 1)

                def evac_cq(t):
                    act.wait_ge(low_t, t + 1)
                    f(cqT[:, :, t * P:(t + 1) * P], o6[:, 0:QR].rearrange("p (k n) -> p k n", n=P), ACT.Copy)\
                        .then_inc(low_ta, 1)

                evac_h(0, 0)
                for t in range(NT):
                    if t + 1 < NT:
                        evac_h(t + 1, 0)
                    low_squares(t)
                    if t == 0:
                        act.wait_ge(in_act, 1)
                        act.dma_start(new_krope[0, l], kr[:, CTX, :]).then_inc(out_done, 16)
                    if t > 0:
                        evac_cq(t - 1)
                    if t == 1:
                        act.wait_ge(keep_s, 1)
                        act.dma_start(new_ckv[0, l], ckv_keep).then_inc(keep_out, 16)
                for g in range(NG):
                    j = NT + g
                    act.wait_ge(in_mm, j + 1)
                    f(u[:, g, LAT0:LAT0 + DEC], pair[j % 2][:, 0:DEC], ACT.Copy).then_inc(in_act, 1)
                    if g == 0:
                        evac_cq(NT - 1)

                def q_squares(t):
                    act.wait_ge(q_mm, t + 1)
                    if t > 0:
                        act.wait_ge(q_ss, t)
                    for n in range(2):
                        m = f(sq_q[:, 4 * n:4 * n + 4, :],
                              pair[0][:, n * HALF:n * HALF + 4 * QH].rearrange("p (h d) -> p h d", d=QH), ACT.Square)
                    m.then_inc(q_sq, 1)

                def kv_read(j):
                    kt = KV_ORDER[j]
                    act.wait_ge(kv_mm, j + 1)
                    if j > 0:
                        act.wait_ge(k_ss, j)
                    f(sq_kr, kr[:, kt, :], ACT.Square, accum_out=kr_ss[:, kt:kt + 1])
                    for n in range(2):
                        m = f(sq_k[:, 4 * n:4 * n + 4, :],
                              pair[1][:, n * HALF:(n + 1) * HALF].rearrange("p (h d) -> p h d", d=P)[:, :, 0:NOPE],
                              ACT.Square)
                    m.then_inc(k_sq, 1)
                    for n in range(2):
                        m = f(V[:, kt, n * 256:(n + 1) * 256].rearrange("p (h d) -> p h d", d=VH),
                              pair[1][:, n * HALF:(n + 1) * HALF].rearrange("p (h d) -> p h d", d=P)[:, :, NOPE:P],
                              ACT.Copy)
                    m.then_inc(v_cp, 1)

                def evac_heads(dst, tile, job):
                    act.wait_ge(qk_t, job + 1)
                    f(dst[0:QH, 0:4, tile * P:(tile + 1) * P], tb4[0:QH, :].rearrange("p (k n) -> p k n", n=P),
                      ACT.Copy).then_inc(qk_ta, 1)

                act.wait_ge(ld_small, (l + 1) * (7 * 16))
                act.wait_ge(keep_out, 16)
                q_squares(0)
                kv_read(0)
                for j in range(NT + 1):
                    if j < NT:
                        evac_heads(qT, j, 2 * j)
                        if j + 1 < NT:
                            q_squares(j + 1)
                    evac_heads(kT, KV_ORDER[j], 2 * j + 1 if j < NT else 2 * NT)
                    if j + 1 <= NT:
                        kv_read(j + 1)
                    for a, step in COL_STEPS[2 * j:2 * j + 2]:
                        if step == 1:
                            ada_rows(a)
                for g in range(NG):
                    act.wait_ge(pool_mm, g + 1)
                    f(actT[:, g, P:NTOK], pair[g % 2][:, 0:DEC], ACT.Copy, scale=pscale[:, g:g + 1])\
                        .then_inc(pool_ea, 1)

                def exps(un):
                    t, _ = UNITS[un]
                    n = 1 if t == 0 else NLK
                    act.wait_ge(s_mx, un + 1)
                    if un >= 2:
                        act.wait_ge(s_pt, un - 1)
                    f(prob[un % 2][:, 0:n, :], pair[un % 2][:, 0:n * P].rearrange("p (k n) -> p k n", n=P), ACT.Exp,
                      bias=nmax[:, un % 2:un % 2 + 1], scale=SCALE, accum_out=esum[:, un:un + 1]).then_inc(s_exp, 1)

                for un in range(NU + 2):
                    if un < NU:
                        exps(un)
                    if un >= H + 1 and (un - 1) % H == 0:
                        t = (un - 1) // H - 1
                        act.wait_ge(s_ot, t + 1)
                        f(actT[:, 4:8, t * P:(t + 1) * P], tb4[:, :].rearrange("p (k n) -> p k n", n=P), ACT.Copy)\
                            .then_inc(s_otc, 1)
                    if un < NU:
                        n = 1 if UNITS[un][0] == 0 else 3
                        act.wait_ge(s_pt, un + 1)
                        if un >= 2:
                            act.wait_ge(s_pv, un - 1)
                        f(probT[un % 2][:, 0:n, :], tb4[:, 0:n * P].rearrange("p (k n) -> p k n", n=P), ACT.Copy)\
                            .then_inc(s_pta, 1)
                    if un in ADA_AT and ADA_AT[un][1] == 1:
                        ada_rows(ADA_AT[un][0])

                for t in range(NT):
                    act.wait_ge(op_x, NT + t + 1)
                    act.wait_ge(x_sq, NT + t)
                    f(sq_x, x[:, t, :], ACT.Square, accum_out=ss[:, NT + t:NT + t + 1]).then_inc(x_sq, 1)
                for t in range(NT):
                    evac_h(t, NT)
                    act.wait_ge(h_ready, NT + t + 1)
                    act.dma_start(h2_rows[t * P:(t + 1) * P, :], xn[t % 2]).then_inc(h_st[t % 2], 16)
                act.wait_ge(r_mm, 1)
                f(sig, o6[:, 0:NT * NE].rearrange("p (a b) -> p a b", b=GE), ACT.Exp, scale=-1.0).then_inc(r_e, 1)

                act.wait_ge(r_ctl, 1)
                act.wait_ge(ada_bc, 20)
                n_pairs = act.value_load(ctl[0:1, 0:1], min_val=NBLK_MIN // 2, max_val=NBLK // 2)
                for count, n in ((b_ta, 1), (b_atc, 1), (b_ya, 1), (b_st, 16)):
                    act.sem_inc(count, n)
                with act.Fori(0, n_pairs) as i:
                    for s in range(2):
                        b = i * 2 + s
                        act.wait_ge(b_t, b + 1)
                        src = pair[0][:, 0:HALF] if s == 0 else o6[:, :]
                        f(xgT[s][:, 0:4, :], src.rearrange("p (k n) -> p k n", n=P), ACT.Copy).then_inc(b_ta, 1)
                    for s in range(2):
                        act.wait_ge(b_gu, i * 2 + s + 1)
                        f(sil[s], (tb4, tb5)[s][:, 0:DE], ACT.Silu).then_inc(b_sil, 1)
                    for s in range(2):
                        b = i * 2 + s
                        act.wait_ge(b_at, b + 3)
                        f(acT[s][:, :, :], (o6, a7)[s][:, 0:2 * P].rearrange("p (k n) -> p k n", n=P), ACT.Copy)\
                            .then_inc(b_atc, 1)
                        act.wait_ge(b_dn, b + 1)
                        act.wait_ge(b_st, b * 16 + 16)
                        f(yb[:, 0:HALF], pair[1][:, 0:HALF], ACT.Copy).then_inc(b_ya, 1)
                        act.wait_ge(b_ya, b + 2)
                        act.wait_ge(b_yd, b + 2)
                        act.dma_start(y_rows[bass.ds(b * P, P), :], yb).then_inc(b_st, 16)
                act.wait_ge(b_st, n_pairs * 32 + 16)
                act.sem_inc(y_done, 1)
                for t in range(NT):
                    k = (2 * t) % 4
                    act.wait_ge(c_in[k], l * (C_USES[k] * 16) + (t // 2 + 1) * 16)
                    f(comb[k], comb[k], ACT.Copy, scale=gates2[:, t:t + 1]).then_inc(c_hi, 1)
                act.sem_inc(layer_end, 1)
                act.wait_ge(layer_go, l + 1)
            

        @block.gpsimd
        def _(pool):
            tt, ts = nc.gpsimd.tensor_tensor, nc.gpsimd.tensor_scalar
            mhalf = k_("mhalf")
            with pool.Fori(0, DEPTH) as l:
                chain = [0]

                def link(ins):
                    ins.then_inc(pl, 1)
                    chain[0] += 1
                    pool.wait_ge(pl, chain[0])

                def row_rs(j):
                    pool.wait_ge(x_sq, j + 1)
                    link(ts(ss[:, j:j + 1], ss[:, j:j + 1], 1.0 / D, EPS, ALU.mult, ALU.add))
                    tt(rs[:, j:j + 1], ss[:, j:j + 1], mhalf[:, 0:1], ALU.pow).then_inc(x_rs, 1)

                pool.wait_ge(ld_start, 16 * 7)
                for t in range(NT):
                    row_rs(t)
                for t in range(NT):
                    pool.wait_ge(low_sq, t + 1)
                    ts(low_ss[:, t, 0:1], low_ss[:, t, 0:1], 1.0 / QR, EPS, ALU.mult, ALU.add)
                    link(ts(low_ss[:, t, 1:2], low_ss[:, t, 1:2], 1.0 / KVR, EPS, ALU.mult, ALU.add))
                    tt(low_rs[:, t, :], low_ss[:, t, :], mhalf[:, 0:2], ALU.pow).then_inc(low_r, 1)
                pool.wait_ge(h_ready, NT)
                for lo, hi in ((0, GAP), (GAP + SEQ, LAT0), (LAT0 + DEC, PW)):
                    m = nc.gpsimd.memset(u[:, :, lo:hi], 0.0)
                m.then_inc(pool_z, 1)

                def rope_key(j):
                    kt = KV_ORDER[j]
                    if j == 0:
                        pool.wait_ge(ld_small, (l + 1) * (7 * 16))
                    if not 1 <= kt <= NT - 1:
                        tt(krr[:, kt, :], kr[:, kt, :], gk[:, NOPE:QH], ALU.mult).then_inc(krr_s, 1)
                        return
                    link(tt(rope_t[:, 0, :], kr[:, kt, :], gk[:, NOPE:QH], ALU.mult))
                    hr = ROPE // 2
                    a, c2 = rope_t[:, 0, :], rope_t[:, 1, :]
                    cos, sin = (k_(n)[:, (kt - 1) * hr:kt * hr] for n in ("cos", "sin"))
                    link(tt(krr[:, kt, 0:hr], a[:, 0:hr], cos, ALU.mult))
                    link(tt(krr[:, kt, hr:ROPE], a[:, 0:hr], sin, ALU.mult))
                    link(tt(c2[:, 0:hr], a[:, hr:ROPE], sin, ALU.mult))
                    link(tt(c2[:, hr:ROPE], a[:, hr:ROPE], cos, ALU.mult))
                    tt(krr[:, kt, 0:hr], krr[:, kt, 0:hr], c2[:, 0:hr], ALU.subtract)
                    tt(krr[:, kt, hr:ROPE], krr[:, kt, hr:ROPE], c2[:, hr:ROPE], ALU.add).then_inc(krr_s, 1)

                def head_rs_of(j, which):
                    s_ = head_ss[:, j % 2, which, :]
                    if which == 1:
                        kt = KV_ORDER[j]
                        link(tt(s_, s_, kr_ss[:, kt:kt + 1].broadcast_to([P, H]), ALU.add))
                    link(ts(s_, s_, 1.0 / QH, EPS, ALU.mult, ALU.add))
                    tt(head_rs[:, j % 2, which, :], s_, mhalf, ALU.pow).then_inc((q_rs, k_rs)[which], 1)

                def pool_group(g):
                    if g == 0:
                        pool.wait_ge(in_act, NT + NG)
                        pool.wait_ge(in_dve, NT + NG)
                        pool.wait_ge(pool_z, 1)
                    src, bufs = u[:, g, :], (pa, pb)
                    link(tt(pa[:, 1:PW], src[:, 0:PW - 1], src[:, 1:PW], ALU.add))
                    for lv in range(1, g + 1):
                        r, lo = 1 << (lv - 1), 1 << lv
                        hi = PW + 1 - lo
                        a, b = bufs[(lv - 1) % 2], bufs[lv % 2]
                        link(tt(b[:, lo:hi], a[:, lo - r:hi - r], a[:, lo + r:hi + r], ALU.add))
                    w = bufs[g % 2]
                    e = k_("edge")[:, 16 * g:16 * g + 16]
                    for first, n in ((CTX0, SEQ), (LAT0, DEC)):
                        link(tt(w[:, first:first + 8], w[:, first:first + 8], e[:, 0:8], ALU.mult))
                        link(tt(w[:, first + n - 8:first + n], w[:, first + n - 8:first + n], e[:, 8:16], ALU.mult))
                    link(ts(w[:, GAP:PW - GAP], w[:, GAP:PW - GAP], 1.0 / WINDOWS[g], 0.0, ALU.mult, ALU.add))
                    tt(u[:, g, GAP:PW - GAP], w[:, GAP:PW - GAP], u[:, g, GAP:PW - GAP], ALU.subtract)\
                        .then_inc(pool_d, 1)

                for j in range(NT + 1):
                    if j < NT:
                        pool.wait_ge(q_ss, j + 1)
                        if j >= 2:
                            pool.wait_ge(q_rd, j - 1)
                        head_rs_of(j, 0)
                    rope_key(j)
                    pool.wait_ge(k_ss, j + 1)
                    if j >= 2:
                        pool.wait_ge(k_n, j - 1)
                    head_rs_of(j, 1)
                    if j < NG:
                        pool_group(j)

                pool.wait_ge(y_fill, FILLS * 16)
                for j in range(2 * NT):
                    n, t = divmod(j, NT)
                    pool.wait_ge(op_g, j + 1)
                    xs = x[:, t, n * HALF:(n + 1) * HALF]
                    tt(xs, xs, out_s[j % 4], ALU.add).then_inc(op_x, 1)
                for t in range(NT):
                    row_rs(NT + t)

                pool.wait_ge(r_idx, 1)
                pool.wait_ge(h_st[0], 16 * 3)
                pool.wait_ge(h_st[1], 16 * 2)
                pool.wait_ge(h_t, 2 * NT)
                pool.wait_ge(r_ctl, 1)
                n_pairs = pool.value_load(ctl[0:1, 0:1], min_val=NBLK_MIN // 2, max_val=NBLK // 2)

                def gather_pair(i):
                    for b in (2 * i, 2 * i + 1):
                        if b >= 2:
                            pool.wait_ge(b_t, b - 1)
                        nc.gpsimd.indirect_dma_start(
                            xg[b % 2], None, h2_rows, bass.IndirectOffsetOnAxis(ap=idx[:, b:b + 1], axis=0))\
                            .then_inc(g_in[b % 2], 16)

                for i in range(NBLK // 2):
                    if i < NBLK_MIN // 2:
                        gather_pair(i)
                    else:
                        with pool.If(n_pairs > i):
                            gather_pair(i)
                pool.wait_ge(y_done, 1)
                for t in range(NT):
                    for w in range(2):
                        k = (2 * t + w) % 4
                        if t >= 2:
                            pool.wait_ge(c_gt, t - 1)
                        nc.gpsimd.indirect_dma_start(
                            comb[k], None, y_rows,
                            bass.IndirectOffsetOnAxis(ap=slot_i[:, w * NT + t:w * NT + t + 1], axis=0))\
                            .then_inc(c_in[k], 16)
                pool.sem_inc(layer_end, 1)
                pool.wait_ge(layer_go, l + 1)

        @block.vector
        def _(ve):
            v = nc.vector
            v.memset(pairs[:, :], 0.0)
            v.memset(condT[:, :, :], 0.0).then_inc(start_d, 1)

            def columns_out(a, counts):
                p, n = divmod(a, 2)
                ve.wait_ge(counts[2], a + 1)
                ks, src = slice(4 * n, 4 * n + 4), a7[:, 0:8].rearrange("p (k c) -> p k c", c=2)
                if p == 0:
                    m = v.tensor_copy(scol[:, ks, :], src)
                else:
                    m = v.scalar_tensor_tensor(gcol[:, ks, :], src, 1.0,
                                               gn1[:, ks].unsqueeze(2).broadcast_to([P, 4, 2]), ALU.add, ALU.mult)
                m.then_inc(counts[3], 1)

            ve.wait_ge(ld_gn1, 16)
            for a in range(4):
                columns_out(a, first_ada)
            with ve.Fori(0, DEPTH) as l:
                chain = [0]

                def link(ins):
                    ins.then_inc(dv, 1)
                    chain[0] += 1
                    ve.wait_ge(dv, chain[0])

                def ada_half(a, cnd):
                    p, n = divmod(a, 2)
                    cols = slice(n * HALF, (n + 1) * HALF)
                    ve.wait_ge(ada_bc, BC_BEFORE[a] + cnd + 1)
                    if p == 4:
                        ve.wait_ge(ld_gain, l * 16 + 16)
                        m = v.scalar_tensor_tensor(G[:, cnd, cols], a7[:, :], 1.0, gain[:, cols], ALU.add, ALU.mult)
                    else:
                        m = v.tensor_copy((S if p == 3 else gate)[:, cnd, cols], a7[:, :])
                    m.then_inc(ada_bc_s, 1)

                def norm(t, j):
                    ve.wait_ge(x_rs, j + 1)
                    if j >= 2:
                        ve.wait_ge(h_t, j - 1)
                    if j >= NT + 2:
                        ve.wait_ge(h_st[t % 2], 16 * (t // 2))
                    if j < NT:
                        v.tensor_scalar(xn[t % 2], x[:, t, :], rs[:, j:j + 1], None, ALU.mult).then_inc(h_ready, 1)
                        return
                    c2 = ctx_of(t)
                    link(v.scalar_tensor_tensor(xn[t % 2], x[:, t, :], rs[:, j:j + 1], G[:, c2, :], ALU.mult, ALU.mult))
                    v.tensor_tensor(xn[t % 2], xn[t % 2], S[:, c2, :], ALU.add).then_inc(h_ready, 1)

                def evac_h(t, first):
                    ve.wait_ge(h_t, first + t + 1)
                    cols, src = slice(t * P, (t + 1) * P), tb5[:, :].rearrange("p (k n) -> p k n", n=P)
                    if first:
                        v.tensor_copy(actT[:, 4:8, cols], src).then_inc(h_td, 1)
                        return
                    c2 = ctx_of(t)
                    for k in range(4):
                        m = v.tensor_scalar(actT[:, 4 + k, cols], src[:, k, :], gcol[:, 4 + k, c2:c2 + 1],
                                            scol[:, 4 + k, c2:c2 + 1], ALU.mult, ALU.add)
                    m.then_inc(h_td, 1)

                ve.wait_ge(ld_start, 16 * 7)
                ve.wait_ge(first_ada[3], 4)
                norm(0, 0)
                norm(1, 1)

                def low_norm(t):
                    ve.wait_ge(low_r, t + 1)
                    ve.wait_ge(in_act, t + 1)
                    if t > 0:
                        ve.wait_ge(low_t, t)
                    else:
                        ve.wait_ge(ld_small, (l + 1) * (7 * 16))
                    src = pair[t % 2]
                    stt = v.scalar_tensor_tensor
                    if t == 0:
                        stt(ckv_keep, src[:, HALF:HALF + KVR], low_rs[:, t, 1:2], gkva, ALU.mult, ALU.mult)\
                            .then_inc(keep_s, 1)
                    stt(cn[:, 0:QR], src[:, 0:QR], low_rs[:, t, 0:1], gqa, ALU.mult, ALU.mult)
                    stt(cn[:, QR:QR + KVR], src[:, HALF:HALF + KVR], low_rs[:, t, 1:2], gkva, ALU.mult, ALU.mult)\
                        .then_inc(in_dve, 1)

                def evac_ckv(j):
                    kt = KV_ORDER[j]
                    ve.wait_ge(low_t, j + 1)
                    v.tensor_copy(ckvT[:, :, kt * P:(kt + 1) * P], a7[:, 0:KVR].rearrange("p (k n) -> p k n", n=P))\
                        .then_inc(low_td, 1)

                evac_h(0, 0)
                for t in range(NT):
                    if t + 2 < NT:
                        norm(t + 2, t + 2)
                    if t + 1 < NT:
                        evac_h(t + 1, 0)
                    low_norm(t)
                    if t > 0:
                        evac_ckv(t - 1)
                for g in range(NG):
                    j = NT + g
                    ve.wait_ge(in_mm, j + 1)
                    v.tensor_copy(u[:, g, CTX0:CTX0 + SEQ], pair[j % 2][:, HALF:HALF + SEQ]).then_inc(in_dve, 1)
                    if g == 0:
                        evac_ckv(NT - 1)
                    if g == 1:
                        evac_ckv(NT)

                def bc(a, n):
                    return a.unsqueeze(2).broadcast_to([P, a.shape[1], n])

                def q_norm(t):
                    ve.wait_ge(q_sq, t + 1)
                    v.tensor_reduce(head_ss[:, t % 2, 0, :], sq_q, AX.X, ALU.add).then_inc(q_ss, 1)
                    ve.wait_ge(q_rs, t + 1)
                    if t > 0:
                        ve.wait_ge(qk_t, 2 * t - 1)
                    for n in range(2):
                        m = v.tensor_tensor(qn[:, 4 * n:4 * n + 4, :],
                                            pair[0][:, n * HALF:n * HALF + 4 * QH].rearrange("p (h d) -> p h d", d=QH),
                                            bc(head_rs[:, t % 2, 0, 4 * n:4 * n + 4], QH), ALU.mult)
                    m.then_inc(q_rd, 1)
                    ve.wait_ge(q_rd, t + 1)
                    gq_b = gq[:, :].unsqueeze(1).broadcast_to([P, H, QH])
                    if t == 0:
                        v.tensor_tensor(qn, qn, gq_b, ALU.mult).then_inc(q_n, 1)
                        return
                    link(v.tensor_tensor(qn, qn, gq_b, ALU.mult))
                    hr = ROPE // 2
                    r1, r2 = qn[:, :, NOPE:NOPE + hr], qn[:, :, NOPE + hr:QH]
                    cos, sin = (k_(n)[:, (t - 1) * hr:t * hr].unsqueeze(1).broadcast_to([P, H, hr])
                                for n in ("cos", "sin"))
                    v.tensor_tensor(rq[0], r1, sin, ALU.mult)
                    v.tensor_tensor(rq[1], r2, sin, ALU.mult)
                    v.tensor_tensor(rq[2], r1, cos, ALU.mult)
                    link(v.tensor_tensor(rq[3], r2, cos, ALU.mult))
                    v.tensor_tensor(r1, rq[2], rq[1], ALU.subtract)
                    v.tensor_tensor(r2, rq[0], rq[3], ALU.add).then_inc(q_n, 1)

                def k_norm(j):
                    kt = KV_ORDER[j]
                    ve.wait_ge(k_sq, j + 1)
                    v.tensor_reduce(head_ss[:, j % 2, 1, :], sq_k, AX.X, ALU.add).then_inc(k_ss, 1)
                    ve.wait_ge(k_rs, j + 1)
                    ve.wait_ge(v_cp, j + 1)
                    if j > 0:
                        ve.wait_ge(qk_t, 2 * j)
                    r = head_rs[:, j % 2, 1, :]
                    for n in range(2):
                        m = v.tensor_tensor(
                            kn[:, 4 * n:4 * n + 4, 0:NOPE],
                            pair[1][:, n * HALF:(n + 1) * HALF].rearrange("p (h d) -> p h d", d=P)[:, :, 0:NOPE],
                            bc(r[:, 4 * n:4 * n + 4], NOPE), ALU.mult)
                    m.then_inc(k_rd, 1)
                    ve.wait_ge(krr_s, j + 1)
                    v.tensor_tensor(kn[:, :, NOPE:QH], krr[:, kt, :].unsqueeze(1).broadcast_to([P, H, ROPE]),
                                    bc(r, ROPE), ALU.mult)
                    ve.wait_ge(k_rd, j + 1)
                    v.tensor_tensor(kn[:, :, 0:NOPE], kn[:, :, 0:NOPE],
                                    gk[:, 0:NOPE].unsqueeze(1).broadcast_to([P, H, NOPE]), ALU.mult).then_inc(k_n, 1)

                def evac_heads(dst, tile, job):
                    ve.wait_ge(qk_t, job + 1)
                    v.tensor_copy(dst[0:QH, 4:8, tile * P:(tile + 1) * P],
                                  tb5[0:QH, :].rearrange("p (k n) -> p k n", n=P)).then_inc(qk_td, 1)

                ve.wait_ge(low_t, NT + 1)
                ve.wait_ge(keep_out, 16)
                q_norm(0)
                k_norm(0)
                for j in range(NT + 1):
                    if j < NT:
                        evac_heads(qT, j, 2 * j)
                        if j + 1 < NT:
                            q_norm(j + 1)
                    evac_heads(kT, KV_ORDER[j], 2 * j + 1 if j < NT else 2 * NT)
                    if j + 1 <= NT:
                        k_norm(j + 1)
                    for a, step in COL_STEPS[2 * j:2 * j + 2]:
                        if step == 2:
                            if a == 2:
                                ve.wait_ge(ld_gn1, (l + 1) * 16 + 16)
                            columns_out(a, layer_ada)
                for g in range(NG):
                    ve.wait_ge(pool_mm, g + 1)
                    v.tensor_scalar(actT[:, g, 0:P], pair[g % 2][:, HALF:HALF + SEQ], pscale[:, g:g + 1], None, ALU.mult)\
                        .then_inc(pool_ed, 1)

                def maxes(un):
                    t, _ = UNITS[un]
                    n = P if t == 0 else NLK * P
                    ve.wait_ge(s_sc, un + 1)
                    link(v.tensor_reduce(mx[:, un % 2:un % 2 + 1], pair[un % 2][:, 0:n], AX.X, ALU.max))
                    if un >= 2:
                        ve.wait_ge(s_exp, un - 1)
                    v.tensor_scalar(nmax[:, un % 2:un % 2 + 1], mx[:, un % 2:un % 2 + 1], -SCALE, None, ALU.mult)\
                        .then_inc(s_mx, 1)

                def tile_out(t):
                    ve.wait_ge(s_exp, (t + 1) * H)
                    link(v.reciprocal(rsum[:, :], esum[:, t * H:(t + 1) * H]))
                    ve.wait_ge(s_pv, (t + 1) * H)
                    if t > 0:
                        ve.wait_ge(s_ot, t)
                    v.tensor_tensor(onat.rearrange("p (h d) -> p h d", d=VH),
                                    o6[:, :].rearrange("p (h d) -> p h d", d=VH), bc(rsum[:, :], VH), ALU.mult)\
                        .then_inc(s_on, 1)

                maxes(0)
                for un in range(NU + 1):
                    if un + 1 < NU:
                        maxes(un + 1)
                    if un >= H and un % H == 0:
                        tile_out(un // H - 1)
                    if un < NU:
                        ve.wait_ge(s_pt, un + 1)
                        if UNITS[un][0] == 0:
                            ve.sem_inc(s_ptb, 1)
                        else:
                            if un >= 2:
                                ve.wait_ge(s_pv, un - 1)
                            v.tensor_copy(probT[un % 2][:, 3:NLK, :], tb5[:, 0:2 * P].rearrange("p (k n) -> p k n", n=P))\
                                .then_inc(s_ptb, 1)
                    if un in ADA_AT and ADA_AT[un][1] >= 2:
                        ada_half(ADA_AT[un][0], ADA_AT[un][1] - 2)
                ve.wait_ge(ada_bc_s, 16)

                for j in range(2 * NT):
                    n, t = divmod(j, NT)
                    ve.wait_ge(op_mm, j + 1)
                    if j >= 4:
                        ve.wait_ge(op_x, j - 3)
                    src = pair[(j % 4) // 2][:, (j % 2) * HALF:(j % 2 + 1) * HALF]
                    v.tensor_tensor(out_s[j % 4], src, gate[:, ctx_of(t), n * HALF:(n + 1) * HALF], ALU.mult)\
                        .then_inc(op_g, 1)

                norm(0, NT)
                norm(1, NT + 1)
                for t in range(NT):
                    evac_h(t, NT)
                    if t + 2 < NT:
                        norm(t + 2, NT + t + 2)

                tt, ts, red = v.tensor_tensor, v.tensor_scalar, v.tensor_reduce
                ve.wait_ge(r_e, 1)
                link(ts(sig, sig, 1.0, None, ALU.add))
                link(v.reciprocal(sig, sig))
                rb_b = rb[:, :].unsqueeze(1).broadcast_to([P, NT, NE])
                by_tile = lambda a: a.rearrange("p (t g) k -> p t (g k)", t=NT)
                link(tt(by_tile(sel_s), by_tile(sig), rb_b, ALU.add))

                def ranks(out, val, gt, eq, n):
                    q = val.shape[1]
                    a = val.unsqueeze(3).broadcast_to([P, q, n, n])
                    b = val.unsqueeze(2).broadcast_to([P, q, n, n])
                    tt(gt, b, a, ALU.is_gt)
                    link(tt(eq, b, a, ALU.is_equal))
                    low_b = k_("lower").unsqueeze(1).broadcast_to([P, q, n * n])
                    link(tt(eq.rearrange("p q i j -> p q (i j)"), eq.rearrange("p q i j -> p q (i j)"), low_b, ALU.mult))
                    link(tt(gt, gt, eq, ALU.add))
                    link(red(out, gt, AX.X, ALU.add))

                ranks(rank, sel_s, cmp4, eq4, GE)
                link(ts(chosen, rank, 2.0, None, ALU.is_lt))
                link(tt(rank, sel_s, chosen, ALU.mult))
                link(red(gsc.rearrange("p t g -> p (t g)"), rank, AX.X, ALU.add))
                ranks(best, gsc, gcmp, geq, EG)
                link(ts(best, best, 1.0, None, ALU.is_lt))
                tt(mask.rearrange("p t (g k) -> p (t g) k", k=GE), chosen,
                   best.rearrange("p t g -> p (t g)").unsqueeze(2).broadcast_to([P, NT * EG, GE]), ALU.mult)\
                    .then_inc(r_mask, 1)
                ve.wait_ge(r_mask, 1)
                link(tt(gts, by_tile(sig), mask, ALU.mult))
                link(red(den, gts, AX.X, ALU.add))
                link(v.reciprocal(den, den))
                link(tt(gts, gts, bc(den, NE), ALU.mult))
                ve.wait_ge(r_tot, 1)
                tot = pair[0][:, HALF:HALF + NE]
                link(tt(nbc, bc(tot, 5), k_("kblock").unsqueeze(1).broadcast_to([P, NE, 5]), ALU.is_gt))
                link(red(nb, nbc, AX.X, ALU.add))
                link(v.tensor_tensor_scan(endb, k_("ones")[:, 0:NE], nb, 0.0, ALU.mult, ALU.add))
                tt(start, endb, nb, ALU.subtract)
                link(tt(ecmp, endb.unsqueeze(1).broadcast_to([P, NBLK, NE]), bc(k_("block"), NE), ALU.is_le))
                link(red(eidf, ecmp, AX.X, ALU.add))
                link(ts(pcmp, k_("block")[:, 0:NBLK:2], endb[:, NE - 1:NE], None, ALU.is_lt))
                link(red(nb[:, 0:1], pcmp, AX.X, ALU.add))
                v.tensor_copy(ctl[:, 0:1], nb[:, 0:1])
                link(v.tensor_copy(ctl[:, 1:2], pairs[:, :]))
                link(tt(pairs[:, :], pairs[:, :], nb[:, 0:1], ALU.add))
                link(ts(eid[:, :], eidf, float(NE - 1), None, ALU.min))
                ve.sem_inc(eid_ready, 1)
                ve.sem_inc(r_ctl, 1)
                pos = pair[0][:, 0:NT * NE].rearrange("p (t e) -> p t e", e=NE)
                link(ts(start, start, float(P), 1.0, ALU.mult, ALU.add))
                link(tt(slot1, pos, start.unsqueeze(1).broadcast_to([P, NT, NE]), ALU.add))
                link(tt(slot1, slot1, mask, ALU.mult))
                red(pick[:, 0, :], slot1, AX.X, ALU.max)
                link(red(den, slot1, AX.X, ALU.add))
                link(tt(pick[:, 1, :], den, pick[:, 0, :], ALU.subtract))
                for w in range(2):
                    m = tt(hot[:, w], slot1, bc(pick[:, w, :], NE), ALU.is_equal)
                link(m)
                for w in range(2):
                    m = tt(prod[:, w], hot[:, w], gts, ALU.mult)
                link(m)
                for w in range(2):
                    m = red(gates2[:, w * NT:(w + 1) * NT], prod[:, w], AX.X, ALU.add)
                link(m)
                flat_pick = pick.rearrange("p w t -> p (w t)")
                link(ts(slot_i[:, :], flat_pick, -1.0, None, ALU.add))
                ts(slot_a[:, :], slot_i[:, :], P - 1, None, ALU.bitwise_and)
                link(ts(slot_b[:, :], slot_i[:, :], 7, None, ALU.logical_shift_right))
                v.tensor_copy(slot_p, slot_a[:, :])
                link(v.tensor_copy(slot_q, slot_b[:, :]))
                for j in range(2 * NT):
                    if j >= 2:
                        ve.wait_ge(r_pe1, j - 1)
                    ts(onep[j % 2], k_("row"), slot_p[:, j:j + 1], None, ALU.is_equal)
                    ts(oneb[j % 2], k_("block"), slot_q[:, j:j + 1], k_("token")[:, j % NT:j % NT + 1], ALU.is_equal,
                       ALU.mult).then_inc(r_one, 1)
                ve.wait_ge(r_pe1, 2 * NT)
                v.tensor_copy(idx[:, :], pair[1][:, 0:NBLK]).then_inc(r_idx, 1)
                for a in (10, 11):
                    for cnd in range(2):
                        ada_half(a, cnd)

                for count, n in ((b_td, 1), (b_act, 2), (b_yd, 1)):
                    ve.sem_inc(count, n)
                n_pairs = ve.value_load(ctl[0:1, 0:1], min_val=NBLK_MIN // 2, max_val=NBLK // 2)
                with ve.Fori(0, n_pairs) as i:
                    for s in range(2):
                        ve.wait_ge(b_t, i * 2 + s + 1)
                        src = pair[0][:, HALF:2 * HALF] if s == 0 else a7[:, :]
                        v.tensor_copy(xgT[s][:, 4:8, :], src.rearrange("p (k n) -> p k n", n=P)).then_inc(b_td, 1)
                    for s in range(2):
                        ve.wait_ge(b_sil, i * 2 + s + 1)
                        ve.wait_ge(b_at, i * 2 + s + 1)
                        v.tensor_tensor(act_n[s], sil[s], (tb4, tb5)[s][:, DE:2 * DE], ALU.mult).then_inc(b_act, 1)
                    for s in range(2):
                        b = i * 2 + s
                        ve.wait_ge(b_dn, b + 1)
                        ve.wait_ge(b_st, b * 16 + 16)
                        v.tensor_copy(yb[:, HALF:D], pair[1][:, HALF:2 * HALF]).then_inc(b_yd, 1)
                ve.wait_ge(ada_bc_s, 20)
                for t in range(NT):
                    k = (2 * t) % 4
                    ve.wait_ge(c_hi, t + 1)
                    ve.wait_ge(c_in[k + 1], l * (C_USES[k + 1] * 16) + (t // 2 + 1) * 16)
                    link(v.scalar_tensor_tensor(comb[k + 1], comb[k + 1], gates2[:, NT + t:NT + t + 1], comb[k],
                                                ALU.mult, ALU.add))
                    link(tt(comb[k + 1], comb[k + 1], gate[:, ctx_of(t), :], ALU.mult))
                    tt(x[:, t, :], x[:, t, :], comb[k + 1], ALU.add).then_inc(c_gt, 1)
                ve.wait_ge(c_gt, NT)
                ve.wait_ge(layer_end, 3)
                for s in cleared:
                    ve.sem_clear(s)
                ve.sem_inc(layer_go, 1)


def kernel(**inputs):
    import concourse.bacc as bacc
    from concourse.bass_utils import run_bass_kernel_spmd

    arrays = {n: np.ascontiguousarray(inputs[n]) for n in INS}
    table, at = constants()
    arrays["consts"] = table
    nc = bacc.Bacc("TRN2", target_bir_lowering=False, num_devices=1)
    ins = {n: nc.dram_tensor(n, a.shape, mybir.dt.from_np(a.dtype), kind="ExternalInput").ap()
           for n, a in arrays.items()}
    outs = {n: nc.dram_tensor(n, s, F32, kind="ExternalOutput").ap() for n, s in OUTS.items()}
    step_kernel(nc, **ins, **outs, const_at=at)
    r = run_bass_kernel_spmd(nc, [arrays], core_ids=[0])
    return tuple(r.results[0][n] for n in OUTS)


INS = ["x_prompt", "x_sample", "cache_ckv", "cache_krope", "c", "c_ctx", "ada_w", "ada_b", "norm1_g", "norm2_g", "w_in",
       "pool_w", "pool_scale", "q_a_norm_g", "w_uq", "kv_a_norm_g", "w_ukv", "q_norm_g", "k_norm_g", "w_out",
       "router_w", "router_b", "w_gate", "w_up", "w_down"]
OUTS = {"y_prompt": (1, SEQ, D), "y_sample": (1, DEC, D), "new_ckv": (1, DEPTH, SEQ, KVR),
        "new_krope": (1, DEPTH, SEQ, ROPE)}
```

```python
from contextlib import ExitStack

import numpy as np

import concourse.bass as bass
from concourse import mybir

F32 = mybir.dt.float32
I32 = mybir.dt.int32
U32 = mybir.dt.uint32
ALU = mybir.AluOpType
ACT = mybir.ActivationFunctionType
AX = mybir.AxisListType

P = 128
DEPTH = 2
D = 1024
DC = D // P
SEQ, DEC = 128, 512
NT = (SEQ + DEC) // P
NTOK = NT * P
GRID_W = 64
WINDOWS = (2, 4, 8, 16)
NG = len(WINDOWS)
POOLW = NG * P
H = 8
NOPE, ROPE, VH = 64, 32, 64
QH = NOPE + ROPE
QR, KVR = 384, 256
QC, KC = QR // P, KVR // P
INW = POOLW + QR + KVR + ROPE
NE, EG, GE = 16, 4, 4
DE = 256
EPS = 1e-6
SCALE = 1.0 / float(np.sqrt(QH))
NKT = NT + 1
NLK = NKT - 1
CTX = NKT - 1
NPIECE = 6
HALF = 512
NBLK = 26
NBLK_MIN = 2 * NTOK // P
FILLS = -(-(NBLK - NBLK_MIN) // NT)
NSLOT = NBLK * P
UNITS = [(t, h) for t in range(NT) for h in range(H)]
NU = len(UNITS)
GAP = 16
PW = GAP + SEQ + GAP + DEC + GAP
CTX0, LAT0 = GAP, GAP + SEQ + GAP

COL_STEPS = [(a, step) for a in range(4) for step in range(3)]
ROW_STEPS = [(a, step) for a in range(4, 10) for step in range(4)] + [(a, step) for a in (10, 11) for step in range(2)]
ADA_AT = {2 + n: st for n, st in enumerate(ROW_STEPS)}
BC_BEFORE = [0, 1, 2, 3] + [4 + 2 * n for n in range(8)] + [20]


def constants():
    cols, at = [], {}

    def put(name, a):
        full = np.zeros((P, a.shape[1]), np.float32)
        full[:a.shape[0]] = a
        at[name] = (sum(c.shape[1] for c in cols), a.shape[1])
        cols.append(full)

    put("ident", np.eye(P, dtype=np.float32))
    for c in range(2):
        put(f"sel{c}", np.repeat((np.arange(P) % 32 == c).astype(np.float32)[:, None], P, 1))
    put("selcol", np.stack([(np.arange(P) % 32 == c).astype(np.float32) for c in range(2)], 1))
    bsel = np.zeros((12, 12, 32), np.float32)
    for j in range(12):
        bsel[j, j, 0:2] = 1
    put("bias_sel", bsel.reshape(12, -1))
    rows = DEC // GRID_W
    inv = (np.float32(10000.0) ** (-np.arange(ROPE // 4, dtype=np.float32) / np.float32(ROPE // 4))).astype(np.float32)
    row = np.repeat(np.arange(rows), GRID_W).astype(np.float32)
    col = np.tile(np.arange(GRID_W), rows).astype(np.float32)
    ang = np.concatenate([row[:, None] * inv, col[:, None] * inv], -1).astype(np.float32)
    for name, f in (("cos", np.cos), ("sin", np.sin)):
        v = f(ang).astype(np.float32).reshape(NT - 1, P, ROPE // 2).transpose(1, 0, 2)
        put(name, v.reshape(P, -1))
    edge = np.ones((NG, 16), np.float32)
    for g, w in enumerate(WINDOWS):
        for t in range(8):
            edge[g, t] = w / min(w, t + w // 2)
            left = 8 - t
            edge[g, 8 + t] = w / min(w, w // 2 + min(left, w // 2))
    put("edge", np.tile(edge.reshape(1, -1), (P, 1)))
    i = np.arange(P)
    put("before", (i[:, None] < i[None, :]).astype(np.float32))
    put("ones", np.ones((P, P), np.float32))
    put("lower", np.tile((i[:4, None] > i[None, :4]).astype(np.float32).reshape(1, -1), (P, 1)))
    put("row", np.tile(i[None, :].astype(np.float32), (P, 1)))
    put("block", np.tile(np.arange(NBLK, dtype=np.float32)[None], (P, 1)))
    put("kblock", np.tile((np.arange(5) * P).astype(np.float32)[None], (P, 1)))
    put("token", (np.arange(NT)[None] * P + i[:, None]).astype(np.float32))
    put("mhalf", np.full((P, 8), -0.5, np.float32))
    return np.concatenate(cols, 1), at


def step_kernel(nc, x_prompt, x_sample, cache_ckv, cache_krope, c, c_ctx, ada_w, ada_b, norm1_g, norm2_g, w_in, pool_w,
                pool_scale, q_a_norm_g, w_uq, kv_a_norm_g, w_ukv, q_norm_g, k_norm_g, w_out, router_w, router_b,
                w_gate, w_up, w_down, consts, y_prompt, y_sample, new_ckv, new_krope, const_at):
    es = ExitStack()
    with es:
        def sb(name, shape, dt=F32):
            return es.enter_context(nc.sbuf_tensor(name, shape, dt))

        def sem(name):
            return es.enter_context(nc.semaphore(name))

        x = sb("x", [P, NT, D])
        actT = sb("actT", [P, DC, NTOK])
        BIGW = 3 * 6144
        big = sb("big", [P, BIGW])
        low = sb("low", [P, 8960])
        ada_ring = [sb(f"ada_ring{i}", [P, 4, HALF]) for i in range(2)]
        mod = sb("mod", [P, 6144])
        cst = sb("cst", [P, sum(n for _, n in const_at.values())])
        bias_rows = sb("bias_rows", [12, HALF])
        part_s = sb("part_s", [P, HALF])
        gain = sb("gain", [P, D])
        condT = sb("condT", [P, DC, 32])
        gcol = sb("gcol", [P, DC, 2])
        scol = sb("scol", [P, DC, 2])
        gn1 = sb("gn1", [P, DC])
        ctl = sb("ctl", [P, 2], I32)
        pairs = sb("pairs", [P, 1])
        rw = sb("rw", [P, DC, NE])
        rb = sb("rb", [P, NE])
        gq = sb("gq", [P, QH])
        gk = sb("gk", [P, QH])
        pscale = sb("pscale", [P, NG])
        kr = sb("kr", [P, NKT, ROPE])
        krr = sb("krr", [P, NKT, ROPE])
        rope_t = sb("rope_t", [P, 2, ROPE])
        ss = sb("ss", [P, 2 * NT])
        rs = sb("rs", [P, 2 * NT])
        head_ss = sb("head_ss", [P, 2, 2, H])
        head_rs = sb("head_rs", [P, 2, 2, H])
        kr_ss = sb("kr_ss", [P, NKT])
        low_ss = sb("low_ss", [P, NT, 2])
        low_rs = sb("low_rs", [P, NT, 2])
        nmax = sb("nmax", [P, 2])
        mx = sb("mx", [P, 2])
        esum = sb("esum", [P, NU])
        rsum = sb("rsum", [P, H])
        slot_i = sb("slot_i", [P, 2 * NT], U32)
        slot_a = sb("slot_a", [P, 2 * NT], U32)
        slot_b = sb("slot_b", [P, 2 * NT], U32)
        gates2 = sb("gates2", [P, 2 * NT])
        idx = sb("idx", [P, NBLK], U32)
        eid = sb("eid", [P, NBLK], I32)

        def k_(name):
            a, n = const_at[name]
            return cst[:, a:a + n]

        ident = k_("ident")

        def view(t, lo, shape):
            n = int(np.prod(shape))
            v = t[:, lo:lo + n]
            if len(shape) == 2:
                return v.rearrange("p (a b) -> p a b", b=shape[1])
            if len(shape) == 3:
                return v.rearrange("p (a b c) -> p a b c", b=shape[1], c=shape[2])
            return v

        win = view(big, 0, (DC, INW))
        cache_n = view(big, DC * INW, (KVR,))
        ckv_keep = view(big, DC * INW + KVR, (KVR,))
        gqa = view(big, DC * INW + 2 * KVR, (QR,))
        gkva = view(big, DC * INW + 2 * KVR + QR, (KVR,))
        crow = part_s[0:16, 0:P]
        qT = view(big, 0, (H, NTOK))
        kT = view(big, 5120, (H, NKT * P))
        V = view(big, 11264, (NKT, H * VH))
        cqT = view(big, 14336, (QC, NTOK))
        ckvT = view(big, 16256, (KC, NKT * P))
        prob = [view(big, 14336 + 640 * i, (NLK, P)) for i in range(2)]
        probT = [view(big, 15616 + 640 * i, (NLK, P)) for i in range(2)]
        onat = view(big, 16896, (HALF,))
        wgu = [view(big, 6144 * i, (DC, 2 * DE)) for i in range(2)]
        wd = [view(big, 6144 * i + 4096, (2, D)) for i in range(2)]
        xn = [view(big, 12288 + D * i, (D,)) for i in range(2)]
        xg = xn
        xgT = [view(big, 14336 + D * i, (DC, P)) for i in range(2)]
        act_n = [view(big, 16384 + DE * i, (DE,)) for i in range(2)]
        sil = [view(big, 16384 + DE * (2 + i), (DE,)) for i in range(2)]
        acT = [view(part_s, 2 * P * i, (2, P)) for i in range(2)]
        yb = [view(mod, D * i, (D,)) for i in range(2)]
        comb = [view(low, D * i, (D,)) for i in range(8)] + [view(big, 14336 + D * i, (D,)) for i in range(2)]
        rt = 14336
        sel_s = view(big, rt, (NT * EG, GE))
        sig = view(big, rt + 80, (NT * EG, GE))
        cmp4 = view(big, rt + 160, (NT * EG, GE, GE))
        eq4 = view(big, rt + 480, (NT * EG, GE, GE))
        chosen = view(big, rt + 800, (NT * EG, GE))
        rank = view(big, rt + 880, (NT * EG, GE))
        gsc = view(big, rt + 960, (NT, EG))
        gcmp = view(big, rt + 980, (NT, EG, EG))
        geq = view(big, rt + 1060, (NT, EG, EG))
        best = view(big, rt + 1140, (NT, EG))
        mask = view(big, rt + 1160, (NT, NE))
        gts = view(big, rt + 1240, (NT, NE))
        den = view(big, rt + 1320, (NT,))
        hot = view(big, rt + 1330, (2, NT, NE))
        slot1 = view(big, rt + 1490, (NT, NE))
        pick = view(big, rt + 1570, (2, NT))
        nbc = view(big, rt + 1590, (NE, 5))
        nb = view(big, rt + 1670, (NE,))
        endb = view(big, rt + 1690, (NE,))
        start = view(big, rt + 1710, (NE,))
        ecmp = view(big, rt + 1730, (NBLK, NE))
        eidf = view(big, rt + 2146, (NBLK,))
        slot_p = view(big, rt + 2180, (2 * NT,))
        slot_q = view(big, rt + 2190, (2 * NT,))
        onep = view(mod, 0, (2 * NT, P))
        oneb = view(mod, 2 * NT * P, (2 * NT, NBLK))
        prod = view(big, rt + 2520, (2, NT, NE))
        pcmp = view(big, rt + 2680, (NBLK // 2,))
        wuq = view(low, 0, (QC, H * QH))
        wukv = view(low, 2304, (KC, H * (NOPE + VH)))
        pw = view(low, 4352, (NG, P))
        wo = [view(low, 4864, (DC, HALF)), view(low, 0, (DC, HALF))]
        first_w = ada_ring + [view(low, 4 * HALF * i, (4, HALF)) for i in range(4)] + ada_ring
        G = view(mod, 0, (2, D))
        S = view(mod, 2 * D, (2, D))
        gate = view(mod, 4 * D, (2, D))
        u = view(mod, 0, (NG, PW))
        pa = view(mod, NG * PW, (PW,))
        pb = view(mod, (NG + 1) * PW, (PW,))
        qn = view(mod, 4480, (H, QH))
        kn = view(mod, 4480 + H * QH, (H, QH))
        cn = view(mod, 4480, (QR + KVR,))
        sq_x = view(big, 17408, (D,))
        sq_cq, sq_ckv = view(big, 17792, (QR,)), view(big, 17792 + QR, (KVR,))
        flat = actT[:, :, :].rearrange("p a b -> p (a b)")
        sq_q = view(flat, 4 * NTOK, (H, QH))
        sq_k = view(flat, 6 * NTOK, (H, NOPE))
        sq_kr = view(flat, 7 * NTOK, (ROPE,))
        rq = [view(gain, i * H * 16, (H, 16)) for i in range(4)]
        out_s = [view(big, 14336 + HALF * i, (HALF,)) for i in range(4)]

        bank = [es.enter_context(nc.psum_tensor(f"bank{i}", [P, HALF], F32)) for i in range(4, 8)]
        pair = [es.enter_context(nc.psum_tensor(f"pair{i}", [P, 2 * HALF], F32)) for i in range(2)]
        tb4, tb5, o6, a7 = bank

        h2_rows = nc.dram_tensor("h2_rows", [NTOK, D], F32, kind="Internal").ap()
        y_rows = nc.dram_tensor("y_rows", [NSLOT, D], F32, kind="Internal").ap()

        ld_start = sem("ld_start")
        ld_ada = [sem("ld_ada0"), sem("ld_ada1")]
        ld_first = [sem(f"ld_first{a}") for a in range(4)]
        ld_bias = sem("ld_bias")
        ld_gain = sem("ld_gain")
        ld_win = sem("ld_win")
        ld_low = sem("ld_low")
        ld_small = sem("ld_small")
        ld_wo = [sem("ld_wo0"), sem("ld_wo1")]
        ld_gu = [sem("ld_gu0"), sem("ld_gu1")]
        ld_dn = [sem("ld_dn0"), sem("ld_dn1")]
        ld_gn1 = sem("ld_gn1")
        ada_used = sem("ada_used")
        gu_used, dn_used = sem("gu_used"), sem("dn_used")
        moe_done = sem("moe_done")
        win_used = sem("win_used")
        proj_used = sem("proj_used")
        wo_used = sem("wo_used")
        eid_ready = sem("eid_ready")
        layer_go = sem("layer_go")
        y_fill = sem("y_fill")
        stream_go = sem("stream_go")
        x_whole = sem("x_whole")
        out_done = sem("out_done")
        g_in = [sem("g_in0"), sem("g_in1")]
        c_in = [sem(f"c_in{t}") for t in range(NT)]
        first_ada = [sem(f"first_{n}") for n in ("part", "part_s", "bc", "bc_s")]
        cond_t = sem("cond_t")
        cond_s = sem("cond_s")
        start_d = sem("start_d")

        cleared = []

        def lsem(name):
            cleared.append(sem(name))
            return cleared[-1]

        layer_end = lsem("layer_end")
        dv = lsem("dve_chain")
        pl = lsem("pool_chain")
        ac = lsem("act_chain")
        ada_part, ada_part_s, ada_bc, ada_bc_s = (lsem(n) for n in ("ada_part", "ada_part_s", "ada_bc", "ada_bc_s"))
        layer_ada = (ada_part, ada_part_s, ada_bc, ada_bc_s)
        x_sq, x_rs = lsem("x_sq"), lsem("x_rs")
        h_ready, h_t, h_ta, h_td = (lsem(n) for n in ("h_ready", "h_t", "h_ta", "h_td"))
        h_st = [lsem("h_st0"), lsem("h_st1")]
        in_mm, in_act, in_dve = lsem("in_mm"), lsem("in_act"), lsem("in_dve")
        low_sq, low_r, low_t, low_ta, low_td = (lsem(n) for n in ("low_sq", "low_r", "low_t", "low_ta", "low_td"))
        ckv_out = lsem("ckv_out")
        q_mm, kv_mm, q_sq, k_sq, q_ss, k_ss, q_rs, k_rs = (lsem(n) for n in ("q_mm", "kv_mm", "q_sq", "k_sq", "q_ss",
                                                                            "k_ss", "q_rs", "k_rs"))
        v_cp, q_n, k_n, q_rd, k_rd = (lsem(n) for n in ("v_cp", "q_n", "k_n", "q_rd", "k_rd"))
        qk_t, qk_ta, qk_td = lsem("qk_t"), lsem("qk_ta"), lsem("qk_td")
        krr_s = lsem("krr_s")
        keep_s, keep_out = lsem("keep_s"), lsem("keep_out")
        pool_z, pool_d, pool_mm, pool_ea, pool_ed = (lsem(n) for n in ("pool_z", "pool_d", "pool_mm", "pool_ea",
                                                                        "pool_ed"))
        s_sc, s_mx, s_exp, s_pt, s_pta, s_ptb, s_pv, s_on, s_ot, s_otc = (lsem(n) for n in (
            "s_sc", "s_mx", "s_exp", "s_pt", "s_pta", "s_ptb", "s_pv", "s_on", "s_ot", "s_otc"))
        op_mm, op_g, op_x = lsem("op_mm"), lsem("op_g"), lsem("op_x")
        r_mm, r_e, r_mask, r_tot, r_one, r_pe1, r_idx, r_ctl, y_done = (lsem(n) for n in (
            "r_mm", "r_e", "r_mask", "r_tot", "r_one", "r_pe1", "r_idx", "r_ctl", "y_done"))
        b_t, b_ta, b_td, b_sil, b_act, b_at, b_atc, b_ya, b_yd = (lsem(n) for n in (
            "b_t", "b_ta", "b_td", "b_sil", "b_act", "b_at", "b_atc", "b_ya", "b_yd"))
        b_st = [lsem("b_st0"), lsem("b_st1")]
        c_hi, c_gt, c_x = lsem("c_hi"), lsem("c_gt"), lsem("c_x")

        ctx_of = lambda t: 0 if t == 0 else 1
        key_tile = lambda t: CTX if t == 0 else t
        KV_ORDER = [key_tile(t) for t in range(NT)] + [0]

        G_ORDER = list(reversed(range(NG)))

        block = es.enter_context(nc.Block())

        @block.sync
        def _(sp):
            sp.dma_start(cst[:, :], consts).then_inc(ld_start, 16)
            sp.dma_start(crow[0:8], c_ctx.rearrange("(k p) -> k p", p=P)).then_inc(ld_start, 16)
            sp.dma_start(crow[8:16], c.rearrange("b (k p) -> (b k) p", p=P)).then_inc(ld_start, 16)
            sp.dma_start(x[:, 0, :], x_prompt[0]).then_inc(ld_start, 16)
            sp.dma_start(x[:, 1:NT, :], x_sample[0].rearrange("(t p) d -> p t d", p=P)).then_inc(ld_start, 16)
            sp.dma_start(rw[:, :, :], router_w.rearrange("(k p) e -> p k e", p=P)).then_inc(ld_start, 16)
            sp.dma_start(rb[:, :], router_b.rearrange("(a e) -> a e", a=1).broadcast_to([P, NE])).then_inc(ld_start, 16)
            sp.dma_start(bias_rows[0:4, :], ada_b[0, 0:2 * D].rearrange("(j n) -> j n", n=HALF)).then_inc(ld_bias, 16)
            sp.dma_start(gn1[:, :], norm1_g[0].rearrange("(k p) -> p k", p=P), allow_slow_non_contiguous=True)\
              .then_inc(ld_gn1, 16)

            def load_quarter(layer, a, kh, dst, count):
                src = ada_w[layer, kh * HALF:(kh + 1) * HALF, a * HALF:(a + 1) * HALF]
                sp.dma_start(dst[:, :, :], src.rearrange("(k p) n -> p k n", p=P)).then_inc(count, 16)

            for q in range(8):
                if q >= 6:
                    sp.wait_ge(ada_used, q - 5)
                load_quarter(0, q // 2, q % 2, first_w[q], ld_first[q // 2])
            with sp.Fori(0, DEPTH) as l:
                nxt = (l + 1) % DEPTH

                def load_ada(p):
                    for q in range(4 * p, 4 * p + 4):
                        sp.wait_ge(ada_used, l * (4 * NPIECE) + (8 + q - 1))
                        load_quarter(nxt if p < 2 else l, q // 2, q % 2, ada_ring[q % 2], ld_ada[q % 2])

                sp.wait_ge(wo_used, l + 1)
                for dst, src in ((gq, q_norm_g), (gk, k_norm_g)):
                    sp.dma_start(dst[:, :], src[l].rearrange("(a n) -> a n", a=1).broadcast_to([P, dst.shape[1]]))\
                      .then_inc(ld_small, 16)
                sp.dma_start(pscale[:, :], pool_scale[l].rearrange("(g p) -> p g", p=P),
                             allow_slow_non_contiguous=True).then_inc(ld_small, 16)
                sp.dma_start(kr[:, 0, :], cache_krope[0, l]).then_inc(ld_small, 16)
                sp.wait_ge(moe_done, l + 1)
                sp.dma_start(cache_n, cache_ckv[0, l]).then_inc(ld_small, 16)
                for dst, src in ((gqa, q_a_norm_g), (gkva, kv_a_norm_g)):
                    sp.dma_start(dst, src[l].rearrange("(a n) -> a n", a=1).broadcast_to([P, dst.shape[1]]))\
                      .then_inc(ld_small, 16)
                sp.dma_start(win[:, :, :], w_in[l].rearrange("(k p) n -> p k n", p=P)).then_inc(ld_win, 16)
                sp.wait_ge(x_whole, l + 1)
                sp.dma_start(wuq[:, :, :], w_uq[l].rearrange("(k p) n -> p k n", p=P)).then_inc(ld_low, 16)
                sp.dma_start(wukv[:, :, :], w_ukv[l].rearrange("(k p) n -> p k n", p=P)).then_inc(ld_low, 16)
                sp.dma_start(pw[:, :, :], pool_w[l].rearrange("g p n -> p g n")).then_inc(ld_low, 16)
                sp.wait_ge(first_ada[3], 4)
                sp.dma_start(bias_rows[0:4, :], ada_b[nxt, 0:2 * D].rearrange("(j n) -> j n", n=HALF))\
                  .then_inc(ld_bias, 16)
                sp.dma_start(bias_rows[4:12, :], ada_b[l, 2 * D:6 * D].rearrange("(j n) -> j n", n=HALF))\
                  .then_inc(ld_bias, 16)
                sp.dma_start(gn1[:, :], norm1_g[nxt].rearrange("(k p) -> p k", p=P), allow_slow_non_contiguous=True)\
                  .then_inc(ld_gn1, 16)
                load_ada(0)
                load_ada(1)
                sp.dma_start(wo[0][:, :, :], w_out[l, :, 0:HALF].rearrange("(k p) n -> p k n", p=P))\
                  .then_inc(ld_wo[0], 16)
                load_ada(2)
                sp.wait_ge(proj_used, l + 1)
                sp.dma_start(gain[:, :], norm2_g[l].rearrange("(a n) -> a n", a=1).broadcast_to([P, D]))\
                  .then_inc(ld_gain, 16)
                load_ada(3)
                sp.dma_start(wo[1][:, :, :], w_out[l, :, HALF:D].rearrange("(k p) n -> p k n", p=P))\
                  .then_inc(ld_wo[1], 16)
                load_ada(4)
                load_ada(5)
                sp.wait_ge(eid_ready, l + 1)
                sp.sem_inc(stream_go, 1)
                n_pairs = sp.value_load(ctl[0:1, 0:1], min_val=NBLK_MIN // 2, max_val=NBLK // 2)
                before = sp.value_load(ctl[0:1, 1:2], min_val=0, max_val=DEPTH * NBLK // 2)
                with sp.Fori(0, n_pairs) as i:
                    es_ = []
                    for s in range(2):
                        sp.wait_ge(gu_used, (before + i) * 2 + (s + 1))
                        e = sp.value_load(eid[0:1, bass.ds(i * 2 + s, 1)], min_val=0, max_val=NE - 1)
                        es_.append(e)
                        sp.dma_start(wgu[s][:, :, 0:DE], w_gate[l, e].rearrange("(k p) n -> p k n", p=P))\
                          .then_inc(ld_gu[s], 16)
                        sp.dma_start(wgu[s][:, :, DE:2 * DE], w_up[l, e].rearrange("(k p) n -> p k n", p=P))\
                          .then_inc(ld_gu[s], 16)
                    for s in range(2):
                        sp.wait_ge(g_in[s], (before + i) * 16 + 16)
                        sp.wait_ge(dn_used, (before + i) * 2 + (s + 1))
                        sp.dma_start(wd[s][:, :, :], w_down[l, es_[s]].rearrange("(k p) n -> p k n", p=P))\
                          .then_inc(ld_dn[s], 16)
            sp.wait_ge(layer_go, DEPTH)
            sp.dma_start(y_prompt[0], x[:, 0, :]).then_inc(out_done, 16)
            sp.dma_start(y_sample[0].rearrange("(t p) d -> p t d", p=P), x[:, 1:NT, :]).then_inc(out_done, 16)
            sp.wait_ge(out_done, (DEPTH + 2) * 16)

        @block.tensor
        def _(pe):
            mm, tr = nc.tensor.matmul, nc.tensor.transpose
            pe.sem_inc(gu_used, 2)
            pe.sem_inc(dn_used, 2)
            pe.sem_inc(moe_done, 1)
            pe.sem_inc(wo_used, 1)
            pe.wait_ge(ld_start, 16 * 7)
            tr(a7[:, 0:16], crow, ident[0:16, 0:16]).then_inc(cond_t, 1)
            pe.wait_ge(cond_s, 1)
            pe.wait_ge(ld_bias, 16)

            def ada_sums(a, step, counts, w):
                for k in range(4):
                    m = mm(a7[32 * k:32 * k + 32, :], condT[:, 4 * step + k, :], w[:, k, :],
                           start=(step == 0), stop=(step == 1 and k > 0), tile_position=(0, 32 * k),
                           skip_group_check=True)
                m.then_inc(ada_used, 1)
                if step == 1:
                    mm(a7[0:32, :], k_("bias_sel")[0:12, 32 * a:32 * a + 32] if counts is layer_ada else
                       k_("bias_sel")[0:4, 32 * a:32 * a + 32],
                       bias_rows[:, :] if counts is layer_ada else bias_rows[0:4, :], start=False, stop=True,
                       skip_group_check=True).then_inc(counts[0], 1)

            def ada_columns(a, counts):
                pe.wait_ge(counts[1], a + 1)
                for k in range(4):
                    m = mm(a7[:, 2 * k:2 * k + 2], part_s[:, k * P:(k + 1) * P], k_("selcol"), start=True, stop=True)
                m.then_inc(counts[2], 1)

            for a in range(4):
                for step in range(2):
                    if step == 0:
                        pe.wait_ge(ld_first[a], 32)
                    if step == 0 and a > 0:
                        pe.wait_ge(first_ada[3], a)
                    ada_sums(a, step, first_ada, first_w[2 * a + step])
                ada_columns(a, first_ada)
            pe.wait_ge(first_ada[3], 4)
            with pe.Fori(0, DEPTH) as l:
                def ada_step(a, step):
                    if step < 2:
                        pe.wait_ge(ld_ada[step], (l * (2 * NPIECE) + (a + 1)) * 16)
                        if step == 0:
                            if a == 0:
                                pe.wait_ge(low_td, NT + 1)
                                pe.wait_ge(ld_bias, (l + 1) * 32 + 16)
                            else:
                                pe.wait_ge(ada_bc_s, BC_BEFORE[min(a, 10)])
                                pe.wait_ge(ada_part_s, a)
                        ada_sums(a, step, layer_ada, ada_ring[step])
                    elif a < 4:
                        ada_columns(a, layer_ada)
                    else:
                        ada_rows_out(a, step - 2, part_s[:, :])

                def ada_rows_out(a, cnd, rows):
                    pe.wait_ge(ada_part_s, a + 1)
                    pe.wait_ge(ada_bc_s, BC_BEFORE[a] + cnd)
                    mm(a7[:, :], k_(f"sel{cnd}"), rows, start=True, stop=True).then_inc(ada_bc, 1)

                def turn_h(t, first):
                    j = first + t
                    pe.wait_ge(h_ready, j + 1)
                    if j > 0:
                        pe.wait_ge(h_ta, j)
                        pe.wait_ge(h_td, j)
                    for k in range(DC):
                        dst = (tb4, tb5)[k // 4]
                        m = tr(dst[:, (k % 4) * P:(k % 4 + 1) * P], xn[t % 2][:, k * P:(k + 1) * P], ident)
                    m.then_inc(h_t, 1)

                def in_proj(t):
                    pe.wait_ge(h_ta, t + 1)
                    pe.wait_ge(h_td, t + 1)
                    if t == 0:
                        pe.wait_ge(ld_win, (l + 1) * 16)
                    if t >= 2:
                        pe.wait_ge(in_act, t - 1)
                        pe.wait_ge(in_dve, t - 1)
                    for lo, n, at in ((POOLW, QR, 0), (POOLW + QR, KVR + ROPE, HALF)):
                        for k in range(DC):
                            m = mm(pair[t % 2][:, at:at + n], actT[:, k, t * P:(t + 1) * P], win[:, k, lo:lo + n],
                                   start=(k == 0), stop=(k == DC - 1))
                    m.then_inc(in_mm, 1)

                def turn_low(j):
                    if j < NT:
                        pe.wait_ge(in_dve, j + 1)
                    else:
                        pe.wait_ge(ld_small, (l + 1) * (7 * 16))
                    if j > 0:
                        pe.wait_ge(low_ta, min(j, NT))
                        pe.wait_ge(low_td, j)
                    if j < NT:
                        for k in range(QC):
                            m = tr(o6[:, k * P:(k + 1) * P], cn[:, k * P:(k + 1) * P], ident)
                    for k in range(KC):
                        src = cn[:, QR + k * P:QR + (k + 1) * P] if j < NT else cache_n[:, k * P:(k + 1) * P]
                        m = tr(a7[:, k * P:(k + 1) * P], src, ident)
                    m.then_inc(low_t, 1)

                turn_h(0, 0)
                for t in range(NT):
                    if t + 1 < NT:
                        turn_h(t + 1, 0)
                    in_proj(t)
                    if t > 0:
                        turn_low(t - 1)
                for n, g in enumerate(G_ORDER):
                    j = NT + n
                    pe.wait_ge(in_act, j - 1)
                    pe.wait_ge(in_dve, j - 1)
                    for at, t0, cols in ((0, P, DEC), (HALF, 0, P)):
                        for k in range(DC):
                            m = mm(pair[j % 2][:, at:at + cols], win[:, k, g * P:(g + 1) * P], actT[:, k, t0:t0 + cols],
                                   start=(k == 0), stop=(k == DC - 1))
                    m.then_inc(in_mm, 1)
                    if n == 0:
                        turn_low(NT - 1)
                    if n == 1:
                        turn_low(NT)
                pe.wait_ge(in_act, NT + NG)
                pe.wait_ge(in_dve, NT + NG)

                pe.wait_ge(ld_low, (l + 1) * 48)

                def q_proj(t):
                    pe.wait_ge(low_ta, t + 1)
                    if t > 0:
                        pe.wait_ge(q_sq, t)
                        pe.wait_ge(q_rd, t)
                    for n in range(2):
                        for k in range(QC):
                            m = mm(pair[0][:, n * HALF:n * HALF + 4 * QH], cqT[:, k, t * P:(t + 1) * P],
                                   wuq[:, k, n * 4 * QH:(n + 1) * 4 * QH], start=(k == 0), stop=(k == QC - 1))
                    m.then_inc(q_mm, 1)

                def kv_proj(j):
                    kt = KV_ORDER[j]
                    pe.wait_ge(low_td, j + 1)
                    if j > 0:
                        pe.wait_ge(k_sq, j)
                        pe.wait_ge(v_cp, j)
                        pe.wait_ge(k_rd, j)
                    for n in range(2):
                        for k in range(KC):
                            m = mm(pair[1][:, n * HALF:(n + 1) * HALF], ckvT[:, k, kt * P:(kt + 1) * P],
                                   wukv[:, k, n * HALF:(n + 1) * HALF], start=(k == 0), stop=(k == KC - 1))
                    m.then_inc(kv_mm, 1)

                def turn_heads(src, job):
                    if job > 0:
                        pe.wait_ge(qk_ta, job)
                        pe.wait_ge(qk_td, job)
                    else:
                        pe.wait_ge(h_ta, NT)
                        pe.wait_ge(h_td, NT)
                    for h in range(H):
                        dst = (tb4, tb5)[h // 4]
                        m = tr(dst[0:QH, (h % 4) * P:(h % 4 + 1) * P], src[:, h, :], ident)
                    m.then_inc(qk_t, 1)

                q_proj(0)
                kv_proj(0)
                for j in range(NT + 1):
                    if j < NT:
                        pe.wait_ge(q_n, j + 1)
                        turn_heads(qn, 2 * j)
                        if j + 1 < NT:
                            q_proj(j + 1)
                    pe.wait_ge(k_n, j + 1)
                    turn_heads(kn, 2 * j + 1 if j < NT else 2 * NT)
                    if j + 1 <= NT:
                        kv_proj(j + 1)
                    for st in COL_STEPS[2 * j:2 * j + 2]:
                        ada_step(*st)
                for g in range(NG):
                    if g == 0:
                        pe.wait_ge(pool_d, NG)
                        pe.wait_ge(k_rd, NT + 1)
                        pe.wait_ge(v_cp, NT + 1)
                        pe.wait_ge(k_sq, NT + 1)
                    if g >= 2:
                        pe.wait_ge(pool_ea, g - 1)
                        pe.wait_ge(pool_ed, g - 1)
                    mm(pair[g % 2][:, 0:DEC], pw[:, g, :], u[:, g, LAT0:LAT0 + DEC], start=True, stop=True)
                    mm(pair[g % 2][:, HALF:HALF + SEQ], pw[:, g, :], u[:, g, CTX0:CTX0 + SEQ], start=True, stop=True)\
                        .then_inc(pool_mm, 1)
                pe.wait_ge(pool_mm, NG)
                pe.sem_inc(proj_used, 1)

                def scores(un):
                    t, h = UNITS[un]
                    if un < 2:
                        if un == 0:
                            pe.wait_ge(qk_ta, 2 * NT + 1)
                            pe.wait_ge(qk_td, 2 * NT + 1)
                        pe.wait_ge(pool_ea, NG - 1 + un)
                        pe.wait_ge(pool_ed, NG - 1 + un)
                    else:
                        pe.wait_ge(s_exp, un - 1)
                    q = qT[0:QH, h, t * P:(t + 1) * P]
                    dst = pair[un % 2]
                    if t == 0:
                        m = mm(dst[:, 0:P], q, kT[0:QH, h, CTX * P:NKT * P], start=True, stop=True)
                    else:
                        mm(dst[:, 0:HALF], q, kT[0:QH, h, 0:HALF], start=True, stop=True)
                        m = mm(dst[:, HALF:NLK * P], q, kT[0:QH, h, HALF:NLK * P], start=True, stop=True)
                    m.then_inc(s_sc, 1)

                def turn_prob(un):
                    t, h = UNITS[un]
                    pe.wait_ge(s_exp, un + 1)
                    if un > 0:
                        pe.wait_ge(s_pta, un)
                        pe.wait_ge(s_ptb, un)
                    for k in range(1 if t == 0 else NLK):
                        dst = tb4[:, k * P:(k + 1) * P] if k < 3 else tb5[:, (k - 3) * P:(k - 2) * P]
                        m = tr(dst, prob[un % 2][:, k, :], ident)
                    m.then_inc(s_pt, 1)

                def weigh(un):
                    t, h = UNITS[un]
                    pe.wait_ge(s_pta, un + 1)
                    pe.wait_ge(s_ptb, un + 1)
                    if h == 0 and t > 0:
                        pe.wait_ge(s_on, t)
                    tiles = [CTX] if t == 0 else list(range(NLK))
                    for k, kt in enumerate(tiles):
                        m = mm(o6[:, h * VH:(h + 1) * VH], probT[un % 2][:, k, :], V[:, kt, h * VH:(h + 1) * VH],
                               start=(k == 0), stop=(k == len(tiles) - 1))
                    m.then_inc(s_pv, 1)

                def turn_out(t):
                    pe.wait_ge(s_on, t + 1)
                    pe.wait_ge(s_pta, min(NU, (t + 1) * H + 1))
                    for k in range(4):
                        m = tr(tb4[:, k * P:(k + 1) * P], onat[:, k * P:(k + 1) * P], ident)
                    m.then_inc(s_ot, 1)
                    pe.wait_ge(s_otc, t + 1)

                scores(0)
                for un in range(NU + 2):
                    if un + 1 < NU:
                        scores(un + 1)
                    if 1 <= un <= NU:
                        weigh(un - 1)
                    if un >= H + 1 and (un - 1) % H == 0:
                        turn_out((un - 1) // H - 1)
                    if un < NU:
                        turn_prob(un)
                    if un in ADA_AT:
                        ada_step(*ADA_AT[un])
                pe.wait_ge(s_otc, NT)

                def route(t):
                    pe.wait_ge(h_ta, NT + t + 1)
                    pe.wait_ge(h_td, NT + t + 1)
                    for k in range(DC):
                        m = mm(o6[:, t * NE:(t + 1) * NE], actT[:, k, t * P:(t + 1) * P], rw[:, k, :],
                               start=(k == 0), stop=(k == DC - 1))
                    return m

                for n in range(2):
                    pe.wait_ge(ld_wo[n], (l + 1) * 16)
                    for t in range(NT):
                        j = n * NT + t
                        if j >= 4:
                            pe.wait_ge(op_g, j - 3)
                        dst = pair[(j % 4) // 2][:, (j % 2) * HALF:(j % 2 + 1) * HALF]
                        for k in range(DC):
                            m = mm(dst, actT[:, k, t * P:(t + 1) * P], wo[n][:, k, :], start=(k == 0),
                                   stop=(k == DC - 1))
                        m.then_inc(op_mm, 1)
                        if n == 1 and t >= 1:
                            turn_h(t - 1, NT)
                        if n == 1 and t >= 2:
                            route(t - 2)
                pe.wait_ge(op_mm, 2 * NT)
                pe.sem_inc(wo_used, 1)
                route(NT - 2)
                turn_h(NT - 1, NT)
                route(NT - 1).then_inc(r_mm, 1)
                for cnd in range(2):
                    ada_rows_out(10, cnd, gain[:, 0:HALF])
                pe.wait_ge(r_mask, 1)
                pe.wait_ge(op_g, 2 * NT)
                pos = pair[0][:, 0:(NT + 1) * NE].rearrange("p (t e) -> p t e", e=NE)
                mm(pos[:, 0:NT, :], k_("before"), mask, start=True, stop=False, skip_group_check=True)
                for i in range(NT):
                    after = NT - i
                    m = mm(pos[:, i + 1:i + 1 + after, :], k_("ones"),
                           mask[:, i, :].unsqueeze(1).broadcast_to([P, after, NE]), start=False, stop=(i == NT - 1),
                           skip_group_check=True)
                m.then_inc(r_tot, 1)
                for cnd in range(2):
                    ada_rows_out(11, cnd, gain[:, HALF:D])
                pe.wait_ge(r_one, 1)
                for j in range(2 * NT):
                    m = mm(pair[1][:, 0:NBLK], onep[:, j, :], oneb[:, j, :], start=(j == 0), stop=(j == 2 * NT - 1))
                m.then_inc(r_pe1, 1)

                pe.sem_inc(b_at, 2)
                pe.wait_ge(r_ctl, 1)
                n_pairs = pe.value_load(ctl[0:1, 0:1], min_val=NBLK_MIN // 2, max_val=NBLK // 2)
                before = pe.value_load(ctl[0:1, 1:2], min_val=0, max_val=DEPTH * NBLK // 2)
                pe.wait_ge(ada_bc_s, 20)
                with pe.Fori(0, n_pairs) as i:
                    for s in range(2):
                        b = i * 2 + s
                        pe.wait_ge(g_in[s], (before + i) * 16 + 16)
                        if s == 0:
                            pe.wait_ge(b_ta, b + 1)
                            pe.wait_ge(b_td, b + 1)
                        else:
                            pe.wait_ge(b_atc, b)
                        for k in range(DC):
                            dst = pair[0][:, k * P:(k + 1) * P] if s == 0 else (o6, a7)[k // 4][:, k % 4 * P:(k % 4 + 1) * P]
                            m = tr(dst, xg[s][:, k * P:(k + 1) * P], ident)
                        m.then_inc(b_t, 1)

                    def gate_up(s, ks):
                        for k in ks:
                            m = mm((tb4, tb5)[s][:, :], xgT[s][:, k, :], wgu[s][:, k, :], start=(k == 0),
                                   stop=(k == DC - 1))
                        return m

                    def turn_act(s):
                        pe.wait_ge(b_act, i * 2 + (s + 3))
                        for k in range(2):
                            m = tr((o6, a7)[s][:, k * P:(k + 1) * P], act_n[s][:, k * P:(k + 1) * P], ident)
                        m.then_inc(b_at, 1)

                    def down(s):
                        pe.wait_ge(b_atc, i * 2 + (s + 2))
                        pe.wait_ge(ld_dn[s], (before + i) * 16 + 16)
                        for n in range(2):
                            dst = pair[1][:, n * HALF:(n + 1) * HALF] if s == 0 else (tb4, tb5)[n][:, :]
                            for k in range(2):
                                m = mm(dst, acT[s][:, k, :], wd[s][:, k, n * HALF:(n + 1) * HALF], start=(k == 0),
                                       stop=(k == 1))
                        m.then_inc(dn_used, 1)

                    for s in range(2):
                        b = i * 2 + s
                        pe.wait_ge(b_ta, b + 2)
                        pe.wait_ge(b_td, b + 2)
                        pe.wait_ge(ld_gu[s], (before + i) * 32 + 32)
                        if s == 0:
                            pe.wait_ge(b_ya, i * 2 + 1)
                            pe.wait_ge(b_yd, i * 2 + 1)
                            gate_up(0, range(DC)).then_inc(gu_used, 1)
                        else:
                            gate_up(1, range(DC // 2))
                            turn_act(0)
                            gate_up(1, range(DC // 2, DC)).then_inc(gu_used, 1)
                    down(0)
                    turn_act(1)
                    down(1)
                pe.wait_ge(dn_used, (before + n_pairs) * 2 + 2)
                pe.sem_inc(moe_done, 1)
                pe.sem_inc(layer_end, 1)
                pe.wait_ge(layer_go, l + 1)

        @block.scalar
        def _(act):
            f = nc.scalar.activation
            act.wait_ge(cond_t, 1)
            act.wait_ge(start_d, 1)
            act.wait_ge(ld_start, 16 * 7)
            f(condT[:, :, 0:2], a7[:, 0:16].rearrange("p (c k) -> p k c", k=DC), ACT.Silu).then_inc(cond_s, 1)
            for a in range(4):
                act.wait_ge(first_ada[0], a + 1)
                if a > 0:
                    act.wait_ge(first_ada[2], a)
                f(part_s[:, :], a7[:, :], ACT.Copy).then_inc(first_ada[1], 1)
            for b in range(NBLK_MIN, NBLK, NT):
                n = min(NT, NBLK - b)
                act.dma_start(y_rows[b * P:(b + n) * P, :].rearrange("(t p) d -> p t d", p=P), x[:, 0:n, :])\
                    .then_inc(y_fill, 16)
            with act.Fori(0, DEPTH) as l:
                def ada_rows(a):
                    act.wait_ge(ada_part, a + 1)
                    if a > 0:
                        act.wait_ge(ada_bc, BC_BEFORE[min(a, 10)])
                    f(part_s[:, :] if a < 10 else gain[:, (a - 10) * HALF:(a - 9) * HALF], a7[:, :], ACT.Copy)\
                        .then_inc(ada_part_s, 1)

                def evac_h(t, first):
                    act.wait_ge(h_t, first + t + 1)
                    cols, src = slice(t * P, (t + 1) * P), tb4[:, :].rearrange("p (k n) -> p k n", n=P)
                    if first:
                        f(actT[:, 0:4, cols], src, ACT.Copy).then_inc(h_ta, 1)
                        return
                    c2 = ctx_of(t)
                    for k in range(4):
                        m = f(actT[:, k, cols], src[:, k, :], ACT.Identity, scale=gcol[:, k, c2:c2 + 1],
                              bias=scol[:, k, c2:c2 + 1])
                    m.then_inc(h_ta, 1)

                for t in range(NT):
                    if t > 0:
                        act.wait_ge(x_sq, t)
                    f(sq_x, x[:, t, :], ACT.Square, accum_out=ss[:, t:t + 1]).then_inc(x_sq, 1)
                act.wait_ge(first_ada[3], 4)

                def low_squares(t):
                    act.wait_ge(in_mm, t + 1)
                    if t > 0:
                        act.wait_ge(low_sq, t)
                    src = pair[t % 2]
                    f(sq_cq, src[:, 0:QR], ACT.Square, accum_out=low_ss[:, t, 0:1])
                    f(sq_ckv, src[:, HALF:HALF + KVR], ACT.Square, accum_out=low_ss[:, t, 1:2]).then_inc(low_sq, 1)
                    f(kr[:, key_tile(t), :], src[:, HALF + KVR:HALF + KVR + ROPE], ACT.Copy).then_inc(in_act, 1)

                def evac_cq(t):
                    act.wait_ge(low_t, t + 1)
                    f(cqT[:, :, t * P:(t + 1) * P], o6[:, 0:QR].rearrange("p (k n) -> p k n", n=P), ACT.Copy)\
                        .then_inc(low_ta, 1)

                evac_h(0, 0)
                for t in range(NT):
                    if t + 1 < NT:
                        evac_h(t + 1, 0)
                    low_squares(t)
                    if t == 0:
                        act.wait_ge(in_act, 1)
                        act.dma_start(new_krope[0, l], kr[:, CTX, :]).then_inc(out_done, 16)
                    if t > 0:
                        evac_cq(t - 1)
                    if t == 1:
                        act.wait_ge(keep_s, 1)
                        act.dma_start(new_ckv[0, l], ckv_keep).then_inc(keep_out, 16)
                for n, g in enumerate(G_ORDER):
                    j = NT + n
                    act.wait_ge(in_mm, j + 1)
                    f(u[:, g, LAT0:LAT0 + DEC], pair[j % 2][:, 0:DEC], ACT.Copy).then_inc(in_act, 1)
                    if n == 0:
                        evac_cq(NT - 1)

                def q_squares(t):
                    act.wait_ge(q_mm, t + 1)
                    if t > 0:
                        act.wait_ge(q_ss, t)
                    for n in range(2):
                        m = f(sq_q[:, 4 * n:4 * n + 4, :],
                              pair[0][:, n * HALF:n * HALF + 4 * QH].rearrange("p (h d) -> p h d", d=QH), ACT.Square)
                    m.then_inc(q_sq, 1)

                def kv_read(j):
                    kt = KV_ORDER[j]
                    act.wait_ge(kv_mm, j + 1)
                    if j > 0:
                        act.wait_ge(k_ss, j)
                    f(sq_kr, kr[:, kt, :], ACT.Square, accum_out=kr_ss[:, kt:kt + 1])
                    for n in range(2):
                        m = f(sq_k[:, 4 * n:4 * n + 4, :],
                              pair[1][:, n * HALF:(n + 1) * HALF].rearrange("p (h d) -> p h d", d=P)[:, :, 0:NOPE],
                              ACT.Square)
                    m.then_inc(k_sq, 1)
                    for n in range(2):
                        m = f(V[:, kt, n * 256:(n + 1) * 256].rearrange("p (h d) -> p h d", d=VH),
                              pair[1][:, n * HALF:(n + 1) * HALF].rearrange("p (h d) -> p h d", d=P)[:, :, NOPE:P],
                              ACT.Copy)
                    m.then_inc(v_cp, 1)

                def evac_heads(dst, tile, job):
                    act.wait_ge(qk_t, job + 1)
                    f(dst[0:QH, 0:4, tile * P:(tile + 1) * P], tb4[0:QH, :].rearrange("p (k n) -> p k n", n=P),
                      ACT.Copy).then_inc(qk_ta, 1)

                act.wait_ge(ld_small, (l + 1) * (7 * 16))
                act.wait_ge(keep_out, 16)
                q_squares(0)
                kv_read(0)
                for j in range(NT + 1):
                    if j < NT:
                        evac_heads(qT, j, 2 * j)
                        if j + 1 < NT:
                            q_squares(j + 1)
                    evac_heads(kT, KV_ORDER[j], 2 * j + 1 if j < NT else 2 * NT)
                    if j + 1 <= NT:
                        kv_read(j + 1)
                    for a, step in COL_STEPS[2 * j:2 * j + 2]:
                        if step == 1:
                            ada_rows(a)
                for g in range(NG):
                    act.wait_ge(pool_mm, g + 1)
                    f(actT[:, g, P:NTOK], pair[g % 2][:, 0:DEC], ACT.Copy, scale=pscale[:, g:g + 1])\
                        .then_inc(pool_ea, 1)

                def exps(un):
                    t, _ = UNITS[un]
                    n = 1 if t == 0 else NLK
                    act.wait_ge(s_mx, un + 1)
                    if un >= 2:
                        act.wait_ge(s_pt, un - 1)
                    f(prob[un % 2][:, 0:n, :], pair[un % 2][:, 0:n * P].rearrange("p (k n) -> p k n", n=P), ACT.Exp,
                      bias=nmax[:, un % 2:un % 2 + 1], scale=SCALE, accum_out=esum[:, un:un + 1]).then_inc(s_exp, 1)

                for un in range(NU + 2):
                    if un < NU:
                        exps(un)
                    if un >= H + 1 and (un - 1) % H == 0:
                        t = (un - 1) // H - 1
                        act.wait_ge(s_ot, t + 1)
                        f(actT[:, 4:8, t * P:(t + 1) * P], tb4[:, :].rearrange("p (k n) -> p k n", n=P), ACT.Copy)\
                            .then_inc(s_otc, 1)
                    if un < NU:
                        n = 1 if UNITS[un][0] == 0 else 3
                        act.wait_ge(s_pt, un + 1)
                        if un >= 2:
                            act.wait_ge(s_pv, un - 1)
                        f(probT[un % 2][:, 0:n, :], tb4[:, 0:n * P].rearrange("p (k n) -> p k n", n=P), ACT.Copy)\
                            .then_inc(s_pta, 1)
                    if un in ADA_AT and ADA_AT[un][1] == 1:
                        ada_rows(ADA_AT[un][0])

                for t in range(NT + 1):
                    if t > 0:
                        act.wait_ge(h_ready, NT + t)
                        act.dma_start(h2_rows[(t - 1) * P:t * P, :], xn[(t - 1) % 2]).then_inc(h_st[(t - 1) % 2], 16)
                        evac_h(t - 1, NT)
                    if t < NT:
                        act.wait_ge(op_x, NT + t + 1)
                        act.wait_ge(x_sq, NT + t)
                        f(sq_x, x[:, t, :], ACT.Square, accum_out=ss[:, NT + t:NT + t + 1]).then_inc(x_sq, 1)
                act.wait_ge(r_mm, 1)
                f(sig, o6[:, 0:NT * NE].rearrange("p (a b) -> p a b", b=GE), ACT.Exp, scale=-1.0).then_inc(r_e, 1)
                for n in range(2):
                    for cnd in range(2):
                        act.wait_ge(ada_bc, BC_BEFORE[10 + n] + cnd + 1)
                        f(gate[:, cnd, n * HALF:(n + 1) * HALF], a7[:, :], ACT.Copy).then_inc(ada_bc_s, 1)

                act.wait_ge(r_ctl, 1)
                act.wait_ge(ada_bc, 20)
                n_pairs = act.value_load(ctl[0:1, 0:1], min_val=NBLK_MIN // 2, max_val=NBLK // 2)
                before = act.value_load(ctl[0:1, 1:2], min_val=0, max_val=DEPTH * NBLK // 2)
                for count, n in ((b_ta, 1), (b_atc, 1), (b_ya, 1), (b_st[0], 16), (b_st[1], 16)):
                    act.sem_inc(count, n)
                with act.Fori(0, n_pairs) as i:
                    for s in range(2):
                        b = i * 2 + s
                        act.wait_ge(b_t, b + 1)
                        src = pair[0][:, 0:HALF] if s == 0 else o6[:, :]
                        f(xgT[s][:, 0:4, :], src.rearrange("p (k n) -> p k n", n=P), ACT.Copy).then_inc(b_ta, 1)
                    for s in range(2):
                        act.wait_ge(gu_used, (before + i) * 2 + (s + 3))
                        f(sil[s], (tb4, tb5)[s][:, 0:DE], ACT.Silu).then_inc(b_sil, 1)
                        act.wait_ge(b_at, i * 2 + (s + 3))
                        f(acT[s][:, :, :], (o6, a7)[s][:, 0:2 * P].rearrange("p (k n) -> p k n", n=P), ACT.Copy)\
                            .then_inc(b_atc, 1)
                    for s in range(2):
                        b = i * 2 + s
                        act.wait_ge(dn_used, (before + i) * 2 + (s + 3))
                        act.wait_ge(b_st[s], i * 16 + 16)
                        f(yb[s][:, 0:HALF], (pair[1][:, 0:HALF], tb4[:, :])[s], ACT.Copy).then_inc(b_ya, 1)
                        act.wait_ge(b_ya, b + 2)
                        act.wait_ge(b_yd, b + 2)
                        act.dma_start(y_rows[bass.ds(b * P, P), :], yb[s]).then_inc(b_st[s], 16)
                act.wait_ge(b_st[0], n_pairs * 16 + 16)
                act.wait_ge(b_st[1], n_pairs * 16 + 16)
                act.sem_inc(y_done, 1)
                for t in range(NT):
                    k = 2 * t
                    act.wait_ge(c_in[t], (l + 1) * 32)
                    f(comb[k], comb[k], ACT.Copy, scale=gates2[:, t:t + 1]).then_inc(c_hi, 1)
                act.sem_inc(layer_end, 1)
                act.wait_ge(layer_go, l + 1)
            

        @block.gpsimd
        def _(pool):
            tt, ts = nc.gpsimd.tensor_tensor, nc.gpsimd.tensor_scalar
            mhalf = k_("mhalf")
            with pool.Fori(0, DEPTH) as l:
                chain = [0]

                def link(ins):
                    ins.then_inc(pl, 1)
                    chain[0] += 1
                    pool.wait_ge(pl, chain[0])

                def row_rs(j):
                    pool.wait_ge(x_sq, j + 1)
                    link(ts(ss[:, j:j + 1], ss[:, j:j + 1], 1.0 / D, EPS, ALU.mult, ALU.add))
                    tt(rs[:, j:j + 1], ss[:, j:j + 1], mhalf[:, 0:1], ALU.pow).then_inc(x_rs, 1)

                pool.wait_ge(ld_start, 16 * 7)
                for t in range(NT):
                    row_rs(t)
                for t in range(NT):
                    pool.wait_ge(low_sq, t + 1)
                    ts(low_ss[:, t, 0:1], low_ss[:, t, 0:1], 1.0 / QR, EPS, ALU.mult, ALU.add)
                    link(ts(low_ss[:, t, 1:2], low_ss[:, t, 1:2], 1.0 / KVR, EPS, ALU.mult, ALU.add))
                    tt(low_rs[:, t, :], low_ss[:, t, :], mhalf[:, 0:2], ALU.pow).then_inc(low_r, 1)
                pool.wait_ge(h_ready, NT)
                for lo, hi in ((0, GAP), (GAP + SEQ, LAT0), (LAT0 + DEC, PW)):
                    m = nc.gpsimd.memset(u[:, :, lo:hi], 0.0)
                m.then_inc(pool_z, 1)

                def rope_key(j):
                    kt = KV_ORDER[j]
                    if j == 0:
                        pool.wait_ge(ld_small, (l + 1) * (7 * 16))
                    if not 1 <= kt <= NT - 1:
                        tt(krr[:, kt, :], kr[:, kt, :], gk[:, NOPE:QH], ALU.mult).then_inc(krr_s, 1)
                        return
                    link(tt(rope_t[:, 0, :], kr[:, kt, :], gk[:, NOPE:QH], ALU.mult))
                    hr = ROPE // 2
                    a, c2 = rope_t[:, 0, :], rope_t[:, 1, :]
                    cos, sin = (k_(n)[:, (kt - 1) * hr:kt * hr] for n in ("cos", "sin"))
                    link(tt(krr[:, kt, 0:hr], a[:, 0:hr], cos, ALU.mult))
                    link(tt(krr[:, kt, hr:ROPE], a[:, 0:hr], sin, ALU.mult))
                    link(tt(c2[:, 0:hr], a[:, hr:ROPE], sin, ALU.mult))
                    link(tt(c2[:, hr:ROPE], a[:, hr:ROPE], cos, ALU.mult))
                    tt(krr[:, kt, 0:hr], krr[:, kt, 0:hr], c2[:, 0:hr], ALU.subtract)
                    tt(krr[:, kt, hr:ROPE], krr[:, kt, hr:ROPE], c2[:, hr:ROPE], ALU.add).then_inc(krr_s, 1)

                def head_rs_of(j, which):
                    s_ = head_ss[:, j % 2, which, :]
                    if which == 1:
                        kt = KV_ORDER[j]
                        link(tt(s_, s_, kr_ss[:, kt:kt + 1].broadcast_to([P, H]), ALU.add))
                    link(ts(s_, s_, 1.0 / QH, EPS, ALU.mult, ALU.add))
                    tt(head_rs[:, j % 2, which, :], s_, mhalf, ALU.pow).then_inc((q_rs, k_rs)[which], 1)

                def pool_group(g):
                    if g == G_ORDER[0]:
                        pool.wait_ge(pool_z, 1)
                    src, bufs = u[:, g, :], (pa, pb)
                    link(tt(pa[:, 1:PW], src[:, 0:PW - 1], src[:, 1:PW], ALU.add))
                    for lv in range(1, g + 1):
                        r, lo = 1 << (lv - 1), 1 << lv
                        hi = PW + 1 - lo
                        a, b = bufs[(lv - 1) % 2], bufs[lv % 2]
                        link(tt(b[:, lo:hi], a[:, lo - r:hi - r], a[:, lo + r:hi + r], ALU.add))
                    w = bufs[g % 2]
                    e = k_("edge")[:, 16 * g:16 * g + 16]
                    for first, n in ((CTX0, SEQ), (LAT0, DEC)):
                        link(tt(w[:, first:first + 8], w[:, first:first + 8], e[:, 0:8], ALU.mult))
                        link(tt(w[:, first + n - 8:first + n], w[:, first + n - 8:first + n], e[:, 8:16], ALU.mult))
                    link(ts(w[:, GAP:PW - GAP], w[:, GAP:PW - GAP], 1.0 / WINDOWS[g], 0.0, ALU.mult, ALU.add))
                    tt(u[:, g, GAP:PW - GAP], w[:, GAP:PW - GAP], u[:, g, GAP:PW - GAP], ALU.subtract)\
                        .then_inc(pool_d, 1)

                pool.wait_ge(in_act, NT)
                for j in range(NT + 1):
                    rope_key(j)
                for n, g in enumerate(G_ORDER):
                    pool.wait_ge(in_act, NT + n + 1)
                    pool.wait_ge(in_dve, NT + n + 1)
                    if n > 0:
                        pool.wait_ge(pool_d, n)
                    pool_group(g)
                for j in range(NT + 1):
                    if j < NT:
                        pool.wait_ge(q_ss, j + 1)
                        if j >= 2:
                            pool.wait_ge(q_rd, j - 1)
                        head_rs_of(j, 0)
                    pool.wait_ge(k_ss, j + 1)
                    if j >= 2:
                        pool.wait_ge(k_n, j - 1)
                    head_rs_of(j, 1)

                pool.wait_ge(y_fill, FILLS * 16)
                for j in range(2 * NT):
                    n, t = divmod(j, NT)
                    pool.wait_ge(op_g, j + 1)
                    xs = x[:, t, n * HALF:(n + 1) * HALF]
                    tt(xs, xs, out_s[j % 4], ALU.add).then_inc(op_x, 1)
                    if n == 1:
                        row_rs(NT + t)

                pool.wait_ge(r_idx, 1)
                pool.wait_ge(h_st[0], 16 * 3)
                pool.wait_ge(h_st[1], 16 * 2)
                pool.wait_ge(h_t, 2 * NT)
                pool.wait_ge(r_ctl, 1)
                n_pairs = pool.value_load(ctl[0:1, 0:1], min_val=NBLK_MIN // 2, max_val=NBLK // 2)

                def gather_pair(i):
                    for b in (2 * i, 2 * i + 1):
                        if b >= 2:
                            pool.wait_ge(b_t, b - 1)
                        nc.gpsimd.indirect_dma_start(
                            xg[b % 2], None, h2_rows, bass.IndirectOffsetOnAxis(ap=idx[:, b:b + 1], axis=0))\
                            .then_inc(g_in[b % 2], 16)

                for i in range(NBLK // 2):
                    if i < NBLK_MIN // 2:
                        gather_pair(i)
                    else:
                        with pool.If(n_pairs > i):
                            gather_pair(i)
                pool.wait_ge(y_done, 1)
                for t in range(NT):
                    for w in range(2):
                        nc.gpsimd.indirect_dma_start(
                            comb[2 * t + w], None, y_rows,
                            bass.IndirectOffsetOnAxis(ap=slot_i[:, w * NT + t:w * NT + t + 1], axis=0))\
                            .then_inc(c_in[t], 16)
                for t in range(NT - 1):
                    pool.wait_ge(c_gt, t + 1)
                    tt(x[:, t, :], x[:, t, :], comb[2 * t + 1], ALU.add).then_inc(c_x, 1)
                pool.sem_inc(layer_end, 1)
                pool.wait_ge(layer_go, l + 1)

        @block.vector
        def _(ve):
            v = nc.vector
            v.memset(pairs[:, :], 0.0)
            v.memset(condT[:, :, :], 0.0).then_inc(start_d, 1)

            def columns_out(a, counts):
                p, n = divmod(a, 2)
                ve.wait_ge(counts[2], a + 1)
                ks, src = slice(4 * n, 4 * n + 4), a7[:, 0:8].rearrange("p (k c) -> p k c", c=2)
                if p == 0:
                    m = v.tensor_copy(scol[:, ks, :], src)
                else:
                    m = v.scalar_tensor_tensor(gcol[:, ks, :], src, 1.0,
                                               gn1[:, ks].unsqueeze(2).broadcast_to([P, 4, 2]), ALU.add, ALU.mult)
                m.then_inc(counts[3], 1)

            ve.wait_ge(ld_gn1, 16)
            for a in range(4):
                columns_out(a, first_ada)
            with ve.Fori(0, DEPTH) as l:
                chain = [0]

                def link(ins):
                    ins.then_inc(dv, 1)
                    chain[0] += 1
                    ve.wait_ge(dv, chain[0])

                def ada_half(a, cnd):
                    p, n = divmod(a, 2)
                    cols = slice(n * HALF, (n + 1) * HALF)
                    ve.wait_ge(ada_bc, BC_BEFORE[a] + cnd + 1)
                    if p == 4:
                        ve.wait_ge(ld_gain, l * 16 + 16)
                        m = v.scalar_tensor_tensor(G[:, cnd, cols], a7[:, :], 1.0, gain[:, cols], ALU.add, ALU.mult)
                    else:
                        m = v.tensor_copy((S if p == 3 else gate)[:, cnd, cols], a7[:, :])
                    m.then_inc(ada_bc_s, 1)

                def norm(t, j):
                    ve.wait_ge(x_rs, j + 1)
                    if j >= 2:
                        ve.wait_ge(h_t, j - 1)
                    if j >= NT + 2:
                        ve.wait_ge(h_st[t % 2], 16 * (t // 2))
                    if j < NT:
                        v.tensor_scalar(xn[t % 2], x[:, t, :], rs[:, j:j + 1], None, ALU.mult).then_inc(h_ready, 1)
                        return
                    c2 = ctx_of(t)
                    link(v.scalar_tensor_tensor(xn[t % 2], x[:, t, :], rs[:, j:j + 1], G[:, c2, :], ALU.mult, ALU.mult))
                    v.tensor_tensor(xn[t % 2], xn[t % 2], S[:, c2, :], ALU.add).then_inc(h_ready, 1)

                def evac_h(t, first):
                    ve.wait_ge(h_t, first + t + 1)
                    cols, src = slice(t * P, (t + 1) * P), tb5[:, :].rearrange("p (k n) -> p k n", n=P)
                    if first:
                        v.tensor_copy(actT[:, 4:8, cols], src).then_inc(h_td, 1)
                        return
                    c2 = ctx_of(t)
                    for k in range(4):
                        m = v.tensor_scalar(actT[:, 4 + k, cols], src[:, k, :], gcol[:, 4 + k, c2:c2 + 1],
                                            scol[:, 4 + k, c2:c2 + 1], ALU.mult, ALU.add)
                    m.then_inc(h_td, 1)

                ve.sem_inc(x_whole, 1)
                ve.wait_ge(ld_start, 16 * 7)
                ve.wait_ge(first_ada[3], 4)
                norm(0, 0)
                norm(1, 1)

                def low_norm(t):
                    ve.wait_ge(low_r, t + 1)
                    ve.wait_ge(in_act, t + 1)
                    if t > 0:
                        ve.wait_ge(low_t, t)
                    else:
                        ve.wait_ge(ld_small, (l + 1) * (7 * 16))
                    src = pair[t % 2]
                    stt = v.scalar_tensor_tensor
                    if t == 0:
                        stt(ckv_keep, src[:, HALF:HALF + KVR], low_rs[:, t, 1:2], gkva, ALU.mult, ALU.mult)\
                            .then_inc(keep_s, 1)
                    stt(cn[:, 0:QR], src[:, 0:QR], low_rs[:, t, 0:1], gqa, ALU.mult, ALU.mult)
                    stt(cn[:, QR:QR + KVR], src[:, HALF:HALF + KVR], low_rs[:, t, 1:2], gkva, ALU.mult, ALU.mult)\
                        .then_inc(in_dve, 1)

                def evac_ckv(j):
                    kt = KV_ORDER[j]
                    ve.wait_ge(low_t, j + 1)
                    v.tensor_copy(ckvT[:, :, kt * P:(kt + 1) * P], a7[:, 0:KVR].rearrange("p (k n) -> p k n", n=P))\
                        .then_inc(low_td, 1)

                evac_h(0, 0)
                for t in range(NT):
                    if t + 2 < NT:
                        norm(t + 2, t + 2)
                    if t + 1 < NT:
                        evac_h(t + 1, 0)
                    low_norm(t)
                    if t > 0:
                        evac_ckv(t - 1)
                for n, g in enumerate(G_ORDER):
                    j = NT + n
                    ve.wait_ge(in_mm, j + 1)
                    v.tensor_copy(u[:, g, CTX0:CTX0 + SEQ], pair[j % 2][:, HALF:HALF + SEQ]).then_inc(in_dve, 1)
                    if n == 0:
                        evac_ckv(NT - 1)
                    if n == 1:
                        evac_ckv(NT)

                def bc(a, n):
                    return a.unsqueeze(2).broadcast_to([P, a.shape[1], n])

                def q_sum(t):
                    ve.wait_ge(q_sq, t + 1)
                    v.tensor_reduce(head_ss[:, t % 2, 0, :], sq_q, AX.X, ALU.add).then_inc(q_ss, 1)

                def q_scale(t):
                    ve.wait_ge(q_rs, t + 1)
                    if t > 0:
                        ve.wait_ge(qk_t, 2 * t - 1)
                    for n in range(2):
                        m = v.tensor_tensor(qn[:, 4 * n:4 * n + 4, :],
                                            pair[0][:, n * HALF:n * HALF + 4 * QH].rearrange("p (h d) -> p h d", d=QH),
                                            bc(head_rs[:, t % 2, 0, 4 * n:4 * n + 4], QH), ALU.mult)
                    m.then_inc(q_rd, 1)

                def q_rest(t):
                    ve.wait_ge(q_rd, t + 1)
                    gq_b = gq[:, :].unsqueeze(1).broadcast_to([P, H, QH])
                    if t == 0:
                        v.tensor_tensor(qn, qn, gq_b, ALU.mult).then_inc(q_n, 1)
                        return
                    link(v.tensor_tensor(qn, qn, gq_b, ALU.mult))
                    hr = ROPE // 2
                    r1, r2 = qn[:, :, NOPE:NOPE + hr], qn[:, :, NOPE + hr:QH]
                    cos, sin = (k_(n)[:, (t - 1) * hr:t * hr].unsqueeze(1).broadcast_to([P, H, hr])
                                for n in ("cos", "sin"))
                    v.tensor_tensor(rq[0], r1, sin, ALU.mult)
                    v.tensor_tensor(rq[1], r2, sin, ALU.mult)
                    v.tensor_tensor(rq[2], r1, cos, ALU.mult)
                    link(v.tensor_tensor(rq[3], r2, cos, ALU.mult))
                    v.tensor_tensor(r1, rq[2], rq[1], ALU.subtract)
                    v.tensor_tensor(r2, rq[0], rq[3], ALU.add).then_inc(q_n, 1)

                def k_sum(j):
                    ve.wait_ge(k_sq, j + 1)
                    v.tensor_reduce(head_ss[:, j % 2, 1, :], sq_k, AX.X, ALU.add).then_inc(k_ss, 1)

                def k_norm(j):
                    kt = KV_ORDER[j]
                    ve.wait_ge(k_rs, j + 1)
                    ve.wait_ge(v_cp, j + 1)
                    if j > 0:
                        ve.wait_ge(qk_t, 2 * j)
                    r = head_rs[:, j % 2, 1, :]
                    for n in range(2):
                        m = v.tensor_tensor(
                            kn[:, 4 * n:4 * n + 4, 0:NOPE],
                            pair[1][:, n * HALF:(n + 1) * HALF].rearrange("p (h d) -> p h d", d=P)[:, :, 0:NOPE],
                            bc(r[:, 4 * n:4 * n + 4], NOPE), ALU.mult)
                    m.then_inc(k_rd, 1)
                    ve.wait_ge(krr_s, j + 1)
                    v.tensor_tensor(kn[:, :, NOPE:QH], krr[:, kt, :].unsqueeze(1).broadcast_to([P, H, ROPE]),
                                    bc(r, ROPE), ALU.mult)
                    ve.wait_ge(k_rd, j + 1)
                    v.tensor_tensor(kn[:, :, 0:NOPE], kn[:, :, 0:NOPE],
                                    gk[:, 0:NOPE].unsqueeze(1).broadcast_to([P, H, NOPE]), ALU.mult).then_inc(k_n, 1)

                def evac_heads(dst, tile, job):
                    ve.wait_ge(qk_t, job + 1)
                    v.tensor_copy(dst[0:QH, 4:8, tile * P:(tile + 1) * P],
                                  tb5[0:QH, :].rearrange("p (k n) -> p k n", n=P)).then_inc(qk_td, 1)

                ve.wait_ge(low_t, NT + 1)
                ve.wait_ge(keep_out, 16)
                q_sum(0)
                q_scale(0)
                k_sum(0)
                q_rest(0)
                k_norm(0)
                for j in range(NT + 1):
                    if j < NT:
                        evac_heads(qT, j, 2 * j)
                    if j + 1 < NT:
                        q_sum(j + 1)
                    evac_heads(kT, KV_ORDER[j], 2 * j + 1 if j < NT else 2 * NT)
                    if j + 1 < NT:
                        q_scale(j + 1)
                    if j + 1 <= NT:
                        k_sum(j + 1)
                    for a, step in COL_STEPS[2 * j:2 * j + 2]:
                        if step == 2:
                            if a == 2:
                                ve.wait_ge(ld_gn1, (l + 1) * 16 + 16)
                            columns_out(a, layer_ada)
                    if j + 1 < NT:
                        q_rest(j + 1)
                    if j + 1 <= NT:
                        k_norm(j + 1)
                for g in range(NG):
                    ve.wait_ge(pool_mm, g + 1)
                    v.tensor_scalar(actT[:, g, 0:P], pair[g % 2][:, HALF:HALF + SEQ], pscale[:, g:g + 1], None, ALU.mult)\
                        .then_inc(pool_ed, 1)

                def maxes(un):
                    t, _ = UNITS[un]
                    n = P if t == 0 else NLK * P
                    ve.wait_ge(s_sc, un + 1)
                    link(v.tensor_reduce(mx[:, un % 2:un % 2 + 1], pair[un % 2][:, 0:n], AX.X, ALU.max))
                    if un >= 2:
                        ve.wait_ge(s_exp, un - 1)
                    v.tensor_scalar(nmax[:, un % 2:un % 2 + 1], mx[:, un % 2:un % 2 + 1], -SCALE, None, ALU.mult)\
                        .then_inc(s_mx, 1)

                def tile_out(t):
                    ve.wait_ge(s_exp, (t + 1) * H)
                    link(v.reciprocal(rsum[:, :], esum[:, t * H:(t + 1) * H]))
                    ve.wait_ge(s_pv, (t + 1) * H)
                    if t > 0:
                        ve.wait_ge(s_ot, t)
                    v.tensor_tensor(onat.rearrange("p (h d) -> p h d", d=VH),
                                    o6[:, :].rearrange("p (h d) -> p h d", d=VH), bc(rsum[:, :], VH), ALU.mult)\
                        .then_inc(s_on, 1)

                maxes(0)
                for un in range(NU + 1):
                    if un + 1 < NU:
                        maxes(un + 1)
                    if un >= H and un % H == 0:
                        tile_out(un // H - 1)
                    if un < NU:
                        ve.wait_ge(s_pt, un + 1)
                        if UNITS[un][0] == 0:
                            ve.sem_inc(s_ptb, 1)
                        else:
                            if un >= 2:
                                ve.wait_ge(s_pv, un - 1)
                            v.tensor_copy(probT[un % 2][:, 3:NLK, :], tb5[:, 0:2 * P].rearrange("p (k n) -> p k n", n=P))\
                                .then_inc(s_ptb, 1)
                    if un in ADA_AT and ADA_AT[un][1] >= 2:
                        ada_half(ADA_AT[un][0], ADA_AT[un][1] - 2)
                ve.wait_ge(ada_bc_s, 16)

                for j in range(2 * NT):
                    n, t = divmod(j, NT)
                    ve.wait_ge(op_mm, j + 1)
                    if j >= 4:
                        ve.wait_ge(op_x, j - 3)
                    src = pair[(j % 4) // 2][:, (j % 2) * HALF:(j % 2 + 1) * HALF]
                    v.tensor_tensor(out_s[j % 4], src, gate[:, ctx_of(t), n * HALF:(n + 1) * HALF], ALU.mult)\
                        .then_inc(op_g, 1)
                    if n == 1:
                        if t > 0:
                            evac_h(t - 1, NT)
                        norm(t, NT + t)
                evac_h(NT - 1, NT)

                tt, ts, red = v.tensor_tensor, v.tensor_scalar, v.tensor_reduce
                ve.wait_ge(r_e, 1)
                link(ts(sig, sig, 1.0, None, ALU.add))
                link(v.reciprocal(sig, sig))
                rb_b = rb[:, :].unsqueeze(1).broadcast_to([P, NT, NE])
                by_tile = lambda a: a.rearrange("p (t g) k -> p t (g k)", t=NT)
                link(tt(by_tile(sel_s), by_tile(sig), rb_b, ALU.add))

                def ranks(out, val, gt, eq, n):
                    q = val.shape[1]
                    a = val.unsqueeze(3).broadcast_to([P, q, n, n])
                    b = val.unsqueeze(2).broadcast_to([P, q, n, n])
                    tt(gt, b, a, ALU.is_gt)
                    link(tt(eq, b, a, ALU.is_equal))
                    low_b = k_("lower").unsqueeze(1).broadcast_to([P, q, n * n])
                    link(tt(eq.rearrange("p q i j -> p q (i j)"), eq.rearrange("p q i j -> p q (i j)"), low_b, ALU.mult))
                    link(tt(gt, gt, eq, ALU.add))
                    link(red(out, gt, AX.X, ALU.add))

                ranks(rank, sel_s, cmp4, eq4, GE)
                link(ts(chosen, rank, 2.0, None, ALU.is_lt))
                link(tt(rank, sel_s, chosen, ALU.mult))
                link(red(gsc.rearrange("p t g -> p (t g)"), rank, AX.X, ALU.add))
                ranks(best, gsc, gcmp, geq, EG)
                link(ts(best, best, 1.0, None, ALU.is_lt))
                tt(mask.rearrange("p t (g k) -> p (t g) k", k=GE), chosen,
                   best.rearrange("p t g -> p (t g)").unsqueeze(2).broadcast_to([P, NT * EG, GE]), ALU.mult)\
                    .then_inc(r_mask, 1)
                ve.wait_ge(r_mask, 1)
                link(tt(gts, by_tile(sig), mask, ALU.mult))
                link(red(den, gts, AX.X, ALU.add))
                link(v.reciprocal(den, den))
                link(tt(gts, gts, bc(den, NE), ALU.mult))
                ve.wait_ge(r_tot, 1)
                tot = pair[0][:, NT * NE:(NT + 1) * NE]
                link(tt(nbc, bc(tot, 5), k_("kblock").unsqueeze(1).broadcast_to([P, NE, 5]), ALU.is_gt))
                link(red(nb, nbc, AX.X, ALU.add))
                link(v.tensor_tensor_scan(endb, k_("ones")[:, 0:NE], nb, 0.0, ALU.mult, ALU.add))
                tt(start, endb, nb, ALU.subtract)
                link(tt(ecmp, endb.unsqueeze(1).broadcast_to([P, NBLK, NE]), bc(k_("block"), NE), ALU.is_le))
                link(red(eidf, ecmp, AX.X, ALU.add))
                link(ts(pcmp, k_("block")[:, 0:NBLK:2], endb[:, NE - 1:NE], None, ALU.is_lt))
                link(red(nb[:, 0:1], pcmp, AX.X, ALU.add))
                v.tensor_copy(ctl[:, 0:1], nb[:, 0:1])
                link(v.tensor_copy(ctl[:, 1:2], pairs[:, :]))
                link(tt(pairs[:, :], pairs[:, :], nb[:, 0:1], ALU.add))
                link(ts(eid[:, :], eidf, float(NE - 1), None, ALU.min))
                ve.sem_inc(eid_ready, 1)
                ve.sem_inc(r_ctl, 1)
                pos = pair[0][:, 0:NT * NE].rearrange("p (t e) -> p t e", e=NE)
                link(ts(start, start, float(P), 1.0, ALU.mult, ALU.add))
                link(tt(slot1, pos, start.unsqueeze(1).broadcast_to([P, NT, NE]), ALU.add))
                link(tt(slot1, slot1, mask, ALU.mult))
                red(pick[:, 0, :], slot1, AX.X, ALU.max)
                link(red(den, slot1, AX.X, ALU.add))
                link(tt(pick[:, 1, :], den, pick[:, 0, :], ALU.subtract))
                for w in range(2):
                    m = tt(hot[:, w], slot1, bc(pick[:, w, :], NE), ALU.is_equal)
                link(m)
                for w in range(2):
                    m = tt(prod[:, w], hot[:, w], gts, ALU.mult)
                link(m)
                for w in range(2):
                    m = red(gates2[:, w * NT:(w + 1) * NT], prod[:, w], AX.X, ALU.add)
                link(m)
                flat_pick = pick.rearrange("p w t -> p (w t)")
                link(ts(slot_i[:, :], flat_pick, -1.0, None, ALU.add))
                ts(slot_a[:, :], slot_i[:, :], P - 1, None, ALU.bitwise_and)
                link(ts(slot_b[:, :], slot_i[:, :], 7, None, ALU.logical_shift_right))
                v.tensor_copy(slot_p, slot_a[:, :])
                link(v.tensor_copy(slot_q, slot_b[:, :]))
                tt(onep, k_("row").unsqueeze(1).broadcast_to([P, 2 * NT, P]), bc(slot_p, P), ALU.is_equal)
                link(tt(oneb, k_("block").unsqueeze(1).broadcast_to([P, 2 * NT, NBLK]), bc(slot_q, NBLK), ALU.is_equal))
                for w in range(2):
                    m = tt(oneb[:, w * NT:(w + 1) * NT], oneb[:, w * NT:(w + 1) * NT], bc(k_("token"), NBLK), ALU.mult)
                m.then_inc(r_one, 1)
                ve.wait_ge(r_pe1, 1)
                v.tensor_copy(idx[:, :], pair[1][:, 0:NBLK]).then_inc(r_idx, 1)

                for count, n in ((b_td, 1), (b_act, 2), (b_yd, 1)):
                    ve.sem_inc(count, n)
                n_pairs = ve.value_load(ctl[0:1, 0:1], min_val=NBLK_MIN // 2, max_val=NBLK // 2)
                before = ve.value_load(ctl[0:1, 1:2], min_val=0, max_val=DEPTH * NBLK // 2)
                with ve.Fori(0, n_pairs) as i:
                    for s in range(2):
                        ve.wait_ge(b_t, i * 2 + s + 1)
                        src = pair[0][:, HALF:2 * HALF] if s == 0 else a7[:, :]
                        v.tensor_copy(xgT[s][:, 4:8, :], src.rearrange("p (k n) -> p k n", n=P)).then_inc(b_td, 1)
                    for s in range(2):
                        ve.wait_ge(b_sil, i * 2 + s + 1)
                        ve.wait_ge(b_at, i * 2 + s + 1)
                        v.tensor_tensor(act_n[s], sil[s], (tb4, tb5)[s][:, DE:2 * DE], ALU.mult).then_inc(b_act, 1)
                    for s in range(2):
                        b = i * 2 + s
                        ve.wait_ge(dn_used, (before + i) * 2 + (s + 3))
                        ve.wait_ge(b_st[s], i * 16 + 16)
                        v.tensor_copy(yb[s][:, HALF:D], (pair[1][:, HALF:2 * HALF], tb5[:, :])[s]).then_inc(b_yd, 1)
                ve.wait_ge(ada_bc_s, 20)
                for t in range(NT):
                    k = 2 * t
                    ve.wait_ge(c_hi, t + 1)
                    ve.wait_ge(c_in[t], (l + 1) * 32)
                    link(v.scalar_tensor_tensor(comb[k + 1], comb[k + 1], gates2[:, NT + t:NT + t + 1], comb[k],
                                                ALU.mult, ALU.add))
                    tt(comb[k + 1], comb[k + 1], gate[:, ctx_of(t), :], ALU.mult).then_inc(c_gt, 1)
                ve.wait_ge(c_gt, NT)
                tt(x[:, NT - 1, :], x[:, NT - 1, :], comb[2 * NT - 1], ALU.add).then_inc(c_x, 1)
                ve.wait_ge(c_x, NT)
                ve.wait_ge(layer_end, 3)
                for s in cleared:
                    ve.sem_clear(s)
                ve.sem_inc(layer_go, 1)


def kernel(**inputs):
    import concourse.bacc as bacc
    from concourse.bass_utils import run_bass_kernel_spmd

    arrays = {n: np.ascontiguousarray(inputs[n]) for n in INS}
    table, at = constants()
    arrays["consts"] = table
    nc = bacc.Bacc("TRN2", target_bir_lowering=False, num_devices=1)
    ins = {n: nc.dram_tensor(n, a.shape, mybir.dt.from_np(a.dtype), kind="ExternalInput").ap()
           for n, a in arrays.items()}
    outs = {n: nc.dram_tensor(n, s, F32, kind="ExternalOutput").ap() for n, s in OUTS.items()}
    step_kernel(nc, **ins, **outs, const_at=at)
    r = run_bass_kernel_spmd(nc, [arrays], core_ids=[0])
    return tuple(r.results[0][n] for n in OUTS)


INS = ["x_prompt", "x_sample", "cache_ckv", "cache_krope", "c", "c_ctx", "ada_w", "ada_b", "norm1_g", "norm2_g", "w_in",
       "pool_w", "pool_scale", "q_a_norm_g", "w_uq", "kv_a_norm_g", "w_ukv", "q_norm_g", "k_norm_g", "w_out",
       "router_w", "router_b", "w_gate", "w_up", "w_down"]
OUTS = {"y_prompt": (1, SEQ, D), "y_sample": (1, DEC, D), "new_ckv": (1, DEPTH, SEQ, KVR),
        "new_krope": (1, DEPTH, SEQ, ROPE)}
```
